# Optimizing a Trainium2 kernel written in Bass

```python
import jax
import jax.numpy as jnp
from jax import lax
import numpy as np

D_MODEL = 1024
BATCH = 1
SEQ = 512
DEPTH = 1

MIX_WIDTH = D_MODEL
ATT_WIDTH = MIX_WIDTH // 2
ATT_HEAD_DIM = 64
ATT_HEADS = ATT_WIDTH // ATT_HEAD_DIM
ROT_DIM = ATT_HEAD_DIM // 4
ROPE_THETA = 500000.0
MOBA_BLOCK = 256
MOBA_TOPK = 3
Q_CHUNK = 128
MLSTM_WIDTH = MIX_WIDTH - ATT_WIDTH
MLSTM_HEADS = 4
MLSTM_HEAD_DIM = MLSTM_WIDTH // MLSTM_HEADS
MLSTM_CHUNK = 64
CONV_WIDTH = 4
NORM_EPS = 1e-6
IN_SPLITS = (ATT_WIDTH,) * 4 + (MLSTM_WIDTH,) * 5 + (MLSTM_HEADS,) * 2

kernel_name = 'hybrid_moba_mlstm_block'

def rms_norm(x, g):
    xf = x.astype(jnp.float32)
    xf = xf * lax.rsqrt(jnp.mean(xf * xf, axis=-1, keepdims=True) + NORM_EPS)
    return xf.astype(x.dtype) * g

def split_columns(proj):
    idx = []
    acc = 0
    for s in IN_SPLITS[:-1]:
        acc += s
        idx.append(acc)
    return jnp.split(proj, idx, axis=-1)

def partial_rope(x, pos):
    half = ROT_DIM // 2
    inv_freq = jnp.power(ROPE_THETA, -jnp.arange(half, dtype=jnp.float32) * 2.0 / ROT_DIM)
    ang = pos.astype(jnp.float32)[:, None] * inv_freq[None, :]
    cos = jnp.cos(ang)[None, :, None, :].astype(x.dtype)
    sin = jnp.sin(ang)[None, :, None, :].astype(x.dtype)
    x1 = x[..., :half]
    x2 = x[..., half:ROT_DIM]
    return jnp.concatenate([x1 * cos - x2 * sin, x2 * cos + x1 * sin, x[..., ROT_DIM:]], axis=-1)

def causal_depthwise_conv(u, w, b):
    K = w.shape[0]
    S = u.shape[1]
    up = jnp.pad(u, ((0, 0), (K - 1, 0), (0, 0)))
    out = b
    for j in range(K):
        out = out + w[j] * up[:, j:j + S]
    return out

def moba_attention(q, k, v):
    B, S, H, dh = q.shape
    s_pad = -(-S // MOBA_BLOCK) * MOBA_BLOCK
    padw = ((0, 0), (0, s_pad - S), (0, 0), (0, 0))
    q = jnp.pad(q, padw) * (dh ** -0.5)
    k = jnp.pad(k, padw)
    v = jnp.pad(v, padw)
    nb = s_pad // MOBA_BLOCK
    nqc = s_pad // Q_CHUNK
    topk = min(MOBA_TOPK, nb)
    qc_per_block = MOBA_BLOCK // Q_CHUNK
    kb = k.reshape(B, nb, MOBA_BLOCK, H, dh).transpose(0, 3, 1, 2, 4)
    vb = v.reshape(B, nb, MOBA_BLOCK, H, dh).transpose(0, 3, 1, 2, 4)
    kmean = jnp.mean(kb.astype(jnp.float32), axis=3).astype(q.dtype)
    q_chunks = q.reshape(B, nqc, Q_CHUNK, H, dh).transpose(0, 1, 3, 2, 4).reshape(B * nqc, H, Q_CHUNK, dh)
    b_idx = jnp.repeat(jnp.arange(B, dtype=jnp.int32), nqc)
    c_idx = jnp.tile(jnp.arange(nqc, dtype=jnp.int32), B)
    h_ix = jnp.arange(H)[:, None, None]
    blk_ids = jnp.arange(nb)

    def one_chunk(args):
        q_c, b, c = args
        cur = c // qc_per_block
        k_b = kb[b]
        v_b = vb[b]
        gate = jnp.einsum('hqd,hnd->hqn', q_c, kmean[b]).astype(jnp.float32)
        gate = jnp.where(blk_ids < cur, gate, -jnp.inf)
        _, idx = lax.top_k(gate, topk)
        valid = idx < cur
        k_sel = k_b[h_ix, idx]
        v_sel = v_b[h_ix, idx]
        s_sel = jnp.einsum('hqd,hqjld->hqjl', q_c, k_sel).astype(jnp.float32)
        s_sel = jnp.where(valid[..., None], s_sel, -jnp.inf).reshape(H, Q_CHUNK, topk * MOBA_BLOCK)
        k_own = lax.dynamic_index_in_dim(k_b, cur, axis=1, keepdims=False)
        v_own = lax.dynamic_index_in_dim(v_b, cur, axis=1, keepdims=False)
        s_own = jnp.einsum('hqd,hld->hql', q_c, k_own).astype(jnp.float32)
        q_pos = c * Q_CHUNK + jnp.arange(Q_CHUNK)
        k_pos = cur * MOBA_BLOCK + jnp.arange(MOBA_BLOCK)
        s_own = jnp.where(k_pos[None, :] <= q_pos[:, None], s_own, -jnp.inf)
        p = jax.nn.softmax(jnp.concatenate([s_sel, s_own], axis=-1), axis=-1).astype(q_c.dtype)
        p_sel = p[..., :topk * MOBA_BLOCK].reshape(H, Q_CHUNK, topk, MOBA_BLOCK)
        p_own = p[..., topk * MOBA_BLOCK:]
        return (jnp.einsum('hqjl,hqjld->hqd', p_sel, v_sel)
                + jnp.einsum('hql,hld->hqd', p_own, v_own))

    out = lax.map(one_chunk, (q_chunks, b_idx, c_idx))
    out = out.reshape(B, nqc, H, Q_CHUNK, dh).transpose(0, 1, 3, 2, 4).reshape(B, s_pad, H * dh)
    return out[:, :S]

def mlstm_chunkwise(q, k, v, ig, fg):
    B, H, S, d = q.shape
    L = MLSTM_CHUNK
    nc = S // L
    q, k, v = (t.astype(jnp.float32) for t in (q, k, v))
    ig = ig.astype(jnp.float32)
    lf = jax.nn.log_sigmoid(fg.astype(jnp.float32))
    to_chunks = lambda t: jnp.moveaxis(t.reshape(B, H, nc, L, *t.shape[3:]), 2, 0)
    xs = (to_chunks(q), to_chunks(k), to_chunks(v), to_chunks(ig), to_chunks(lf))
    causal = jnp.tril(jnp.ones((L, L), dtype=bool))

    def step(carry, inp):
        C, n, m = carry
        qc, kc, vc, ic, fc = inp
        bcum = jnp.cumsum(fc, axis=-1)
        D = jnp.where(causal, bcum[..., :, None] - bcum[..., None, :] + ic[..., None, :], -jnp.inf)
        inter = bcum + m[..., None]
        m_t = jnp.maximum(inter, jnp.max(D, axis=-1))
        w_inter = jnp.exp(inter - m_t)
        s = jnp.einsum('bhtd,bhsd->bhts', qc, kc) * jnp.exp(D - m_t[..., None])
        num = (w_inter[..., None] * jnp.einsum('bhvd,bhtd->bhtv', C, qc)
               + jnp.einsum('bhts,bhsv->bhtv', s, vc))
        nq = w_inter * jnp.einsum('bhd,bhtd->bht', n, qc) + jnp.sum(s, axis=-1)
        h = num / jnp.maximum(jnp.abs(nq), jnp.exp(-m_t))[..., None]
        b_last = bcum[..., -1]
        g = b_last[..., None] - bcum + ic
        m_new = jnp.maximum(b_last + m, jnp.max(g, axis=-1))
        decay = jnp.exp(b_last + m - m_new)
        w = jnp.exp(g - m_new[..., None])
        C = decay[..., None, None] * C + jnp.einsum('bhs,bhsv,bhsd->bhvd', w, vc, kc)
        n = decay[..., None] * n + jnp.einsum('bhs,bhsd->bhd', w, kc)
        return (C, n, m_new), h

    init = (jnp.zeros((B, H, d, d), jnp.float32), jnp.zeros((B, H, d), jnp.float32),
            jnp.zeros((B, H), jnp.float32))
    _, hs = lax.scan(step, init, xs)
    return jnp.moveaxis(hs, 0, 2).reshape(B, H, S, d)

def setup_inputs(seed: int = 0) -> dict:
    key = jax.random.key(seed)
    ks = jax.random.split(key, 12)
    f32 = jnp.float32
    nrm = lambda k, shape: jax.random.normal(k, shape, f32)
    in_cols = sum(IN_SPLITS)
    return {
        'x': nrm(ks[0], (BATCH, SEQ, D_MODEL)),
        'pre_norm_g': 1.0 + 0.05 * nrm(ks[1], (DEPTH, D_MODEL)),
        'w_in': nrm(ks[2], (DEPTH, D_MODEL, in_cols)) * D_MODEL ** -0.5,
        'mlstm_i_bias': 0.1 * nrm(ks[3], (DEPTH, MLSTM_HEADS)),
        'mlstm_f_bias': jnp.linspace(3.0, 6.0, MLSTM_HEADS, dtype=f32)[None, :] + 0.01 * nrm(ks[4], (DEPTH, MLSTM_HEADS)),
        'conv_w': nrm(ks[5], (DEPTH, CONV_WIDTH, 2 * MLSTM_WIDTH)) * CONV_WIDTH ** -0.5,
        'conv_b': 0.01 * nrm(ks[6], (DEPTH, 2 * MLSTM_WIDTH)),
        'attn_out_g': 1.0 + 0.05 * nrm(ks[7], (DEPTH, ATT_WIDTH)),
        'mlstm_out_g': 1.0 + 0.05 * nrm(ks[8], (DEPTH, MLSTM_WIDTH)),
        'w_out': nrm(ks[9], (DEPTH, MIX_WIDTH, D_MODEL)) * MIX_WIDTH ** -0.5,
        'post_norm_g': 1.0 + 0.05 * nrm(ks[10], (DEPTH, D_MODEL)),
    }

def reference(x, pre_norm_g, w_in, mlstm_i_bias, mlstm_f_bias, conv_w, conv_b,
              attn_out_g, mlstm_out_g, w_out, post_norm_g):
    B, S, _ = x.shape
    pos = jnp.arange(S, dtype=jnp.int32)
    att_heads = lambda t: t.reshape(B, S, ATT_HEADS, ATT_HEAD_DIM)
    ml_heads = lambda t: t.reshape(B, S, MLSTM_HEADS, MLSTM_HEAD_DIM).transpose(0, 2, 1, 3)
    for l in range(DEPTH):
        h = rms_norm(x, pre_norm_g[l])
        proj = jnp.einsum('bsd,dc->bsc', h, w_in[l])
        aq, ak, av, az, mq, mk, mv, mo, mz, mi, mf = split_columns(proj)

        ya = moba_attention(partial_rope(att_heads(aq), pos), partial_rope(att_heads(ak), pos), att_heads(av))
        ya = rms_norm(ya, attn_out_g[l]) * jax.nn.silu(az)

        qk = jax.nn.silu(causal_depthwise_conv(jnp.concatenate([mq, mk], axis=-1), conv_w[l], conv_b[l]))
        mq_c, mk_c = jnp.split(qk, 2, axis=-1)
        hm = mlstm_chunkwise(ml_heads(mq_c), ml_heads(mk_c) * MLSTM_HEAD_DIM ** -0.5, ml_heads(mv),
                             (mi + mlstm_i_bias[l]).transpose(0, 2, 1),
                             (mf + mlstm_f_bias[l]).transpose(0, 2, 1))
        mu = jnp.mean(hm, axis=-1, keepdims=True)
        var = jnp.mean(jnp.square(hm - mu), axis=-1, keepdims=True)
        hm = (hm - mu) * lax.rsqrt(var + NORM_EPS)
        hm = hm.transpose(0, 2, 1, 3).reshape(B, S, MLSTM_WIDTH).astype(x.dtype) * mlstm_out_g[l]
        ym = jax.nn.sigmoid(mo) * hm * jax.nn.silu(mz)

        y = jnp.einsum('bsc,cd->bsd', jnp.concatenate([ya, ym], axis=-1), w_out[l])
        x = x + rms_norm(y, post_norm_g[l])
    return x


_drawn_inputs = setup_inputs


def setup_inputs(seed=0):
    import zlib

    import numpy as np

    out = dict(_drawn_inputs(seed))
    spreads = {}
    factors = {'mlstm_i_bias': 200.0, 'conv_b': 8.0, 'mlstm_out_g': 12.237, 'attn_out_g': 3.435}
    for name, (base, spread) in spreads.items():
        noise = np.random.default_rng([zlib.crc32(name.encode()), seed]).standard_normal(out[name].shape)
        drawn = base * np.exp(spread * noise) if base else spread * noise
        out[name] = jnp.asarray(drawn.astype(out[name].dtype))
    for name, factor in factors.items():
        out[name] = (out[name] * factor).astype(out[name].dtype)
    return out
```

```python
from contextlib import ExitStack

import numpy as np

import concourse.bass as bass
from concourse import mybir

F32 = mybir.dt.float32
F32R = mybir.dt.float32r
ALU = mybir.AluOpType
ACT = mybir.ActivationFunctionType

P = 128
SEQ = 512
D = 1024
NT = SEQ // P
NK = D // P
AW = 512
AH, DH = 8, 64
MH, MD = 4, 128
MV = MD + 2
ROT = DH // 4
HALF = ROT // 2
KCONV = 4
EPS = 1e-6
FAR = -1e30
BIG = 3e38
Q_SCALE = DH ** -0.5
K_SCALE = MD ** -0.5

AQ, AK, AV, AZ, MQ, MK, MVC, MO, MZ, MG = (AW * i for i in range(10))

SLOTS = [("in", "cols", k, MVC) for k in range(NK)]
for _h in range(MH):
    for _c in (MQ, MK):
        SLOTS += [("in", "heads", k, _c + _h * MD) for k in (0, 4)]
for _c in (AZ, MZ, MO, AK, AV):
    SLOTS += [("in", "cols", k, _c) for k in range(NK)]
SLOTS += [("out", "cols", 4 + k, c * AW) for c in range(2) for k in range(4)]
SLOTS += [("in", "cols", k, AQ) for k in range(NK)]
SLOTS += [("out", "cols", k, c * AW) for c in range(2) for k in range(4)]
S_MV, S_QK, S_AZ, S_MZ, S_MO, S_AK, S_AV, S_OM, S_AQ, S_OA = 0, 8, 24, 32, 40, 48, 56, 64, 72, 80
NSLOT = len(SLOTS)
RAW = 4
RING = 8
AHEAD = 6

R_PRE, R_AG, R_MG, R_CB, R_CW, R_END = 0, 8, 12, 16, 24, 56

F_E, F_U, F_ACC, F_PM, F_END = 0, 5120, 6152, 7176, 8200
F_X = 0
F_QK, F_SM, F_P, F_YA, F_XR, F_Y = 0, 1024, 2048, 3072, 4096, 6144
R_QK, R_MV, R_P = 0, 4096, 8256
R_KT, R_V, R_QT, R_PT, R_YA, R_SIZE = 0, 4096, 8192, 10240, 12288, 14336
R_YM = R_PT
E_AT = [0, 2048, 3584, 4608]
P_AT = [0, 512, 896, 1152]

NU = NT * AH


UNIT_SLOT = {3: S_QK, 15: S_MZ, 19: S_MO, 23: S_AK, 27: S_AV, 31: S_OM, 35: S_OM + 4, 39: S_AQ, 43: S_OA}
UNIT_SLOT.update({4 + n: S_QK + 2 * n + 2 for n in range(2 * MH)})

PE_ST = {S_QK + 7 + 4 * h: h for h in range(MH)}
PE_PV = {S_QK + 9 + 4 * h: h for h in range(MH)}

LAG_T, LAG_PV = 2, 3
EVENTS = {}


def _event(step, kind, i):
    EVENTS.setdefault(step, []).append((kind, i))


for _i in range(1, NT):
    for _k in range(NK):
        _event({1: _k // 2, 2: 4 + _k, 3: 12 + _k // 2}[_i], "aq", (_i, _k))
for _i, (_a, _b) in {1: (4, 6), 2: (12, 14), 3: (16, 18)}.items():
    _event(_a, "q_copy", _i)
    _event(_b, "q_T", _i)
for _k in range(NK):
    _event(13 + _k // 2, "cut", S_OA + _k)
for _i in range(NT):
    _s = AH * _i + AH - 1 + LAG_PV
    _event(_s, "ya", _i)
    _event(_s + 1, "ya_ms", _i)
    _event(_s + 2, "ya_gate", _i)
    _event(_s + 3, "ya_T", _i)
    _o = (17, 25, 33, 38)[_i]
    for _k in range(8):
        _event(_o + (_k, _k, _k // 2, 0)[_i], "oa", (_i, _k))
    _e = (25, 33, 37, 39)[_i]
    _event((21, 29, 35, 38)[_i], "y", (_i, 0))
    _event(_e, "y", (_i, 1))
    _event(_e + 1, "y_ms", _i)
    _event(_e + 2, "y_fin", _i)
STEPS = max(EVENTS) + 1


def unit(u):
    return NT - 1 - u // AH, u % AH


def build(nc, x, pre_g, w_in, i_bias, f_bias, conv_w, conv_b, attn_g, mlstm_g, w_out, post_g, rope, out):
    with ExitStack() as ctx:
        def sb(name, shape, dt=F32):
            return ctx.enter_context(nc.sbuf_tensor(name, shape, dt))

        def sem(name):
            return ctx.enter_context(nc.semaphore(name))

        xT_hi = sb("xT_hi", [P, NK, SEQ], F32R)
        xT_lo = sb("xT_lo", [P, NK, SEQ], F32R)
        w_raw = sb("w_raw", [P, RAW, AW])
        w_hi = sb("w_hi", [P, RING, AW], F32R)
        w_lo = sb("w_lo", [P, RING, AW], F32R)
        farena = sb("farena", [P, F_END])
        rarena = sb("rarena", [P, R_SIZE], F32R)
        silu_az = sb("silu_az", [P, NT, AW])
        gy = sb("gy", [P, 2, NT, AW])
        post = sb("post", [P, D])
        tmp = sb("tmp", [P, 2, AW])
        rbc = sb("rbc", [P, SEQ])
        junk = sb("junk", [P, D], mybir.dt.bfloat16)
        ident = sb("ident", [P, P])
        ones = sb("ones", [P, P])
        causal = sb("causal", [P, SEQ])
        causalT = sb("causalT", [P, P])
        rope_sb = sb("rope_sb", [P, NT, 2 * ROT])
        rtmp = sb("rtmp", [P, 2, AH * ROT])
        prow = sb("prow", [R_END, P])
        pcol = sb("pcol", [P, R_END])
        wg_raw = sb("wg_raw", [P, NK, 8])
        wg_hi = sb("wg_hi", [P, NK, 32], F32R)
        wg_lo = sb("wg_lo", [P, NK, 32], F32R)
        bias8 = sb("bias8", [P, 8])
        bias32 = sb("bias32", [P, 32])
        gsb = sb("gsb", [P, NT, 32])
        aT = sb("aT", [P, NT, 16])
        emt = sb("emt", [P, NT, MH])
        ssx = sb("ssx", [P, NT])
        msx = sb("msx", [P, NT])
        rx = sb("rx", [P, NT])
        mhalf = sb("mhalf", [P, NT])
        bns = sb("bns", [P, 2, 6])
        mva = sb("mva", [P, 2, 2])
        den = sb("den", [P, 2])
        iden = sb("iden", [P, 2])
        vs1 = sb("vs1", [P, 2])
        vs2 = sb("vs2", [P, 2])
        vr = sb("vr", [P, 2])
        hsc = sb("hsc", [P, 2])
        mx = sb("mx", [P, NU])
        rsum = sb("rsum", [P, NU])
        rrec = sb("rrec", [P, NU])
        ssa = sb("ssa", [P, NT])
        msa = sb("msa", [P, NT])
        ra = sb("ra", [P, NT])
        ssy = sb("ssy", [P, 2 * NT])
        msy = sb("msy", [P, NT])
        ry = sb("ry", [P, NT])

        bank = [ctx.enter_context(nc.psum_tensor(f"bank{i}", [P, 512], F32)) for i in range(8)]

        def f_part(at, *shape):
            n = int(np.prod(shape))
            v = farena[:, at:at + n]
            return v if len(shape) == 1 else v.rearrange("p (a b) -> p a b", a=shape[0]) if len(shape) == 2 \
                else v.rearrange("p (a b c) -> p a b c", a=shape[0], b=shape[1])

        def r_part(at, *shape):
            n = int(np.prod(shape))
            v = rarena[:, at:at + n]
            return v if len(shape) == 1 else v.rearrange("p (a b) -> p a b", a=shape[0]) if len(shape) == 2 \
                else v.rearrange("p (a b c) -> p a b c", a=shape[0], b=shape[1])

        x_sb = f_part(F_X, NT, D)
        decay = [f_part(F_E + E_AT[j], MH, SEQ - P * j) for j in range(NT)]
        upad = f_part(F_U, 2, 516)
        cacc = f_part(F_ACC, 2, SEQ)
        pm = f_part(F_PM, 2, SEQ)
        qk_hi = r_part(R_QK, 4, SEQ)
        qk_lo = r_part(R_QK + 4 * SEQ, 4, SEQ)
        mv_hi = r_part(R_MV, NT, MH, MV)
        mv_lo = r_part(R_MV + NT * MH * MV, NT, MH, MV)
        pm_hi = r_part(R_P, 1280)
        pm_lo = r_part(R_P + 1280, 1280)
        gate, ym = gy[:, 0], gy[:, 1]
        y_mlstm = gy[:].rearrange("p a t c -> p (a t c)").rearrange("p (t c) -> p t c", t=NT)
        rows = [gy[0:16, i // 4, i % 4, :] for i in range(8)]
        queries = f_part(F_QK, 2, AW)
        keys = f_part(F_XR, NT, AW)
        sm = f_part(F_SM, 2, SEQ)
        prob = f_part(F_P, 2, SEQ)
        ya = f_part(F_YA, 2, AW)
        xr = f_part(F_XR, 2, D)
        yb = f_part(F_Y, 2, D)
        kT_hi = r_part(R_KT, 4, SEQ)
        kT_lo = r_part(R_KT + 4 * SEQ, 4, SEQ)
        v_hi = r_part(R_V, NT, AW)
        v_lo = r_part(R_V + NT * AW, NT, AW)
        qT = r_part(R_QT, 4, AW)
        pT = r_part(R_PT, 4, SEQ)
        yaT = r_part(R_YA, 4, AW)
        ymT_hi = r_part(R_YM, 4, SEQ)
        ymT_lo = r_part(R_YM + 4 * SEQ, 4, SEQ)
        g_dram = nc.dram_tensor("g_rows", (16, SEQ), F32, kind="Internal").ap()

        x_in = [sem(f"x_in{t}") for t in range(NT)]
        par_in = sem("par_in")
        wg_in = sem("wg_in")
        bias_in = sem("bias_in")
        rope_in = sem("rope_in")
        post_in = sem("post_in")
        raw_in = [sem(f"raw_in{r}") for r in range(RAW)]
        w_hi_done = sem("w_hi_done")
        w_lo_done = sem("w_lo_done")
        w_used = sem("w_used")
        consts = sem("consts")
        cleared = sem("cleared")
        par_ps = sem("par_ps")
        par_done = sem("par_done")
        xt_ps = sem("xt_ps")
        xt_scaled = sem("xt_scaled")
        xt_hi = sem("xt_hi")
        xt_lo = sem("xt_lo")
        ssx_done = sem("ssx_done")
        msx_done = sem("msx_done")
        rx_done = sem("rx_done")
        diag_done = sem("diag_done")
        rbc_ps = sem("rbc_ps")
        rbc_done = sem("rbc_done")
        wg_done = sem("wg_done")
        gate_ps = sem("gate_ps")
        gate_sb = sem("gate_sb")
        grow_ps = sem("grow_ps")
        absf_done = sem("absf_done")
        expf_done = sem("expf_done")
        onep_done = sem("onep_done")
        ln_done = sem("ln_done")
        grows_done = sem("grows_done")
        gcol_ps = sem("gcol_ps")
        aT_done = sem("aT_done")
        emt_done = sem("emt_done")
        g_out = sem("g_out")
        g_back = sem("g_back")
        g_masked = sem("g_masked")
        decay_done = sem("decay_done")
        proj_ps = sem("proj_ps")
        mv_hi_done = sem("mv_hi_done")
        mv_lo_done = sem("mv_lo_done")
        mv_ones = sem("mv_ones")
        u_done = sem("u_done")
        conv_done = sem("conv_done")
        silu_done = sem("silu_done")
        qk_hi_done = sem("qk_hi_done")
        qk_lo_done = sem("qk_lo_done")
        st_ps = sem("st_ps")
        pm_done = sem("pm_done")
        pm_hi_done = sem("pm_hi_done")
        pm_lo_done = sem("pm_lo_done")
        mpv_ps = sem("mpv_ps")
        var_done = sem("var_done")
        vr_done = sem("vr_done")
        ym_done = sem("ym_done")
        z_done = sem("z_done")
        gate_mul = sem("gate_mul")
        ym_gated = sem("ym_gated")
        ymt_ps = sem("ymt_ps")
        ymt_scaled = sem("ymt_scaled")
        ymt_hi = sem("ymt_hi")
        ymt_lo = sem("ymt_lo")
        k_raw = sem("k_raw")
        k_roped = sem("k_roped")
        kt_ps = sem("kt_ps")
        kt_hi = sem("kt_hi")
        kt_lo = sem("kt_lo")
        v_hi_done = sem("v_hi_done")
        v_lo_done = sem("v_lo_done")
        q_raw = sem("q_raw")
        q_roped = sem("q_roped")
        qt_ps = sem("qt_ps")
        qt_hi = sem("qt_hi")
        qt_lo = sem("qt_lo")
        score_ps = sem("score_ps")
        masked = sem("masked")
        prob_done = sem("prob_done")
        pt_ps = sem("pt_ps")
        pt_hi = sem("pt_hi")
        pt_lo = sem("pt_lo")
        pv_ps = sem("pv_ps")
        ya_done = sem("ya_done")
        ssa_done = sem("ssa_done")
        msa_done = sem("msa_done")
        ra_done = sem("ra_done")
        ya_gated = sem("ya_gated")
        yat_ps = sem("yat_ps")
        yat_scaled = sem("yat_scaled")
        yat_hi = sem("yat_hi")
        yat_lo = sem("yat_lo")
        om_done = sem("om_done")
        oa_ps = sem("oa_ps")
        y_done = sem("y_done")
        ssy_done = sem("ssy_done")
        msy_done = sem("msy_done")
        ry_done = sem("ry_done")
        y_normed = sem("y_normed")
        xr_in = [sem(f"xr_in{t}") for t in range(NT)]
        out_ready = sem("out_ready")
        out_done = [sem(f"out_done{t}") for t in range(NT)]
        vchain = sem("vchain")
        achain = sem("achain")

        block = ctx.enter_context(nc.Block())

        def projected(eng, p):
            if p in UNIT_SLOT:
                eng.wait_ge(w_used, UNIT_SLOT[p])
            else:
                eng.wait_ge(proj_ps, sum(1 for q in range(p + 1) if q not in UNIT_SLOT))

        def store(sp, i):
            t = NT - 1 - i
            for c in range(2):
                cols = slice(c * AW, (c + 1) * AW)
                sp.wait_ge(out_ready, 2 * i + c + 1)
                sp.dma_start(out[0, t * P:(t + 1) * P, cols], xr[:, i % 2, cols]).then_inc(out_done[i], 16)

        @block.sync
        def _(sp):
            x2 = x.rearrange("b s d -> (b s) d")

            def rows_of(v, n):
                return v.rearrange("o (c p) -> (o c) p", p=P)

            sp.dma_start(x_sb[:, 0, :], x2[0:P, :]).then_inc(x_in[0], 16)
            sp.dma_start(prow[R_PRE:R_AG, :], rows_of(pre_g, 8)).then_inc(par_in, 16)
            sp.dma_start(prow[R_AG:R_MG, :], rows_of(attn_g, 4)).then_inc(par_in, 16)
            sp.dma_start(prow[R_MG:R_CB, :], rows_of(mlstm_g, 4)).then_inc(par_in, 16)
            sp.dma_start(prow[R_CB:R_CW, :], rows_of(conv_b, 8)).then_inc(par_in, 16)
            sp.dma_start(prow[R_CW:R_END, :], conv_w.rearrange("o j (c p) -> (o j c) p", p=P)).then_inc(par_in, 16)
            for t in range(1, NT):
                sp.dma_start(x_sb[:, t, :], x2[t * P:(t + 1) * P, :]).then_inc(x_in[t], 16)
            sp.dma_start(wg_raw[:], w_in[0, :, MG:MG + 8].rearrange("(k p) c -> p k c", p=P)).then_inc(wg_in, 16)
            sp.dma_start(bias8[:, 0:MH], i_bias.to_broadcast([P, MH])).then_inc(bias_in, 16)
            sp.dma_start(bias8[:, MH:2 * MH], f_bias.to_broadcast([P, MH])).then_inc(bias_in, 16)
            for n, (mat, kind, k, c) in enumerate(SLOTS):
                if n >= RAW:
                    sp.wait_ge(w_lo_done, n - RAW + 1)
                w = w_in if mat == "in" else w_out
                if kind == "cols":
                    src = w[0, k * P:(k + 1) * P, c:c + AW]
                    dst = w_raw[:, n % RAW, :]
                else:
                    src = w[0, k * P:(k + 4) * P, c:c + MD].rearrange("(k p) c -> p k c", p=P)
                    dst = w_raw[:, n % RAW, :].rearrange("p (k c) -> p k c", k=4)
                sp.dma_start(dst, src).then_inc(raw_in[n % RAW], 16)
                if n == S_QK:
                    sp.dma_start(rope_sb[:], rope.rearrange("(t p) c -> p t c", p=P)).then_inc(rope_in, 16)
                    sp.dma_start(post[:], post_g.to_broadcast([P, D])).then_inc(post_in, 16)
            for i in range(NT):
                t = NT - 1 - i
                if i == 0:
                    sp.wait_ge(pm_lo_done, MH * NT)
                    sp.wait_ge(mpv_ps, 2 * MH)
                    sp.wait_ge(kt_ps, NT)
                if i >= 2:
                    sp.wait_ge(out_done[i - 2], 32)
                sp.dma_start(xr[:, i % 2, :], x2[t * P:(t + 1) * P, :]).then_inc(xr_in[i], 16)
                if i >= 1:
                    store(sp, i - 1)
            store(sp, NT - 1)
            for i in range(NT):
                sp.wait_ge(out_done[i], 32)

        def final(g, i, rsqrt):
            g.wait_ge(msy_done, i + 1)
            rsqrt(ry[:, i:i + 1], msy[:, i:i + 1]).then_inc(ry_done, 1)
            g.wait_ge(xr_in[i], 16)
            for c in range(2):
                cols = slice(c * AW, (c + 1) * AW)
                g.wait_ge(y_normed, 2 * i + c + 1)
                g.tensor_tensor(xr[:, i % 2, cols], xr[:, i % 2, cols], yb[:, i % 2, cols], ALU.add)\
                    .then_inc(out_ready, 1)

        @block.gpsimd
        def _(g):
            g.memset(ident[:], 0.0).then_inc(cleared, 1)
            g.memset(causal[:], 0.0).then_inc(cleared, 1)
            g.memset(causalT[:], 0.0).then_inc(cleared, 1)
            g.memset(rows[7], 1.0).then_inc(cleared, 1)
            g.memset(upad[:, :, 0:KCONV - 1], 0.0).then_inc(cleared, 1)
            g.wait_ge(cleared, 5)
            g.affine_select(out=ident[:], in_=ident[:], compare_op=ALU.not_equal, fill=1.0, base=0,
                            pattern=[[-1, P]], channel_multiplier=1).then_inc(consts, 1)
            g.memset(ones[:], 1.0).then_inc(consts, 1)
            g.memset(mhalf[:], -0.5).then_inc(consts, 1)
            g.affine_select(out=causal[:, SEQ - P:], in_=causal[:, SEQ - P:], compare_op=ALU.is_ge, fill=FAR, base=0,
                            pattern=[[-1, P]], channel_multiplier=1).then_inc(consts, 1)
            g.affine_select(out=causalT[:], in_=causalT[:], compare_op=ALU.is_ge, fill=FAR, base=0,
                            pattern=[[1, P]], channel_multiplier=-1).then_inc(consts, 1)
            g.affine_select(out=rows[7].rearrange("p (t c) -> p t c", t=NT),
                            in_=rows[7].rearrange("p (t c) -> p t c", t=NT), compare_op=ALU.is_ge, fill=0.0,
                            base=3, pattern=[[4, NT], [0, P]], channel_multiplier=-1).then_inc(consts, 1)
            g.memset(mv_hi[:, :, :, MD:MV].bitcast(F32), 1.0).then_inc(mv_ones, 1)
            g.memset(mv_lo[:, :, :, MD:MV].bitcast(F32), 0.0).then_inc(mv_ones, 1)

            def rsqrt(dst, src):
                return g.tensor_tensor(dst, src, mhalf[:, 0:src.shape[1]], ALU.pow)

            g.wait_ge(consts, 3)
            g.wait_ge(msx_done, 1)
            rsqrt(rx[:], msx[:]).then_inc(rx_done, 1)
            g.wait_ge(grows_done, 1)
            g.dma_start(g_dram, rows[4]).then_inc(g_out, 16)
            g.wait_ge(g_out, 16)
            for j in range(NT):
                g.dma_start(decay[j], g_dram[4 * j:4 * j + 4, j * P:].rearrange("(o h) c -> o h c", o=1)
                            .to_broadcast([P, MH, SEQ - j * P])).then_inc(g_back, 16)
            g.wait_ge(g_back, 16 * NT)
            for j in range(NT):
                v = decay[j][:, :, 0:P]
                g.tensor_tensor(v, v, causalT[:].unsqueeze(1).to_broadcast([P, MH, P]), ALU.add).then_inc(g_masked, 1)
            for n in range(2 * MH):
                g.wait_ge(var_done, n + 1)
                rsqrt(vr[:], vs2[:]).then_inc(vr_done, 1)
            for t in range(NT):
                g.wait_ge(z_done, 2 * NT + t + 1)
                g.tensor_tensor(gate[:, t, :], gate[:, t, :], tmp[:, t % 2, :], ALU.mult).then_inc(gate_mul, 1)
                g.wait_ge(gate_mul, t + 1)
                g.wait_ge(ym_done, 2 * MH)
                g.tensor_tensor(ym[:, t, :], ym[:, t, :], gate[:, t, :], ALU.mult).then_inc(ym_gated, 1)
            for i in range(NT):
                g.wait_ge(msa_done, i + 1)
                rsqrt(ra[:, i:i + 1], msa[:, i:i + 1]).then_inc(ra_done, 1)
                if i >= 1:
                    final(g, i - 1, rsqrt)
            final(g, NT - 1, rsqrt)

        def z_evac(a, which, t):
            p = 12 + 4 * which + t
            projected(a, p)
            if which == 2 and t >= 2:
                a.wait_ge(gate_mul, t - 1)
            dst = (silu_az[:, t, :], gate[:, t, :], tmp[:, t % 2, :])[which]
            a.activation(dst, bank[p % 4][:], ACT.Sigmoid if which == 2 else ACT.Silu,
                         scale=rx[:, t:t + 1]).then_inc(z_done, 1)

        def om_evac(a, c, t):
            projected(a, 32 + NT * c + t)
            a.wait_ge(ymt_ps, NT)
            a.activation(y_mlstm[:, t, c * AW:(c + 1) * AW], bank[t][:], ACT.Copy).then_inc(om_done, 1)

        def kt_high(a, t):
            a.wait_ge(kt_ps, t + 1)
            a.activation(kT_hi[:, :, t * P:(t + 1) * P], bank[6 + t % 2][:].rearrange("p (k c) -> p k c", k=4),
                         ACT.Copy).then_inc(kt_hi, 1)

        @block.scalar
        def _(a):
            links = [0]

            def link(ins):
                links[0] += 1
                ins.then_inc(achain, 1)
                a.wait_ge(achain, links[0])

            def cut(n):
                if n >= NSLOT:
                    return
                a.wait_ge(raw_in[n % RAW], 16 * (n // RAW + 1))
                if n >= RING:
                    a.wait_ge(w_used, n - RING + 1)
                a.activation(w_hi[:, n % RING, :], w_raw[:, n % RAW, :], ACT.Copy).then_inc(w_hi_done, 1)

            def x_hi(n):
                t, j = n // 2, n % 2
                a.wait_ge(xt_scaled, n + 1)
                a.activation(xT_hi[:, 4 * j:4 * j + 4, t * P:(t + 1) * P],
                             tmp[:, n % 2, :].rearrange("p (k c) -> p k c", k=4), ACT.Copy).then_inc(xt_hi, 1)

            for t in range(NT):
                x_hi(2 * t)
                x_hi(2 * t + 1)
                a.wait_ge(x_in[t], 16)
                if t:
                    a.wait_ge(ssx_done, t)
                a.activation(junk[:], x_sb[:, t, :], ACT.Square,
                             accum_out=ssx[:, t:t + 1]).then_inc(ssx_done, 1)
                if t < NT - 1:
                    cut(t)
            for n in range(NT - 1, AHEAD):
                cut(n)
            a.wait_ge(grow_ps, 1)
            a.activation(rows[0], bank[5][0:16, :], ACT.Abs).then_inc(absf_done, 1)
            a.wait_ge(absf_done, 1)
            a.activation(rows[1], rows[0], ACT.Exp, scale=-1.0).then_inc(expf_done, 1)
            cut(AHEAD)
            a.wait_ge(onep_done, 1)
            a.activation(rows[0], rows[2], ACT.Ln).then_inc(ln_done, 1)
            for n in range(1, 6):
                cut(AHEAD + n)
            a.wait_ge(aT_done, 1)
            a.activation(emt[:], bank[6][:, 0:NT * 32].rearrange("p (t c) -> p t c", t=NT)[:, :, 16:16 + MH],
                         ACT.Exp).then_inc(emt_done, 1)
            for n in range(6, NK):
                cut(AHEAD + n)
            for t in range(NT):
                projected(a, t)
                a.wait_ge(rx_done, 1)
                a.activation(mv_hi[:, t, :, 0:MD], bank[t][:].rearrange("p (h d) -> p h d", h=MH), ACT.Copy,
                             scale=rx[:, t:t + 1]).then_inc(mv_hi_done, 1)

            def decays(j):
                a.wait_ge(g_masked, j + 1)
                for h in range(MH):
                    a.activation(decay[j][:, h, :], decay[j][:, h, :], ACT.Exp,
                                 bias=aT[:, j, 4 * j + h:4 * j + h + 1]).then_inc(decay_done, 1)

            def conv_silu(n):
                a.wait_ge(conv_done, n + 1)
                a.activation(cacc[:, n % 2, :], cacc[:, n % 2, :], ACT.Silu).then_inc(silu_done, 1)
                a.wait_ge(silu_done, n + 1)
                if n >= 4:
                    a.wait_ge(st_ps, 4 * (n // 2 - 1))
                a.activation(qk_hi[:, n % 4, :], cacc[:, n % 2, :], ACT.Copy).then_inc(qk_hi_done, 1)

            def pm_high(n):
                h, j = n // NT, n % NT
                w = SEQ - P * j
                a.wait_ge(pm_done, n + 1)
                if h >= 1:
                    a.wait_ge(mpv_ps, 2 * h)
                a.activation(pm_hi[:, P_AT[j]:P_AT[j] + w], pm[:, n % 2, 0:w], ACT.Copy).then_inc(pm_hi_done, 1)

            for b in range(S_QK, S_AZ):
                cut(b + AHEAD)
                if b < S_QK + NT:
                    decays(b - S_QK)
                if b % 2 == 1 and b >= S_QK + 3:
                    conv_silu((b - S_QK - 3) // 2)
                if b in PE_ST:
                    for j in range(NT):
                        pm_high(PE_ST[b] * NT + j)
            for b in range(S_AZ, S_AK):
                cut(b + AHEAD)
                if b == S_AZ + 1:
                    conv_silu(7)
                if b in PE_ST:
                    for j in range(NT):
                        pm_high(PE_ST[b] * NT + j)
                if b in (S_MZ, S_MO):
                    for t in range(NT):
                        z_evac(a, b // NK - 4, t)
            for b in range(S_AK, S_OM):
                cut(b + AHEAD)
                if b == S_AK:
                    for t in range(NT):
                        z_evac(a, 2, t)
                if S_AK + 4 <= b < S_AK + 8:
                    t = b - S_AK - 4
                    a.wait_ge(ymt_scaled, t + 1)
                    a.activation(ymT_hi[:, :, t * P:(t + 1) * P], tmp[:, t % 2, :].rearrange("p (k c) -> p k c", k=4),
                                 ACT.Copy).then_inc(ymt_hi, 1)
                if b == S_AV:
                    for t in range(NT):
                        projected(a, 24 + t)
                        a.activation(keys[:, t, :], bank[t][:], ACT.Copy, scale=rx[:, t:t + 1]).then_inc(k_raw, 1)
                if S_AV + 2 <= b < S_AV + 6:
                    kt_high(a, b - S_AV - 2)
            for b in range(S_OM, S_AQ):
                if b + AHEAD < S_OA:
                    cut(b + AHEAD)
                if b == S_OM:
                    for t in range(NT):
                        projected(a, 28 + t)
                        a.activation(v_hi[:, t, :], bank[t][:], ACT.Copy, scale=rx[:, t:t + 1]).then_inc(v_hi_done, 1)
                if b == S_OM + 4:
                    for t in range(NT):
                        om_evac(a, 0, t)
            for n in range(S_AQ + AHEAD, S_OA):
                cut(n)
            for t in range(NT):
                om_evac(a, 1, t)

            def q_copy(i):
                t = NT - 1 - i
                projected(a, 40 + i)
                if i >= 2:
                    a.wait_ge(qt_ps, i - 1)
                a.activation(queries[:, i % 2, :], bank[i % 2][:], ACT.Copy, scale=rx[:, t:t + 1]).then_inc(q_raw, 1)

            def q_high(i):
                a.wait_ge(qt_ps, i + 1)
                if i >= 2:
                    a.wait_ge(score_ps, AH * (i - 1))
                a.activation(qT[:, 2 * (i % 2), :], bank[7][:], ACT.Copy).then_inc(qt_hi, 1)

            def ya_high(i):
                a.wait_ge(yat_scaled, i + 1)
                if i >= 2:
                    a.wait_ge(oa_ps, 2 * (i - 1))
                a.activation(yaT[:, 2 * (i % 2), :], tmp[:, i % 2, :], ACT.Copy).then_inc(yat_hi, 1)

            squares = {"ya": 0, "y": 0}

            def junk_free():
                a.wait_ge(ssx_done, NT)
                for kind, done in (("ya", ssa_done), ("y", ssy_done)):
                    if squares[kind]:
                        a.wait_ge(done, squares[kind])

            q_copy(0)
            q_high(0)
            for s in range(STEPS):
                if s < NU:
                    n = (unit(s)[0] + 1) * P
                    a.wait_ge(masked, s + 1)
                    if s >= 2:
                        a.wait_ge(pt_ps, s - 1)
                    a.activation(prob[:, s % 2, 0:n], sm[:, s % 2, 0:n], ACT.Exp, scale=-1.0, bias=mx[:, s:s + 1],
                                 accum_out=rsum[:, s:s + 1]).then_inc(prob_done, 1)
                u = s - LAG_T
                if 0 <= u < NU:
                    n = (unit(u)[0] + 1) * P
                    a.wait_ge(pt_ps, u + 1)
                    if u >= 2:
                        a.wait_ge(pv_ps, u - 1)
                    a.activation(pT[:, 2 * (u % 2), 0:n], bank[4 + u % 2][:, 0:n], ACT.Copy).then_inc(pt_hi, 1)
                for kind, i in EVENTS.get(s, ()):
                    if kind == "q_copy":
                        q_copy(i)
                    elif kind == "q_T":
                        q_high(i)
                    elif kind == "cut":
                        cut(i)
                    elif kind == "ya":
                        a.wait_ge(ya_done, i + 1)
                        junk_free()
                        squares["ya"] += 1
                        a.activation(junk[:, 0:AW], ya[:, i % 2, :], ACT.Square,
                                     accum_out=ssa[:, i:i + 1]).then_inc(ssa_done, 1)
                    elif kind == "ya_T":
                        ya_high(i)
                    elif kind == "y":
                        i, c = i
                        a.wait_ge(y_done, 2 * i + c + 1)
                        junk_free()
                        squares["y"] += 1
                        a.activation(junk[:, 0:AW], yb[:, i % 2, c * AW:(c + 1) * AW], ACT.Square,
                                     accum_out=ssy[:, 2 * i + c:2 * i + c + 1]).then_inc(ssy_done, 1)


        @block.vector
        def _(v):
            links = [0]

            def link(ins):
                links[0] += 1
                ins.then_inc(vchain, 1)
                v.wait_ge(vchain, links[0])

            def f32(ap):
                return ap.bitcast(F32)

            def cut(n):
                if n >= NSLOT:
                    return
                v.wait_ge(w_hi_done, n + 1)
                v.tensor_tensor(w_lo[:, n % RING, :], w_raw[:, n % RAW, :], f32(w_hi[:, n % RING, :]),
                                ALU.subtract).then_inc(w_lo_done, 1)

            def scaled(dst, src, row):
                return v.tensor_tensor(dst.rearrange("p (k c) -> p k c", k=4), src.rearrange("p (k c) -> p k c", k=4),
                                       pcol[:, row:row + 4].unsqueeze(2).to_broadcast([P, 4, P]), ALU.mult)

            v.wait_ge(par_ps, 1)
            v.tensor_copy(pcol[:], bank[3][:, 0:R_END]).then_inc(par_done, 1)
            v.wait_ge(par_done, 1)

            def x_scale(n):
                v.wait_ge(xt_ps, n + 1)
                if n >= 2:
                    v.wait_ge(xt_lo, n - 1)
                scaled(tmp[:, n % 2, :], bank[4 + n % 4][:], R_PRE + 4 * (n % 2)).then_inc(xt_scaled, 1)

            def x_low(n):
                t, j = n // 2, n % 2
                part = (slice(None), slice(4 * j, 4 * j + 4), slice(t * P, (t + 1) * P))
                v.wait_ge(xt_hi, n + 1)
                v.tensor_tensor(xT_lo[part], tmp[:, n % 2, :].rearrange("p (k c) -> p k c", k=4), f32(xT_hi[part]),
                                ALU.subtract).then_inc(xt_lo, 1)

            for n in range(2 * NT):
                x_scale(n)
                if n >= 1:
                    x_low(n - 1)
                if n == 1:
                    v.wait_ge(wg_in, 16)
                    for q in range(2):
                        raw = wg_raw[:, :, 4 * q:4 * q + 4].unsqueeze(2).to_broadcast([P, NK, NT, MH])
                        hi = wg_hi[:, :, 16 * q:16 * q + 16].rearrange("p k (j h) -> p k j h", j=NT)
                        lo = wg_lo[:, :, 16 * q:16 * q + 16].rearrange("p k (j h) -> p k j h", j=NT)
                        link(v.tensor_copy(hi, raw))
                        v.tensor_tensor(lo, raw, f32(hi), ALU.subtract).then_inc(wg_done, 1)
                if n == 2:
                    v.wait_ge(bias_in, 32)
                    for q in range(2):
                        ins = v.tensor_copy(bias32[:, 16 * q:16 * q + 16].rearrange("p (j h) -> p j h", j=NT),
                                            bias8[:, 4 * q:4 * q + 4].unsqueeze(1).to_broadcast([P, NT, MH]))
                        link(ins)
                if n in (3, 5, 7):
                    cut(n // 2 - 1)
            x_low(2 * NT - 1)
            v.wait_ge(ssx_done, NT)
            v.tensor_scalar(msx[:], ssx[:], 1.0 / D, EPS, ALU.mult, ALU.add).then_inc(msx_done, 1)
            for n in range(NT - 1, AHEAD):
                cut(n)
            v.wait_ge(rx_done, 1)
            v.wait_ge(gate_ps, 1)
            for t in range(NT):
                v.scalar_tensor_tensor(out=gsb[:, t, :], in0=bank[3][:, 32 * t:32 * t + 32], scalar=rx[:, t:t + 1],
                                       in1=bias32[:], op0=ALU.mult, op1=ALU.add).then_inc(gate_sb, 1)
            v.wait_ge(consts, 6)
            v.wait_ge(xt_lo, 2 * NT)
            for t in range(NT):
                v.tensor_scalar(tmp[:, 0, t * P:(t + 1) * P], ident[:], rx[:, t:t + 1], None,
                                ALU.mult).then_inc(diag_done, 1)
            v.wait_ge(expf_done, 1)
            v.tensor_scalar(rows[2], rows[1], 1.0, None, ALU.add).then_inc(onep_done, 1)
            v.wait_ge(onep_done, 1)
            cut(AHEAD)
            link(v.scalar_tensor_tensor(out=rows[1], in0=rows[2], scalar=-1.0, in1=rows[1], op0=ALU.add,
                                        op1=ALU.subtract))
            v.wait_ge(ln_done, 1)
            link(v.scalar_tensor_tensor(out=rows[3], in0=bank[5][0:16, :], scalar=0.0, in1=rows[0], op0=ALU.min,
                                        op1=ALU.subtract))
            link(v.tensor_tensor(rows[3], rows[3], rows[1], ALU.add))
            link(v.tensor_tensor(rows[0], rows[3], rows[7], ALU.mult))
            link(v.tensor_tensor_scan(rows[1], rows[7], rows[0], 0.0, ALU.mult, ALU.add))
            link(v.tensor_tensor_scan(rows[2], rows[3], bank[4][0:16, :], 0.0, ALU.add, ALU.max))
            link(v.tensor_tensor(rows[5], bank[4][0:16, :], rows[1], ALU.subtract))
            link(v.tensor_scalar(rows[6], rows[2], -1.0, None, ALU.mult))
            v.tensor_tensor(rows[4], rows[1], rows[2], ALU.subtract).then_inc(grows_done, 1)
            v.wait_ge(grows_done, 1)
            for n in range(1, 6):
                cut(AHEAD + n)
            v.wait_ge(gcol_ps, 1)
            v.tensor_copy(aT[:], bank[6][:, 0:NT * 32].rearrange("p (t c) -> p t c", t=NT)[:, :, 0:16])\
                .then_inc(aT_done, 1)
            v.wait_ge(rbc_ps, 1)
            v.tensor_copy(rbc[:], bank[7][:]).then_inc(rbc_done, 1)
            for n in range(6, NK):
                cut(AHEAD + n)
            v.wait_ge(mv_ones, 2)
            for t in range(NT):
                v.wait_ge(mv_hi_done, t + 1)
                v.scalar_tensor_tensor(out=mv_lo[:, t, :, 0:MD], in0=bank[t][:].rearrange("p (h d) -> p h d", h=MH),
                                       scalar=rx[:, t:t + 1], in1=f32(mv_hi[:, t, :, 0:MD]), op0=ALU.mult,
                                       op1=ALU.subtract).then_inc(mv_lo_done, 1)

            def conv(n):
                c = n // 2 + MH * (n % 2)
                u, acc = upad[:, n % 2, :], cacc[:, n % 2, :]
                projected(v, 4 + n)
                v.wait_ge(rbc_done, 1)
                if n >= 2:
                    v.wait_ge(conv_done, n - 1)
                    v.wait_ge(qk_lo_done, n - 1)
                v.tensor_tensor(u[:, KCONV - 1:KCONV - 1 + SEQ], bank[n % 4][:], rbc[:], ALU.mult).then_inc(u_done, 1)
                v.wait_ge(u_done, n + 1)
                v.wait_ge(cleared, 5)
                tap = [pcol[:, R_CW + 8 * j + c:R_CW + 8 * j + c + 1] for j in range(KCONV)]
                link(v.tensor_scalar(acc, u[:, 0:SEQ], tap[0], pcol[:, R_CB + c:R_CB + c + 1], ALU.mult, ALU.add))
                for j in range(1, KCONV):
                    ins = v.scalar_tensor_tensor(out=acc, in0=u[:, j:j + SEQ], scalar=tap[j], in1=acc, op0=ALU.mult,
                                                 op1=ALU.add)
                    if j < KCONV - 1:
                        link(ins)
                    else:
                        ins.then_inc(conv_done, 1)

            def qk_low(n):
                v.wait_ge(qk_hi_done, n + 1)
                v.tensor_tensor(qk_lo[:, n % 4, :], cacc[:, n % 2, :], f32(qk_hi[:, n % 4, :]),
                                ALU.subtract).then_inc(qk_lo_done, 1)

            def pm_low(n):
                j = n % NT
                w = SEQ - P * j
                v.wait_ge(pm_hi_done, n + 1)
                v.tensor_tensor(pm_lo[:, P_AT[j]:P_AT[j] + w], pm[:, n % 2, 0:w], f32(pm_hi[:, P_AT[j]:P_AT[j] + w]),
                                ALU.subtract).then_inc(pm_lo_done, 1)

            def weighted(h):
                for j in range(NT):
                    n = h * NT + j
                    w = SEQ - P * j
                    v.wait_ge(st_ps, n + 1)
                    v.wait_ge(decay_done, MH * NT)
                    if n >= 2:
                        v.wait_ge(pm_lo_done, n - 1)
                    v.scalar_tensor_tensor(out=pm[:, n % 2, 0:w], in0=bank[4 + n % 2][:, 0:w], scalar=K_SCALE,
                                           in1=decay[j][:, h, :], op0=ALU.mult, op1=ALU.mult).then_inc(pm_done, 1)
                    if j >= 1:
                        pm_low(n - 1)
                pm_low(h * NT + NT - 1)

            def head_stats(n):
                h, t0 = n // 2, 2 * (n % 2)
                pv = bank[6 + n % 2][:, 0:2 * MV].rearrange("p (t c) -> p t c", t=2)
                v.wait_ge(mpv_ps, n + 1)
                v.wait_ge(emt_done, 1)
                if n:
                    v.wait_ge(ym_done, n)
                for q in range(2):
                    v.bn_stats(bns[:, q, :], pv[:, q, 0:MD])
                link(v.scalar_tensor_tensor(out=den[:], in0=pv[:, :, MD], scalar=-1.0, in1=emt[:, t0:t0 + 2, h],
                                            op0=ALU.mult, op1=ALU.max))
                link(v.tensor_tensor(den[:], pv[:, :, MD], den[:], ALU.max))
                for q in range(2):
                    v.bn_aggr(mva[:, q, :], bns[:, q, :])
                link(v.reciprocal(iden[:], den[:]))
                link(v.tensor_tensor(vs1[:], mva[:, :, 1], iden[:], ALU.mult))
                link(v.tensor_tensor(vs1[:], vs1[:], iden[:], ALU.mult))
                v.tensor_scalar(vs2[:], vs1[:], EPS, None, ALU.add).then_inc(var_done, 1)

            def head_norm(n):
                h, t0 = n // 2, 2 * (n % 2)
                pv = bank[6 + n % 2][:, 0:2 * MV].rearrange("p (t c) -> p t c", t=2)
                v.wait_ge(vr_done, n + 1)
                link(v.tensor_tensor(hsc[:], vr[:], iden[:], ALU.mult))
                for q in range(2):
                    ins = v.tensor_scalar(ym[:, t0 + q, h * MD:(h + 1) * MD], pv[:, q, 0:MD], mva[:, q, 0:1],
                                          hsc[:, q:q + 1], ALU.subtract, ALU.mult)
                ins.then_inc(ym_done, 1)

            for b in range(S_QK, S_AK):
                cut(b + AHEAD)
                if b % 2 == 1 and b < S_AZ:
                    conv((b - S_QK) // 2)
                if b % 2 == 0 and S_QK + 4 <= b < S_AZ + 4:
                    qk_low((b - S_QK - 4) // 2)
                if b in PE_ST:
                    weighted(PE_ST[b])
                for q in (0, 1):
                    if b - q in PE_PV:
                        head_stats(2 * PE_PV[b - q] + q)
                    if b - q - 1 in PE_PV:
                        head_norm(2 * PE_PV[b - q - 1] + q)

            def rope(buf, t):
                xs = buf.rearrange("p (h d) -> p h d", h=AH)
                ra_, rb = (rtmp[:, q, :].rearrange("p (h d) -> p h d", h=AH) for q in range(2))

                def table(at, n):
                    return rope_sb[:, t, at:at + n].unsqueeze(1).to_broadcast([P, AH, n])

                v.tensor_tensor(ra_, xs[:, :, 0:ROT], table(0, ROT), ALU.mult)
                v.tensor_tensor(rb[:, :, 0:HALF], xs[:, :, HALF:ROT], table(ROT, HALF), ALU.mult)
                link(v.tensor_tensor(rb[:, :, HALF:ROT], xs[:, :, 0:HALF], table(ROT + HALF, HALF), ALU.mult))
                return v.tensor_tensor(xs[:, :, 0:ROT], ra_, rb, ALU.add)

            def kt_low(t):
                part = (slice(None), slice(None), slice(t * P, (t + 1) * P))
                v.wait_ge(kt_hi, t + 1)
                v.tensor_tensor(kT_lo[part], bank[6 + t % 2][:].rearrange("p (k c) -> p k c", k=4), f32(kT_hi[part]),
                                ALU.subtract).then_inc(kt_lo, 1)

            v.wait_ge(rope_in, 16)
            for b in range(S_AK, S_OM):
                cut(b + AHEAD)
                if S_AK + 4 <= b < S_AK + 8:
                    t = b - S_AK - 4
                    v.wait_ge(ymt_ps, t + 1)
                    v.wait_ge(gate_mul, NT)
                    if t >= 2:
                        v.wait_ge(ymt_lo, t - 1)
                    scaled(tmp[:, t % 2, :], bank[4 + t % 2][:], R_MG).then_inc(ymt_scaled, 1)
                    v.wait_ge(ymt_hi, t + 1)
                    cols = slice(t * P, (t + 1) * P)
                    v.tensor_tensor(ymT_lo[:, :, cols], tmp[:, t % 2, :].rearrange("p (k c) -> p k c", k=4),
                                    f32(ymT_hi[:, :, cols]), ALU.subtract).then_inc(ymt_lo, 1)
                if S_AV <= b < S_AV + 4:
                    t = b - S_AV
                    v.wait_ge(k_raw, t + 1)
                    if t:
                        v.wait_ge(k_roped, t)
                    rope(keys[:, t, :], t).then_inc(k_roped, 1)
                if S_AV + 2 <= b < S_AV + 6:
                    kt_low(b - S_AV - 2)
            for b in range(S_OM, S_AQ):
                if b + AHEAD < S_OA:
                    cut(b + AHEAD)
                if b == S_OM:
                    for t in range(NT):
                        v.wait_ge(v_hi_done, t + 1)
                        v.scalar_tensor_tensor(out=v_lo[:, t, :], in0=bank[t][:], scalar=rx[:, t:t + 1],
                                               in1=f32(v_hi[:, t, :]), op0=ALU.mult, op1=ALU.subtract)\
                            .then_inc(v_lo_done, 1)
            for n in range(S_AQ + AHEAD, S_OA):
                cut(n)

            def q_rope(i):
                v.wait_ge(q_raw, i + 1)
                v.wait_ge(k_roped, NT)
                if i:
                    v.wait_ge(q_roped, i)
                rope(queries[:, i % 2, :], NT - 1 - i).then_inc(q_roped, 1)

            def q_low(i):
                v.wait_ge(qt_hi, i + 1)
                v.tensor_tensor(qT[:, 2 * (i % 2) + 1, :], bank[7][:], f32(qT[:, 2 * (i % 2), :]),
                                ALU.subtract).then_inc(qt_lo, 1)

            q_rope(0)
            q_low(0)
            for s in range(STEPS):
                if s < NU:
                    n = (unit(s)[0] + 1) * P
                    v.wait_ge(score_ps, s + 1)
                    if s >= 2:
                        v.wait_ge(prob_done, s - 1)
                    v.tensor_tensor_reduce(sm[:, s % 2, 0:n], bank[2 + s % 2][:, 0:n], causal[:, SEQ - n:], -Q_SCALE,
                                           BIG, ALU.add, ALU.min, mx[:, s:s + 1]).then_inc(masked, 1)
                u = s - LAG_T
                if 0 <= u < NU:
                    n = (unit(u)[0] + 1) * P
                    v.wait_ge(pt_hi, u + 1)
                    v.tensor_tensor(pT[:, 2 * (u % 2) + 1, 0:n], bank[4 + u % 2][:, 0:n],
                                    f32(pT[:, 2 * (u % 2), 0:n]), ALU.subtract).then_inc(pt_lo, 1)
                for kind, i in EVENTS.get(s, ()):
                    if kind == "q_copy":
                        q_rope(i)
                    elif kind == "q_T":
                        q_low(i)
                    elif kind == "cut":
                        cut(i)
                    elif kind == "ya":
                        v.wait_ge(pv_ps, AH * (i + 1))
                        link(v.reciprocal(rrec[:, AH * i:AH * i + AH], rsum[:, AH * i:AH * i + AH]))
                        v.tensor_tensor(ya[:, i % 2, :].rearrange("p (h d) -> p h d", h=AH),
                                        bank[6][:].rearrange("p (h d) -> p h d", h=AH),
                                        rrec[:, AH * i:AH * i + AH].unsqueeze(2).to_broadcast([P, AH, DH]),
                                        ALU.mult).then_inc(ya_done, 1)
                    elif kind == "ya_ms":
                        v.wait_ge(ssa_done, i + 1)
                        v.tensor_scalar(msa[:, i:i + 1], ssa[:, i:i + 1], 1.0 / AW, EPS, ALU.mult, ALU.add)\
                            .then_inc(msa_done, 1)
                    elif kind == "ya_gate":
                        v.wait_ge(ra_done, i + 1)
                        v.scalar_tensor_tensor(out=ya[:, i % 2, :], in0=ya[:, i % 2, :], scalar=ra[:, i:i + 1],
                                               in1=silu_az[:, NT - 1 - i, :], op0=ALU.mult, op1=ALU.mult)\
                            .then_inc(ya_gated, 1)
                    elif kind == "ya_T":
                        v.wait_ge(yat_ps, i + 1)
                        v.wait_ge(ymt_lo, NT)
                        if i >= 2:
                            v.wait_ge(yat_lo, i - 1)
                        scaled(tmp[:, i % 2, :], bank[7][:], R_AG).then_inc(yat_scaled, 1)
                        v.wait_ge(yat_hi, i + 1)
                        v.tensor_tensor(yaT[:, 2 * (i % 2) + 1, :], tmp[:, i % 2, :], f32(yaT[:, 2 * (i % 2), :]),
                                        ALU.subtract).then_inc(yat_lo, 1)
                    elif kind == "y":
                        i, c = i
                        cols = slice(c * AW, (c + 1) * AW)
                        v.wait_ge(oa_ps, 2 * i + c + 1)
                        v.wait_ge(om_done, 2 * NT)
                        if i >= 2:
                            v.wait_ge(out_ready, 2 * (i - 1))
                        v.tensor_tensor(yb[:, i % 2, cols], bank[c][:], y_mlstm[:, NT - 1 - i, cols],
                                        ALU.add).then_inc(y_done, 1)
                    elif kind == "y_ms":
                        v.wait_ge(ssy_done, 2 * i + 2)
                        link(v.tensor_tensor(msy[:, i:i + 1], ssy[:, 2 * i:2 * i + 1], ssy[:, 2 * i + 1:2 * i + 2],
                                             ALU.add))
                        v.tensor_scalar(msy[:, i:i + 1], msy[:, i:i + 1], 1.0 / D, EPS, ALU.mult, ALU.add)\
                            .then_inc(msy_done, 1)
                    elif kind == "y_fin":
                        v.wait_ge(ry_done, i + 1)
                        v.wait_ge(post_in, 16)
                        for c in range(2):
                            cols = slice(c * AW, (c + 1) * AW)
                            v.scalar_tensor_tensor(out=yb[:, i % 2, cols], in0=yb[:, i % 2, cols],
                                                   scalar=ry[:, i:i + 1], in1=post[:, cols], op0=ALU.mult,
                                                   op1=ALU.mult).then_inc(y_normed, 1)

        @block.tensor
        def _(pe):
            def product(o, hi, lo, m_hi, m_lo, start, stop):
                pe.matmul(o, hi, m_hi, start=start, stop=False)
                pe.matmul(o, hi, m_lo, start=False, stop=False)
                return pe.matmul(o, lo, m_hi, start=False, stop=stop)

            def x_part(k, t):
                cols = slice(t * P, (t + 1) * P)
                return xT_hi[:, k, cols], xT_lo[:, k, cols]

            def w_part(n, cols=slice(0, AW)):
                return w_hi[:, n % RING, cols], w_lo[:, n % RING, cols]

            pe.wait_ge(consts, 6)
            pe.wait_ge(par_in, 80)
            pe.transpose(bank[3][:, 0:R_END], prow[:], ident[0:R_END, 0:R_END]).then_inc(par_ps, 1)
            for n in range(2 * NT):
                t, j = n // 2, n % 2
                if j == 0:
                    pe.wait_ge(x_in[t], 16)
                if n >= 4:
                    pe.wait_ge(xt_scaled, n - 3)
                for k in range(4):
                    mm = pe.transpose(bank[4 + n % 4][:, k * P:(k + 1) * P],
                                      x_sb[:, t, (4 * j + k) * P:(4 * j + k + 1) * P], ident[:])
                mm.then_inc(xt_ps, 1)
            pe.wait_ge(wg_done, 2)
            pe.wait_ge(par_done, 1)
            for t in range(NT):
                pe.wait_ge(xt_lo, 2 * t + 2)
                for k in range(NK):
                    mm = product(bank[3][:, 32 * t:32 * t + 32], *x_part(k, t), wg_hi[:, k, :], wg_lo[:, k, :],
                                 k == 0, k == NK - 1)
            mm.then_inc(gate_ps, 1)

            def by_slot(n, k, nk, p0, part, free):
                pe.wait_ge(w_lo_done, n + 1)
                for t in range(NT):
                    if k == 0:
                        free(t)
                    mm = product(bank[t][:], *part(k, t), *w_part(n), k == 0, k == nk - 1)
                    if k == nk - 1 and t < NT - 1:
                        mm.then_inc(proj_ps, 1)
                mm.then_inc(w_used, 1)

            def gate_rows():
                pe.wait_ge(gate_sb, NT)
                pe.wait_ge(xt_scaled, 2 * NT)
                for q in range(2):
                    for t in range(NT):
                        mm = pe.transpose(bank[4 + q][0:16, t * P:(t + 1) * P], gsb[:, t, 16 * q:16 * q + 16], ident[:])
                mm.then_inc(grow_ps, 1)

            def rms_rows():
                for t in range(NT):
                    pe.wait_ge(diag_done, t + 1)
                    mm = pe.matmul(bank[7][:, t * P:(t + 1) * P], ones[:], tmp[:, 0, t * P:(t + 1) * P],
                                   start=True, stop=True)
                mm.then_inc(rbc_ps, 1)

            def gate_cols():
                pe.wait_ge(grows_done, 1)
                for t in range(NT):
                    pe.transpose(bank[6][:, 32 * t:32 * t + 16], rows[5][:, t * P:(t + 1) * P], ident[0:16, 0:16])
                    mm = pe.transpose(bank[6][:, 32 * t + 16:32 * t + 32], rows[6][:, t * P:(t + 1) * P],
                                      ident[0:16, 0:16])
                mm.then_inc(gcol_ps, 1)

            def free_mv(t):
                if t == 3:
                    pe.wait_ge(gate_sb, NT)

            for b in range(S_MV, S_QK):
                by_slot(b, b - S_MV, NK, 0, x_part, free_mv)
                if b == S_MV:
                    gate_rows()
                if b == S_MV + 2:
                    rms_rows()
                if b == S_MV + 4:
                    gate_cols()

            def head_scores(h):
                q, kk = 2 * (h % 2), 2 * (h % 2) + 1
                pe.wait_ge(qk_lo_done, 2 * h + 2)
                for j in range(NT):
                    n = h * NT + j
                    if n < 2:
                        pe.wait_ge(grows_done, 1)
                    else:
                        pe.wait_ge(pm_done, n - 1)
                    src = slice(j * P, (j + 1) * P)
                    product(bank[4 + n % 2][:, 0:SEQ - j * P], qk_hi[:, kk, src], qk_lo[:, kk, src],
                            qk_hi[:, q, j * P:], qk_lo[:, q, j * P:], True, True).then_inc(st_ps, 1)

            def head_values(h):
                pe.wait_ge(mv_lo_done, NT)
                pe.wait_ge(pm_lo_done, NT * (h + 1))
                for half in range(2):
                    n = 2 * h + half
                    if n == 0:
                        pe.wait_ge(emt_done, 1)
                    elif n == 1:
                        pe.wait_ge(rbc_done, 1)
                    else:
                        pe.wait_ge(ym_done, n - 1)
                    for q in range(2):
                        t = 2 * half + q
                        for j in range(t + 1):
                            w = slice(P_AT[j] + (t - j) * P, P_AT[j] + (t - j + 1) * P)
                            mm = product(bank[6 + half][:, MV * q:MV * (q + 1)], pm_hi[:, w], pm_lo[:, w],
                                         mv_hi[:, j, h, :], mv_lo[:, j, h, :], j == 0, j == t)
                    mm.then_inc(mpv_ps, 1)

            def mlstm(b):
                if b in PE_ST:
                    head_scores(PE_ST[b])
                if b in PE_PV:
                    head_values(PE_PV[b])

            for b in range(S_QK, S_AZ):
                p = 4 + (b - S_QK) // 2
                pe.wait_ge(w_lo_done, b + 1)
                if b % 2 == 0:
                    if p < 8:
                        pe.wait_ge(mv_lo_done, p - 3)
                    else:
                        pe.wait_ge(u_done, p - 7)
                for kk in range(4):
                    k = 4 * (b % 2) + kk
                    mm = product(bank[p % 4][:], *w_part(b, slice(kk * P, (kk + 1) * P)), xT_hi[:, k, :],
                                 xT_lo[:, k, :], k == 0, k == NK - 1)
                mm.then_inc(w_used, 1)
                mlstm(b)
            for b in range(S_AZ, S_AK):
                p0 = 12 + NT * ((b - S_AZ) // NK)
                by_slot(b, b % NK, NK, p0, x_part,
                        lambda t: pe.wait_ge(u_done, 5 + t) if p0 == 12 else pe.wait_ge(z_done, p0 - 15 + t))
                mlstm(b)
            for b in range(S_AK, S_AV):
                by_slot(b, b % NK, NK, 24, x_part, lambda t: pe.wait_ge(z_done, 9 + t))
                t = b - S_AK - 4
                if t >= 0:
                    pe.wait_ge(ym_gated, t + 1)
                    if t < 2:
                        pe.wait_ge(pm_lo_done, MH * NT)
                    else:
                        pe.wait_ge(ymt_scaled, t - 1)
                    for k in range(4):
                        mm = pe.transpose(bank[4 + t % 2][:, k * P:(k + 1) * P], ym[:, t, k * P:(k + 1) * P], ident[:])
                    mm.then_inc(ymt_ps, 1)
            for b in range(S_AV, S_OM):
                by_slot(b, b % NK, NK, 28, x_part, lambda t: pe.wait_ge(k_raw, t + 1))
                t = b - S_AV - 2
                if 0 <= t < NT:
                    pe.wait_ge(k_roped, t + 1)
                    if t < 2:
                        pe.wait_ge(ym_done, 2 * MH)
                    else:
                        pe.wait_ge(kt_lo, t - 1)
                    for k in range(4):
                        mm = pe.transpose(bank[6 + t % 2][:, k * P:(k + 1) * P], keys[:, t, k * P:(k + 1) * P],
                                          ident[:])
                    mm.then_inc(kt_ps, 1)

            def ym_part(k, t):
                cols = slice(t * P, (t + 1) * P)
                return ymT_hi[:, k, cols], ymT_lo[:, k, cols]

            pe.wait_ge(ymt_lo, NT)
            for b in range(S_OM, S_AQ):
                c = (b - S_OM) // 4
                by_slot(b, b % 4, 4, 32 + NT * c, ym_part,
                        lambda t: pe.wait_ge(om_done, t + 1) if c else pe.wait_ge(v_lo_done, t + 1))

            def aq(i, k):
                n = S_AQ + k
                if i == 0:
                    pe.wait_ge(w_lo_done, n + 1)
                if k == 0:
                    if i < 2:
                        pe.wait_ge(om_done, NT + i + 1)
                    else:
                        pe.wait_ge(q_raw, i - 1)
                mm = product(bank[i % 2][:], *x_part(k, NT - 1 - i), *w_part(n), k == 0, k == NK - 1)
                if i == NT - 1:
                    mm.then_inc(w_used, 1)
                elif k == NK - 1:
                    mm.then_inc(proj_ps, 1)

            def turn_q(i):
                pe.wait_ge(q_roped, i + 1)
                if i == 0:
                    pe.wait_ge(kt_lo, NT)
                else:
                    pe.wait_ge(qt_lo, i)
                    if i >= 2:
                        pe.wait_ge(yat_scaled, 1)
                for k in range(4):
                    mm = pe.transpose(bank[7][:, k * P:(k + 1) * P], queries[:, i % 2, k * P:(k + 1) * P], ident[:])
                mm.then_inc(qt_ps, 1)

            def turn_ya(i):
                pe.wait_ge(ya_gated, i + 1)
                pe.wait_ge(qt_lo, (2, 4, 4, 4)[i])
                if i >= 1:
                    pe.wait_ge(yat_scaled, i)
                for k in range(4):
                    mm = pe.transpose(bank[7][:, k * P:(k + 1) * P], ya[:, i % 2, k * P:(k + 1) * P], ident[:])
                mm.then_inc(yat_ps, 1)

            def oa(i, k):
                c, kk = k // 4, k % 4
                pe.wait_ge(yat_lo, i + 1)
                pe.wait_ge(w_lo_done, S_OA + k + 1)
                if kk == 0:
                    if i == 0:
                        pe.wait_ge(q_raw, 3 + c)
                    else:
                        pe.wait_ge(y_done, 2 * i - 1 + c)
                cols = slice(kk * P, (kk + 1) * P)
                mm = product(bank[c][:], yaT[:, 2 * (i % 2), cols], yaT[:, 2 * (i % 2) + 1, cols], *w_part(S_OA + k),
                             kk == 0, kk == 3)
                if kk == 3:
                    mm.then_inc(oa_ps, 1)

            for k in range(NK):
                aq(0, k)
            turn_q(0)
            for s in range(STEPS):
                events = EVENTS.get(s, ())
                if s < NU:
                    t, h = unit(s)
                    i, n, half = s // AH, (t + 1) * P, slice(DH * (h % 2), DH * (h % 2 + 1))
                    pe.wait_ge(qt_lo, i + 1)
                    if s < 2:
                        pe.wait_ge(om_done, 2 * NT)
                    else:
                        pe.wait_ge(masked, s - 1)
                    cols = slice(h // 2 * P, (h // 2 + 1) * P)
                    product(bank[2 + s % 2][:, 0:n], qT[half, 2 * (i % 2), cols], qT[half, 2 * (i % 2) + 1, cols],
                            kT_hi[half, h // 2, 0:n], kT_lo[half, h // 2, 0:n], True, True).then_inc(score_ps, 1)
                for kind, i in events:
                    if kind == "aq":
                        aq(*i)
                    elif kind == "oa":
                        oa(*i)
                u = s - LAG_T
                if 0 <= u < NU:
                    t, h = unit(u)
                    pe.wait_ge(prob_done, u + 1)
                    if u >= 2:
                        pe.wait_ge(pt_lo, u - 1)
                    for j in range(t + 1):
                        mm = pe.transpose(bank[4 + u % 2][:, j * P:(j + 1) * P], prob[:, u % 2, j * P:(j + 1) * P],
                                          ident[:])
                    mm.then_inc(pt_ps, 1)
                u = s - LAG_PV
                if 0 <= u < NU:
                    t, h = unit(u)
                    pe.wait_ge(pt_lo, u + 1)
                    pe.wait_ge(v_lo_done, NT)
                    if h == 0 and u:
                        pe.wait_ge(ya_done, u // AH)
                    for j in range(t + 1):
                        cols = slice(j * P, (j + 1) * P)
                        mm = product(bank[6][:, h * DH:(h + 1) * DH], pT[:, 2 * (u % 2), cols],
                                     pT[:, 2 * (u % 2) + 1, cols], v_hi[:, j, h * DH:(h + 1) * DH],
                                     v_lo[:, j, h * DH:(h + 1) * DH], j == 0, j == t)
                    mm.then_inc(pv_ps, 1)
                for kind, i in events:
                    if kind == "q_T":
                        turn_q(i)
                    elif kind == "ya_T":
                        turn_ya(i)


_INS = ["x", "pre_norm_g", "w_in", "mlstm_i_bias", "mlstm_f_bias", "conv_w", "conv_b", "attn_out_g", "mlstm_out_g",
        "w_out", "post_norm_g"]


def rope_table():
    inv = np.power(np.float32(500000.0), -np.arange(HALF, dtype=np.float32) * np.float32(2.0) / np.float32(ROT))
    ang = np.arange(SEQ, dtype=np.float32)[:, None] * inv.astype(np.float32)[None, :]
    cos, sin = np.cos(ang), np.sin(ang)
    return np.concatenate([cos, cos, -sin, sin], axis=1).astype(np.float32)


def kernel(**inputs):
    import concourse.bacc as _bacc
    from concourse.bass_utils import run_bass_kernel_spmd as _run

    nc = _bacc.Bacc("TRN2", target_bir_lowering=False, num_devices=1)
    arrays = {f"in_{n}": np.ascontiguousarray(inputs[n]) for n in _INS}
    arrays["in_rope"] = rope_table()
    args = [nc.dram_tensor(n, a.shape, mybir.dt.from_np(a.dtype), kind="ExternalInput").ap() for n, a in arrays.items()]
    args.append(nc.dram_tensor("out_y", (1, SEQ, D), F32, kind="ExternalOutput").ap())
    build(nc, *args)
    r = _run(nc, [arrays], core_ids=[0])
    return r.results[0]["out_y"]
```

```python
from contextlib import ExitStack

import numpy as np

import concourse.bass as bass
from concourse import mybir

F32 = mybir.dt.float32
F32R = mybir.dt.float32r
ALU = mybir.AluOpType
ACT = mybir.ActivationFunctionType

P = 128
SEQ = 512
D = 1024
NT = SEQ // P
NK = D // P
AW = 512
AH, DH = 8, 64
MH, MD = 4, 128
MV = MD + 2
ROT = DH // 4
HALF = ROT // 2
KCONV = 4
EPS = 1e-6
FAR = -1e30
BIG = 3e38
Q_SCALE = DH ** -0.5
K_SCALE = MD ** -0.5

AQ, AK, AV, AZ, MQ, MK, MVC, MO, MZ, MG = (AW * i for i in range(10))

SLOTS = [("in", "cols", k, MVC) for k in range(NK)]
for _h in range(MH):
    for _c in (MQ, MK):
        SLOTS += [("in", "heads", k, _c + _h * MD) for k in (0, 4)]
for _c in (AZ, AK, AV, AQ, MZ, MO):
    SLOTS += [("in", "cols", k, _c) for k in range(NK)]
for _r in (4, 0):
    SLOTS += [("out", "cols", _r + k, c * AW) for c in range(2) for k in range(4)]
S_MV, S_QK, S_AZ, S_AK, S_AV, S_AQ, S_MZ, S_MO, S_OM, S_OA = 0, 8, 24, 32, 40, 48, 56, 64, 72, 80
NSLOT = len(SLOTS)
RAW = 4
RING = 8
AHEAD = 6
X_AFTER = {3: 1, 5: 2, 7: 3}

R_PRE, R_AG, R_MG, R_CB, R_CW, R_END = 0, 8, 12, 16, 24, 56

F_E, F_U, F_ACC, F_PM, F_END = 0, 5120, 6152, 7176, 8200
F_X = 0
F_SC, F_SM, F_P, F_YA, F_XR, F_Y = 0, 1024, 2048, 3072, 4096, 6144
R_QK, R_MV, R_P = 0, 4096, 8256
R_KT, R_V, R_QT, R_PT, R_SIZE = 0, 4096, 8192, 12288, 14336
E_AT = [0, 2048, 3584, 4608]
P_AT = [0, 512, 896, 1152]

NU = NT * AH


U_AZ, U_AK, U_AV, U_AQ, U_MZ, U_MO, U_OM = 12, 16, 20, 24, 28, 32, 36
UNIT_SLOT = {3: S_QK, 15: S_AK, 19: S_AV, 23: S_AQ, 27: S_MZ, 31: S_MO, 35: S_OM, 42: S_OM + 4, 43: S_OA}
UNIT_SLOT.update({4 + n: S_QK + 2 * n + 2 for n in range(2 * MH)})

PE_ST = {S_QK + 7 + 4 * h + j: (h, j) for h in range(MH) for j in range(NT)}
PE_PV = {S_QK + 11 + 4 * h + q: (h, q) for h in range(MH) for q in range(2)}

LAG_T, LAG_PV = 2, 3
EVENTS = {}
PRIORITY = ("q_T", "z_part", "om", "oa", "cut", "ya", "ya_ms", "ya_gate", "z", "om_out", "y", "y_ms", "y_fin", "turn")


def _event(step, kind, *what):
    EVENTS.setdefault(step, []).append((kind, what))


_event(0, "q_T", 2)
_event(1, "q_T", 3)
Z_END = [0] + [3 * n - 1 for n in range(1, 2 * NT)]
for _n in range(1, 2 * NT):
    for _k in range(NK):
        _event(Z_END[_n] - 2 + _k // 3, "z_part", _n, _k)
        if _n in (NT - 1, 2 * NT - 1):
            _event(Z_END[_n] - 2 + _k // 3, "cut", (S_MO if _n == NT - 1 else S_OM) + _k)
    _event(Z_END[_n], "z", _n)
OM_START = Z_END[-1] + 1
for _n in range(2 * NT):
    for _k in range(4):
        _event(OM_START + _n, "om", _n, _k)
        if _n // 2 == NT - 1:
            _event(OM_START + _n, "cut", S_OA + 4 * (_n % 2) + _k)
    _event(OM_START + _n, "om_out", _n)
TURNS = [(Z_END[NT + _t] + 1, "ym", _t) for _t in range(NT)]
TURNS += [(OM_START + 1, "ya", 0), (OM_START + 2, "ya", 1), (AH * 3 + LAG_PV + 2, "ya", 2), (AH * 4 + LAG_PV + 2, "ya", 3)]
for _n, _turn in enumerate(TURNS):
    _event(_turn[0], "turn", _n)
OA_STEPS = ((30,) * 4 + (32,) * 4, (35,) * 4 + (36,) * 4, (37,) * 4 + (38,) * 4, (39,) * 8)
for _i, _steps in enumerate(OA_STEPS):
    _s = AH * _i + AH - 1 + LAG_PV
    _event(_s, "ya", _i)
    _event(_s + 1, "ya_ms", _i)
    _event(_s + 2, "ya_gate", _i)
    for _k in range(8):
        _event(_steps[_k], "oa", _i, _k)
        if _k % 4 == 3:
            _event(_steps[_k], "y", _i, _k // 4)
    _event(_steps[-1] + 1, "y_ms", _i)
    _event(_steps[-1] + 2, "y_fin", _i)
STEPS = max(EVENTS) + 1
for _s in EVENTS:
    EVENTS[_s].sort(key=lambda e: PRIORITY.index(e[0]))


def oa_bank(i, c):
    return 3 if c and i >= 2 else 0


def unit(u):
    return NT - 1 - u // AH, u % AH


def build(nc, x, pre_g, w_in, i_bias, f_bias, conv_w, conv_b, attn_g, mlstm_g, w_out, post_g, rope, out):
    with ExitStack() as ctx:
        def sb(name, shape, dt=F32):
            return ctx.enter_context(nc.sbuf_tensor(name, shape, dt))

        def sem(name):
            return ctx.enter_context(nc.semaphore(name))

        xT_hi = sb("xT_hi", [P, NK, SEQ], F32R)
        xT_lo = sb("xT_lo", [P, NK, SEQ], F32R)
        w_raw = sb("w_raw", [P, RAW, AW])
        w_hi = sb("w_hi", [P, RING, AW], F32R)
        w_lo = sb("w_lo", [P, RING, AW], F32R)
        farena = sb("farena", [P, F_END])
        rarena = sb("rarena", [P, R_SIZE], F32R)
        silu_az = sb("silu_az", [P, NT, AW])
        gy = sb("gy", [P, 2, NT, AW])
        post = sb("post", [P, D])
        tmp = sb("tmp", [P, 2, AW])
        rbc = sb("rbc", [P, SEQ])
        junk = sb("junk", [P, D], mybir.dt.bfloat16)
        ident = sb("ident", [P, P])
        ones = sb("ones", [P, P])
        causal = sb("causal", [P, SEQ])
        causalT = sb("causalT", [P, P])
        rope_sb = sb("rope_sb", [P, NT, 2 * ROT])
        rtmp = sb("rtmp", [P, 2, AH * ROT])
        prow = sb("prow", [R_AG, P])
        prow2 = sb("prow2", [R_END - R_AG, P])
        pcol = sb("pcol", [P, R_END])
        wg_raw = sb("wg_raw", [P, NK, 8])
        wg_hi = sb("wg_hi", [P, NK, 32], F32R)
        wg_lo = sb("wg_lo", [P, NK, 32], F32R)
        bias8 = sb("bias8", [P, 8])
        bias32 = sb("bias32", [P, 32])
        bcol = sb("bcol", [16, 2])
        aT = sb("aT", [P, NT, 16])
        emt = sb("emt", [P, NT, MH])
        ssx = sb("ssx", [P, NT])
        msx = sb("msx", [P, NT])
        rx = sb("rx", [P, NT])
        mhalf = sb("mhalf", [P, NT])
        bns = sb("bns", [P, 2, 6])
        mva = sb("mva", [P, 2, 2])
        den = sb("den", [P, 2])
        iden = sb("iden", [P, 2])
        vs1 = sb("vs1", [P, 2])
        vs2 = sb("vs2", [P, 2])
        vr = sb("vr", [P, 2])
        hsc = sb("hsc", [P, 2])
        mx = sb("mx", [P, NU])
        rsum = sb("rsum", [P, NU])
        rrec = sb("rrec", [P, NU])
        ssa = sb("ssa", [P, NT])
        msa = sb("msa", [P, NT])
        ra = sb("ra", [P, NT])
        ssy = sb("ssy", [P, 2 * NT])
        msy = sb("msy", [P, NT])
        ry = sb("ry", [P, NT])

        bank = [ctx.enter_context(nc.psum_tensor(f"bank{i}", [P, 512], F32)) for i in range(8)]

        def f_part(at, *shape):
            n = int(np.prod(shape))
            v = farena[:, at:at + n]
            return v if len(shape) == 1 else v.rearrange("p (a b) -> p a b", a=shape[0]) if len(shape) == 2 \
                else v.rearrange("p (a b c) -> p a b c", a=shape[0], b=shape[1])

        def r_part(at, *shape):
            n = int(np.prod(shape))
            v = rarena[:, at:at + n]
            return v if len(shape) == 1 else v.rearrange("p (a b) -> p a b", a=shape[0]) if len(shape) == 2 \
                else v.rearrange("p (a b c) -> p a b c", a=shape[0], b=shape[1])

        x_sb = f_part(F_X, NT, D)
        decay = [f_part(F_E + E_AT[j], MH, SEQ - P * j) for j in range(NT)]
        upad = f_part(F_U, 2, 516)
        cacc = f_part(F_ACC, 2, SEQ)
        pm = f_part(F_PM, 2, SEQ)
        qk_hi = r_part(R_QK, 4, SEQ)
        qk_lo = r_part(R_QK + 4 * SEQ, 4, SEQ)
        mv_hi = r_part(R_MV, NT, MH, MV)
        mv_lo = r_part(R_MV + NT * MH * MV, NT, MH, MV)
        pm_hi = r_part(R_P, 2, 1280)
        pm_lo = r_part(R_P + 2560, 2, 1280)
        gate, ym = gy[:, 0], gy[:, 1]
        rows = [gy[0:16, i // 4, i % 4, :] for i in range(8)]
        gate_rows = gy[0:32, 1, 2, :]
        y_mlstm = gy
        turned = f_part(F_SC, 2, AW)
        queries = f_part(F_Y, NT, AW)
        keys = f_part(F_XR, NT, AW)
        sm = f_part(F_SM, 2, SEQ)
        prob = f_part(F_P, 2, SEQ)
        ya = f_part(F_YA, 2, AW)
        xr = f_part(F_XR, 2, D)
        yb = f_part(F_Y, 2, D)
        kT_hi = r_part(R_KT, 4, SEQ)
        kT_lo = r_part(R_KT + 4 * SEQ, 4, SEQ)
        v_hl = r_part(R_V, NT * AH, 2 * DH)
        qT = r_part(R_QT, 2 * NT, AW)
        pT = r_part(R_PT, 4, SEQ)
        g_dram = nc.dram_tensor("g_rows", (16, SEQ), F32, kind="Internal").ap()

        x_in = [sem(f"x_in{t}") for t in range(NT)]
        par_in = sem("par_in")
        wg_in = sem("wg_in")
        bias_in = sem("bias_in")
        rope_in = sem("rope_in")
        post_in = sem("post_in")
        raw_in = [sem(f"raw_in{r}") for r in range(RAW)]
        w_hi_done = sem("w_hi_done")
        w_lo_done = sem("w_lo_done")
        w_used = sem("w_used")
        consts = sem("consts")
        cleared = sem("cleared")
        par_ps = sem("par_ps")
        par_done = sem("par_done")
        xt_ps = sem("xt_ps")
        xt_scaled = sem("xt_scaled")
        xt_hi = sem("xt_hi")
        xt_lo = sem("xt_lo")
        ssx_done = sem("ssx_done")
        msx_done = sem("msx_done")
        rx_done = sem("rx_done")
        diag_done = sem("diag_done")
        rbc_ps = sem("rbc_ps")
        rbc_done = sem("rbc_done")
        wg_done = sem("wg_done")
        gate_ps = sem("gate_ps")
        gate_sb = sem("gate_sb")
        bias32_done = sem("bias32_done")
        bias_ps = sem("bias_ps")
        bcol_done = sem("bcol_done")
        fgate_ps = sem("fgate_ps")
        igate_done = sem("igate_done")
        par2_in = sem("par2_in")
        par2_ps = sem("par2_ps")
        ident_done = sem("ident_done")
        absf_done = sem("absf_done")
        expf_done = sem("expf_done")
        onep_done = sem("onep_done")
        ln_done = sem("ln_done")
        grows_done = sem("grows_done")
        gcol_ps = sem("gcol_ps")
        aT_done = sem("aT_done")
        emt_done = sem("emt_done")
        g_out = sem("g_out")
        g_back = sem("g_back")
        g_masked = sem("g_masked")
        decay_done = sem("decay_done")
        proj_ps = sem("proj_ps")
        mv_hi_done = sem("mv_hi_done")
        mv_lo_done = sem("mv_lo_done")
        mv_ones = sem("mv_ones")
        u_done = sem("u_done")
        conv_done = sem("conv_done")
        silu_done = sem("silu_done")
        qk_hi_done = sem("qk_hi_done")
        qk_lo_done = sem("qk_lo_done")
        st_ps = sem("st_ps")
        pm_done = sem("pm_done")
        pm_hi_done = sem("pm_hi_done")
        pm_lo_done = sem("pm_lo_done")
        mpv_ps = sem("mpv_ps")
        var_done = sem("var_done")
        vr_done = sem("vr_done")
        ym_done = sem("ym_done")
        az_done = sem("az_done")
        z_done = sem("z_done")
        gate_mul = sem("gate_mul")
        turn_ps = sem("turn_ps")
        turn_scaled = sem("turn_scaled")
        turn_hi = sem("turn_hi")
        turn_lo = sem("turn_lo")
        ym_gated = sem("ym_gated")
        k_raw = sem("k_raw")
        k_roped = sem("k_roped")
        kt_ps = sem("kt_ps")
        kt_hi = sem("kt_hi")
        kt_lo = sem("kt_lo")
        v_hi_done = sem("v_hi_done")
        v_lo_done = sem("v_lo_done")
        q_raw = sem("q_raw")
        q_roped = sem("q_roped")
        qt_ps = sem("qt_ps")
        qt_hi = sem("qt_hi")
        qt_lo = sem("qt_lo")
        score_ps = sem("score_ps")
        masked = sem("masked")
        prob_done = sem("prob_done")
        pt_ps = sem("pt_ps")
        pt_hi = sem("pt_hi")
        pt_lo = sem("pt_lo")
        pv_ps = sem("pv_ps")
        ya_done = sem("ya_done")
        ssa_done = sem("ssa_done")
        msa_done = sem("msa_done")
        ra_done = sem("ra_done")
        ya_gated = sem("ya_gated")
        om_done = sem("om_done")
        oa_ps = sem("oa_ps")
        y_done = sem("y_done")
        ssy_done = sem("ssy_done")
        msy_done = sem("msy_done")
        ry_done = sem("ry_done")
        y_normed = sem("y_normed")
        xr_in = [sem(f"xr_in{t}") for t in range(NT)]
        out_ready = sem("out_ready")
        out_done = [sem(f"out_done{t}") for t in range(NT)]
        vchain = sem("vchain")
        achain = sem("achain")

        block = ctx.enter_context(nc.Block())

        def projected(eng, p):
            if p in UNIT_SLOT:
                eng.wait_ge(w_used, UNIT_SLOT[p])
            else:
                eng.wait_ge(proj_ps, sum(1 for q in range(p + 1) if q not in UNIT_SLOT))

        def turn_tile(n):
            step, kind, i = TURNS[n]
            return (0, i) if kind == "ym" else (4, NT - 1 - i)

        def store(sp, i):
            t = NT - 1 - i
            for c in range(2):
                cols = slice(c * AW, (c + 1) * AW)
                sp.wait_ge(out_ready, 2 * i + c + 1)
                sp.dma_start(out[0, t * P:(t + 1) * P, cols], xr[:, i % 2, cols]).then_inc(out_done[i], 16)

        @block.sync
        def _(sp):
            x2 = x.rearrange("b s d -> (b s) d")

            def load_x(t):
                sp.dma_start(x_sb[:, t, :], x2[t * P:(t + 1) * P, :]).then_inc(x_in[t], 16)

            load_x(0)
            for n, (mat, kind, k, c) in enumerate(SLOTS):
                if n >= RAW:
                    sp.wait_ge(w_lo_done, n - RAW + 1)
                w = w_in if mat == "in" else w_out
                if kind == "cols":
                    src = w[0, k * P:(k + 1) * P, c:c + AW]
                    dst = w_raw[:, n % RAW, :]
                else:
                    src = w[0, k * P:(k + 4) * P, c:c + MD].rearrange("(k p) c -> p k c", p=P)
                    dst = w_raw[:, n % RAW, :].rearrange("p (k c) -> p k c", k=4)
                sp.dma_start(dst, src).then_inc(raw_in[n % RAW], 16)
                if n in X_AFTER:
                    load_x(X_AFTER[n])
                if n == NK - 1:
                    sp.dma_start(wg_raw[:], w_in[0, :, MG:MG + 8].rearrange("(k p) c -> p k c", p=P)).then_inc(wg_in, 16)
                if n == S_QK + 4:
                    sp.dma_start(rope_sb[:], rope.rearrange("(t p) c -> p t c", p=P)).then_inc(rope_in, 16)
                    sp.dma_start(post[:], post_g.to_broadcast([P, D])).then_inc(post_in, 16)
            for i in range(NT):
                t = NT - 1 - i
                if i == 0:
                    sp.wait_ge(pm_lo_done, MH * NT)
                    sp.wait_ge(mpv_ps, 2 * MH)
                    sp.wait_ge(kt_ps, NT)
                if i >= 2:
                    sp.wait_ge(out_done[i - 2], 32)
                sp.dma_start(xr[:, i % 2, :], x2[t * P:(t + 1) * P, :]).then_inc(xr_in[i], 16)
                if i >= 1:
                    store(sp, i - 1)
            store(sp, NT - 1)
            for i in range(NT):
                sp.wait_ge(out_done[i], 32)

        @block.gpsimd
        def _(g):
            def rows_of(p):
                return p.rearrange("o (c p) -> (o c) p", p=P)

            g.dma_start(prow[:], rows_of(pre_g)).then_inc(par_in, 16)
            g.memset(ident[:], 0.0).then_inc(cleared, 1)
            g.wait_ge(cleared, 1)
            g.affine_select(out=ident[:], in_=ident[:], compare_op=ALU.not_equal, fill=1.0, base=0,
                            pattern=[[-1, P]], channel_multiplier=1).then_inc(ident_done, 1)
            g.dma_start(prow2[0:4, :], rows_of(attn_g)).then_inc(par2_in, 16)
            g.dma_start(prow2[4:8, :], rows_of(mlstm_g)).then_inc(par2_in, 16)
            g.dma_start(prow2[8:16, :], rows_of(conv_b)).then_inc(par2_in, 16)
            g.dma_start(prow2[16:48, :], conv_w.rearrange("o j (c p) -> (o j c) p", p=P)).then_inc(par2_in, 16)
            g.dma_start(bias8[:, 0:MH], i_bias.to_broadcast([P, MH])).then_inc(bias_in, 16)
            g.dma_start(bias8[:, MH:2 * MH], f_bias.to_broadcast([P, MH])).then_inc(bias_in, 16)
            g.memset(causal[:], 0.0).then_inc(cleared, 1)
            g.memset(causalT[:], 0.0).then_inc(cleared, 1)
            g.memset(rows[7], 1.0).then_inc(cleared, 1)
            g.memset(upad[:, :, 0:KCONV - 1], 0.0).then_inc(cleared, 1)
            g.wait_ge(cleared, 5)
            g.memset(ones[:], 1.0).then_inc(consts, 1)
            g.memset(mhalf[:], -0.5).then_inc(consts, 1)
            g.affine_select(out=causal[:, SEQ - P:], in_=causal[:, SEQ - P:], compare_op=ALU.is_ge, fill=FAR, base=0,
                            pattern=[[-1, P]], channel_multiplier=1).then_inc(consts, 1)
            g.affine_select(out=causalT[:], in_=causalT[:], compare_op=ALU.is_ge, fill=FAR, base=0,
                            pattern=[[1, P]], channel_multiplier=-1).then_inc(consts, 1)
            g.affine_select(out=rows[7].rearrange("p (t c) -> p t c", t=NT),
                            in_=rows[7].rearrange("p (t c) -> p t c", t=NT), compare_op=ALU.is_ge, fill=0.0,
                            base=3, pattern=[[4, NT], [0, P]], channel_multiplier=-1).then_inc(consts, 1)
            g.memset(mv_hi[:, :, :, MD:MV].bitcast(F32), 1.0).then_inc(mv_ones, 1)
            g.memset(mv_lo[:, :, :, MD:MV].bitcast(F32), 0.0).then_inc(mv_ones, 1)

            def rsqrt(dst, src):
                return g.tensor_tensor(dst, src, mhalf[:, 0:src.shape[1]], ALU.pow)

            g.wait_ge(consts, 2)
            g.wait_ge(msx_done, 1)
            rsqrt(rx[:], msx[:]).then_inc(rx_done, 1)
            g.wait_ge(grows_done, 1)
            g.dma_start(g_dram, rows[4]).then_inc(g_out, 16)
            g.wait_ge(g_out, 16)
            for j in range(NT):
                g.dma_start(decay[j], g_dram[4 * j:4 * j + 4, j * P:].rearrange("(o h) c -> o h c", o=1)
                            .to_broadcast([P, MH, SEQ - j * P])).then_inc(g_back, 16)
            g.wait_ge(g_back, 16 * NT)
            for j in range(NT):
                v = decay[j][:, :, 0:P]
                g.tensor_tensor(v, v, causalT[:].unsqueeze(1).to_broadcast([P, MH, P]), ALU.add).then_inc(g_masked, 1)
            for n in range(2 * MH):
                g.wait_ge(var_done, n + 1)
                rsqrt(vr[:], vs2[:]).then_inc(vr_done, 1)

            def z_gate(n):
                t = n - NT
                g.wait_ge(z_done, n + 1)
                g.tensor_tensor(gate[:, t, :], gate[:, t, :], tmp[:, t % 2, :], ALU.mult).then_inc(gate_mul, 1)
                g.wait_ge(gate_mul, t + 1)
                if t == 0:
                    g.wait_ge(ym_done, 2 * MH)
                g.tensor_tensor(ym[:, t, :], ym[:, t, :], gate[:, t, :], ALU.mult).then_inc(ym_gated, 1)

            for s in range(STEPS):
                for kind, what in EVENTS.get(s, ()):
                    i = what[0]
                    if kind == "z" and i >= NT:
                        z_gate(i)
                    elif kind == "ya_ms":
                        g.wait_ge(msa_done, i + 1)
                        rsqrt(ra[:, i:i + 1], msa[:, i:i + 1]).then_inc(ra_done, 1)
                    elif kind == "y_ms":
                        g.wait_ge(msy_done, i + 1)
                        rsqrt(ry[:, i:i + 1], msy[:, i:i + 1]).then_inc(ry_done, 1)
                    elif kind == "y_fin":
                        g.wait_ge(xr_in[i], 16)
                        for c in range(2):
                            cols = slice(c * AW, (c + 1) * AW)
                            g.wait_ge(y_normed, 2 * i + c + 1)
                            g.tensor_tensor(xr[:, i % 2, cols], xr[:, i % 2, cols], yb[:, i % 2, cols], ALU.add)\
                                .then_inc(out_ready, 1)

        def az_evac(a, t):
            projected(a, U_AZ + t)
            a.activation(silu_az[:, t, :], bank[t][:], ACT.Silu, scale=rx[:, t:t + 1]).then_inc(az_done, 1)

        def z_evac(a, n):
            t = n % NT
            projected(a, U_MZ + n)
            if n >= NT + 2:
                a.wait_ge(gate_mul, t - 1)
            a.activation(gate[:, t, :] if n < NT else tmp[:, t % 2, :], bank[0][:],
                         ACT.Silu if n < NT else ACT.Sigmoid, scale=rx[:, t:t + 1]).then_inc(z_done, 1)

        def om_evac(a, n):
            t, c = n // 2, n % 2
            projected(a, U_OM + n)
            a.wait_ge(turn_ps, t + 1)
            a.wait_ge(ym_gated, t + 1)
            a.activation(y_mlstm[:, c, t, :], bank[0][:], ACT.Copy).then_inc(om_done, 1)

        def kt_high(a, t):
            a.wait_ge(kt_ps, t + 1)
            a.activation(kT_hi[:, :, t * P:(t + 1) * P], bank[6 + t % 2][:].rearrange("p (k c) -> p k c", k=4),
                         ACT.Copy).then_inc(kt_hi, 1)

        @block.scalar
        def _(a):
            links = [0]

            def link(ins):
                links[0] += 1
                ins.then_inc(achain, 1)
                a.wait_ge(achain, links[0])

            def cut(n):
                if n >= NSLOT:
                    return
                a.wait_ge(raw_in[n % RAW], 16 * (n // RAW + 1))
                if n >= RING:
                    a.wait_ge(w_used, n - RING + 1)
                a.activation(w_hi[:, n % RING, :], w_raw[:, n % RAW, :], ACT.Copy).then_inc(w_hi_done, 1)

            def x_hi(n):
                t, j = n // 2, n % 2
                a.wait_ge(xt_scaled, n + 1)
                a.activation(xT_hi[:, 4 * j:4 * j + 4, t * P:(t + 1) * P],
                             tmp[:, n % 2, :].rearrange("p (k c) -> p k c", k=4), ACT.Copy).then_inc(xt_hi, 1)

            def x_squares(t):
                if t:
                    a.wait_ge(ssx_done, t)
                a.wait_ge(x_in[t], 16)
                a.activation(junk[:], x_sb[:, t, :], ACT.Square, accum_out=ssx[:, t:t + 1]).then_inc(ssx_done, 1)

            x_hi(0)
            x_hi(1)
            for n in range(4):
                cut(n)
            x_hi(2)
            x_hi(3)
            for n in range(4, 8):
                cut(n)
            x_squares(0)
            x_squares(1)
            x_hi(4)
            x_hi(5)
            x_squares(2)
            x_hi(6)
            x_hi(7)
            x_squares(3)
            for n in range(RING, RING + 4):
                cut(n)
            a.wait_ge(fgate_ps, 1)
            a.wait_ge(bcol_done, 1)
            a.activation(rows[0], bank[5][0:16, :], ACT.Abs, bias=bcol[:, 1:2]).then_inc(absf_done, 1)
            a.wait_ge(absf_done, 1)
            a.activation(rows[1], rows[0], ACT.Exp, scale=-1.0).then_inc(expf_done, 1)
            a.wait_ge(onep_done, 1)
            a.activation(rows[0], rows[2], ACT.Ln).then_inc(ln_done, 1)
            for t in range(NT):
                projected(a, t)
                a.wait_ge(rx_done, 1)
                a.activation(mv_hi[:, t, :, 0:MD], bank[t][:].rearrange("p (h d) -> p h d", h=MH), ACT.Copy,
                             scale=rx[:, t:t + 1]).then_inc(mv_hi_done, 1)

            def decays(j):
                a.wait_ge(g_masked, j + 1)
                for h in range(MH):
                    a.activation(decay[j][:, h, :], decay[j][:, h, :], ACT.Exp,
                                 bias=aT[:, j, 4 * j + h:4 * j + h + 1]).then_inc(decay_done, 1)

            def conv_silu(n):
                a.wait_ge(conv_done, n + 1)
                a.activation(cacc[:, n % 2, :], cacc[:, n % 2, :], ACT.Silu).then_inc(silu_done, 1)
                a.wait_ge(silu_done, n + 1)
                if n >= 4:
                    a.wait_ge(st_ps, 4 * (n // 2 - 1))
                a.activation(qk_hi[:, n % 4, :], cacc[:, n % 2, :], ACT.Copy).then_inc(qk_hi_done, 1)

            def pm_high(n):
                h, j = n // NT, n % NT
                w = SEQ - P * j
                a.wait_ge(pm_done, n + 1)
                if h >= 2:
                    a.wait_ge(mpv_ps, 2 * (h - 1))
                a.activation(pm_hi[:, h % 2, P_AT[j]:P_AT[j] + w], pm[:, n % 2, 0:w], ACT.Copy).then_inc(pm_hi_done, 1)

            for b in range(S_QK, S_AV):
                if b == S_AK:
                    for t in range(NT):
                        az_evac(a, t)
                if b == S_QK:
                    cut(b + AHEAD - 2)
                    cut(b + AHEAD - 1)
                cut(b + AHEAD)
                if b == S_QK + 6:
                    a.wait_ge(aT_done, 1)
                    a.activation(emt[:], bank[6][:, 0:NT * 32].rearrange("p (t c) -> p t c", t=NT)[:, :, 16:16 + MH],
                                 ACT.Exp).then_inc(emt_done, 1)
                    for j in range(NT):
                        decays(j)
                if b % 2 == 1 and S_QK + 3 <= b < S_QK + 3 + 4 * MH:
                    conv_silu((b - S_QK - 3) // 2)
                if b in PE_ST:
                    h, j = PE_ST[b]
                    pm_high(h * NT + j)
            for b in range(S_AV, S_MZ):
                if b == S_AV:
                    for t in range(NT):
                        projected(a, U_AK + t)
                        a.activation(keys[:, t, :], bank[t][:], ACT.Copy, scale=rx[:, t:t + 1]).then_inc(k_raw, 1)
                if b == S_AQ:
                    for t in range(NT):
                        projected(a, U_AV + t)
                        a.activation(v_hl[:, t * AH:(t + 1) * AH, 0:DH], bank[t][:].rearrange("p (h d) -> p h d", h=AH),
                                     ACT.Copy, scale=rx[:, t:t + 1]).then_inc(v_hi_done, 1)
                cut(b + AHEAD)
                if S_AV + 2 <= b < S_AV + 6:
                    kt_high(a, b - S_AV - 2)

            def q_copy(i):
                t = NT - 1 - i
                projected(a, U_AQ + i)
                a.activation(queries[:, i, :], bank[i][:], ACT.Copy, scale=rx[:, t:t + 1]).then_inc(q_raw, 1)

            def q_high(i):
                a.wait_ge(qt_ps, i + 1)
                a.activation(qT[:, 2 * i, :], bank[4 + i][:], ACT.Copy).then_inc(qt_hi, 1)

            def turn_high(n):
                k, t = turn_tile(n)
                a.wait_ge(turn_scaled, n + 1)
                projected(a, U_MO + t)
                a.activation(xT_hi[:, k:k + 4, t * P:(t + 1) * P], turned[:, n % 2, :].rearrange("p (k c) -> p k c", k=4),
                             ACT.Copy).then_inc(turn_hi, 1)

            squares = {"ya": 0, "y": 0}

            def junk_free():
                a.wait_ge(ssx_done, NT)
                for kind, done in (("ya", ssa_done), ("y", ssy_done)):
                    if squares[kind]:
                        a.wait_ge(done, squares[kind])

            q_copy(0)
            q_copy(1)
            cut(S_MZ + AHEAD)
            q_copy(2)
            q_copy(3)
            cut(S_MZ + AHEAD + 1)
            q_high(0)
            q_high(1)
            z_evac(a, 0)
            for s in range(STEPS):
                if s < NU:
                    n = (unit(s)[0] + 1) * P
                    a.wait_ge(masked, s + 1)
                    if s >= 2:
                        a.wait_ge(pt_ps, s - 1)
                    a.activation(prob[:, s % 2, 0:n], sm[:, s % 2, 0:n], ACT.Exp, scale=-1.0, bias=mx[:, s:s + 1],
                                 accum_out=rsum[:, s:s + 1]).then_inc(prob_done, 1)
                for kind, what in EVENTS.get(s, ()):
                    if kind == "z":
                        z_evac(a, *what)
                    elif kind == "om_out":
                        om_evac(a, *what)
                u = s - LAG_T
                if 0 <= u < NU:
                    n = (unit(u)[0] + 1) * P
                    a.wait_ge(pt_ps, u + 1)
                    if u >= 2:
                        a.wait_ge(pv_ps, u - 1)
                    a.activation(pT[:, 2 * (u % 2), 0:n], bank[4 + u % 2][:, 0:n], ACT.Copy).then_inc(pt_hi, 1)
                for kind, what in EVENTS.get(s, ()):
                    i = what[0]
                    if kind == "q_T":
                        q_high(i)
                    elif kind == "cut":
                        cut(i)
                    elif kind == "turn":
                        turn_high(i)
                    elif kind == "ya":
                        a.wait_ge(ya_done, i + 1)
                        junk_free()
                        squares["ya"] += 1
                        a.activation(junk[:, 0:AW], ya[:, i % 2, :], ACT.Square,
                                     accum_out=ssa[:, i:i + 1]).then_inc(ssa_done, 1)
                    elif kind == "y":
                        i, c = what
                        a.wait_ge(y_done, 2 * i + c + 1)
                        junk_free()
                        squares["y"] += 1
                        a.activation(junk[:, 0:AW], yb[:, i % 2, c * AW:(c + 1) * AW], ACT.Square,
                                     accum_out=ssy[:, 2 * i + c:2 * i + c + 1]).then_inc(ssy_done, 1)


        @block.vector
        def _(v):
            links = [0]

            def link(ins):
                links[0] += 1
                ins.then_inc(vchain, 1)
                v.wait_ge(vchain, links[0])

            def f32(ap):
                return ap.bitcast(F32)

            def cut(n):
                if n >= NSLOT:
                    return
                v.wait_ge(w_hi_done, n + 1)
                v.tensor_tensor(w_lo[:, n % RING, :], w_raw[:, n % RAW, :], f32(w_hi[:, n % RING, :]),
                                ALU.subtract).then_inc(w_lo_done, 1)

            def scaled(dst, src, row):
                return v.tensor_tensor(dst.rearrange("p (k c) -> p k c", k=4), src.rearrange("p (k c) -> p k c", k=4),
                                       pcol[:, row:row + 4].unsqueeze(2).to_broadcast([P, 4, P]), ALU.mult)

            v.wait_ge(par_ps, 1)
            v.tensor_copy(pcol[:, 0:R_AG], bank[3][:, 0:R_AG]).then_inc(par_done, 1)
            v.wait_ge(par_done, 1)

            def x_scale(n):
                v.wait_ge(xt_ps, n + 1)
                if n >= 2:
                    v.wait_ge(xt_lo, n - 1)
                scaled(tmp[:, n % 2, :], bank[4 + n % 4][:], R_PRE + 4 * (n % 2)).then_inc(xt_scaled, 1)

            def x_low(n):
                t, j = n // 2, n % 2
                part = (slice(None), slice(4 * j, 4 * j + 4), slice(t * P, (t + 1) * P))
                v.wait_ge(xt_hi, n + 1)
                v.tensor_tensor(xT_lo[part], tmp[:, n % 2, :].rearrange("p (k c) -> p k c", k=4), f32(xT_hi[part]),
                                ALU.subtract).then_inc(xt_lo, 1)

            def x_cut(t):
                for n in (2 * t, 2 * t + 1):
                    x_scale(n)
                for n in (2 * t, 2 * t + 1):
                    x_low(n)

            x_cut(0)
            for n in range(4):
                cut(n)
            x_cut(1)
            for n in range(4, 8):
                cut(n)
            x_cut(2)
            v.wait_ge(wg_in, 16)
            v.wait_ge(bias_in, 32)
            for q in range(2):
                raw = wg_raw[:, :, 4 * q:4 * q + 4].unsqueeze(2).to_broadcast([P, NK, NT, MH])
                hi = wg_hi[:, :, 16 * q:16 * q + 16].rearrange("p k (j h) -> p k j h", j=NT)
                lo = wg_lo[:, :, 16 * q:16 * q + 16].rearrange("p k (j h) -> p k j h", j=NT)
                link(v.tensor_copy(hi, raw))
                v.tensor_tensor(lo, raw, f32(hi), ALU.subtract).then_inc(wg_done, 1)
                v.tensor_copy(bias32[:, 16 * q:16 * q + 16].rearrange("p (j h) -> p j h", j=NT),
                              bias8[:, 4 * q:4 * q + 4].unsqueeze(1).to_broadcast([P, NT, MH])).then_inc(bias32_done, 1)
            x_cut(3)
            v.wait_ge(par2_ps, 1)
            v.tensor_copy(pcol[:, R_AG:], bank[3][:, 0:R_END - R_AG]).then_inc(par_done, 1)
            v.wait_ge(ssx_done, NT)
            v.tensor_scalar(msx[:], ssx[:], 1.0 / D, EPS, ALU.mult, ALU.add).then_inc(msx_done, 1)
            v.wait_ge(rx_done, 1)
            for t in range(NT):
                v.tensor_scalar(rbc[:, t * P:(t + 1) * P], ident[:], rx[:, t:t + 1], None,
                                ALU.mult).then_inc(diag_done, 1)
            cut(RING)
            cut(RING + 1)
            v.wait_ge(rbc_ps, 1)
            v.tensor_copy(rbc[:], bank[7][:]).then_inc(rbc_done, 1)
            v.wait_ge(rbc_done, 1)
            v.wait_ge(gate_ps, 1)
            v.wait_ge(consts, 5)
            v.tensor_tensor(gate_rows, bank[4][0:32, :], rbc[0:32, :], ALU.mult).then_inc(gate_sb, 1)
            v.wait_ge(gate_sb, 1)
            v.wait_ge(bias_ps, 1)
            v.tensor_copy(bcol[:], bank[6][0:16, 0:2 * P].rearrange("p (a c) -> p a c", a=2)[:, :, 0])\
                .then_inc(bcol_done, 1)
            v.wait_ge(bcol_done, 1)
            cut(RING + 2)
            cut(RING + 3)
            v.wait_ge(fgate_ps, 1)
            v.tensor_scalar(rows[6], rows[6], bcol[:, 0:1], None, ALU.add).then_inc(igate_done, 1)
            v.wait_ge(expf_done, 1)
            v.tensor_scalar(rows[2], rows[1], 1.0, None, ALU.add).then_inc(onep_done, 1)
            v.wait_ge(onep_done, 1)
            link(v.scalar_tensor_tensor(out=rows[1], in0=rows[2], scalar=-1.0, in1=rows[1], op0=ALU.add,
                                        op1=ALU.subtract))
            link(v.tensor_scalar(rows[3], bank[5][0:16, :], bcol[:, 1:2], 0.0, ALU.add, ALU.min))
            link(v.tensor_tensor(rows[3], rows[3], rows[1], ALU.add))
            v.wait_ge(ln_done, 1)
            link(v.tensor_tensor(rows[3], rows[3], rows[0], ALU.subtract))
            link(v.tensor_tensor(rows[0], rows[3], rows[7], ALU.mult))
            link(v.tensor_tensor_scan(rows[1], rows[7], rows[0], 0.0, ALU.mult, ALU.add))
            v.wait_ge(igate_done, 1)
            link(v.tensor_tensor_scan(rows[2], rows[3], rows[6], 0.0, ALU.add, ALU.max))
            link(v.tensor_tensor(rows[5], rows[6], rows[1], ALU.subtract))
            link(v.tensor_scalar(rows[0], rows[2], -1.0, None, ALU.mult))
            v.tensor_tensor(rows[4], rows[1], rows[2], ALU.subtract).then_inc(grows_done, 1)
            v.wait_ge(grows_done, 1)
            v.wait_ge(mv_ones, 2)
            for t in range(NT):
                v.wait_ge(mv_hi_done, t + 1)
                v.scalar_tensor_tensor(out=mv_lo[:, t, :, 0:MD], in0=bank[t][:].rearrange("p (h d) -> p h d", h=MH),
                                       scalar=rx[:, t:t + 1], in1=f32(mv_hi[:, t, :, 0:MD]), op0=ALU.mult,
                                       op1=ALU.subtract).then_inc(mv_lo_done, 1)

            def conv(n):
                c = n // 2 + MH * (n % 2)
                u, acc = upad[:, n % 2, :], cacc[:, n % 2, :]
                projected(v, 4 + n)
                v.wait_ge(rbc_done, 1)
                if n >= 2:
                    v.wait_ge(conv_done, n - 1)
                    v.wait_ge(qk_lo_done, n - 1)
                v.tensor_tensor(u[:, KCONV - 1:KCONV - 1 + SEQ], bank[n % 4][:], rbc[:], ALU.mult).then_inc(u_done, 1)
                v.wait_ge(u_done, n + 1)
                v.wait_ge(cleared, 5)
                tap = [pcol[:, R_CW + 8 * j + c:R_CW + 8 * j + c + 1] for j in range(KCONV)]
                link(v.tensor_scalar(acc, u[:, 0:SEQ], tap[0], pcol[:, R_CB + c:R_CB + c + 1], ALU.mult, ALU.add))
                for j in range(1, KCONV):
                    ins = v.scalar_tensor_tensor(out=acc, in0=u[:, j:j + SEQ], scalar=tap[j], in1=acc, op0=ALU.mult,
                                                 op1=ALU.add)
                    if j < KCONV - 1:
                        link(ins)
                    else:
                        ins.then_inc(conv_done, 1)

            def qk_low(n):
                v.wait_ge(qk_hi_done, n + 1)
                v.tensor_tensor(qk_lo[:, n % 4, :], cacc[:, n % 2, :], f32(qk_hi[:, n % 4, :]),
                                ALU.subtract).then_inc(qk_lo_done, 1)

            def pm_low(n):
                j = n % NT
                w = SEQ - P * j
                v.wait_ge(pm_hi_done, n + 1)
                part = (slice(None), n // NT % 2, slice(P_AT[j], P_AT[j] + w))
                v.tensor_tensor(pm_lo[part], pm[:, n % 2, 0:w], f32(pm_hi[part]), ALU.subtract).then_inc(pm_lo_done, 1)

            def weighted(h, j):
                n = h * NT + j
                w = SEQ - P * j
                v.wait_ge(st_ps, n + 1)
                v.wait_ge(decay_done, MH * NT)
                if n >= 2:
                    v.wait_ge(pm_lo_done, n - 1)
                v.scalar_tensor_tensor(out=pm[:, n % 2, 0:w], in0=bank[4 + n % 2][:, 0:w], scalar=K_SCALE,
                                       in1=decay[j][:, h, :], op0=ALU.mult, op1=ALU.mult).then_inc(pm_done, 1)

            def head_stats(n):
                h, t0 = n // 2, 2 * (n % 2)
                pv = bank[6 + n % 2][:, 0:2 * MV].rearrange("p (t c) -> p t c", t=2)
                v.wait_ge(mpv_ps, n + 1)
                v.wait_ge(emt_done, 1)
                if n:
                    v.wait_ge(ym_done, n)
                for q in range(2):
                    v.bn_stats(bns[:, q, :], pv[:, q, 0:MD])
                link(v.scalar_tensor_tensor(out=den[:], in0=pv[:, :, MD], scalar=-1.0, in1=emt[:, t0:t0 + 2, h],
                                            op0=ALU.mult, op1=ALU.max))
                link(v.tensor_tensor(den[:], pv[:, :, MD], den[:], ALU.max))
                for q in range(2):
                    v.bn_aggr(mva[:, q, :], bns[:, q, :])
                link(v.reciprocal(iden[:], den[:]))
                link(v.tensor_tensor(vs1[:], mva[:, :, 1], iden[:], ALU.mult))
                link(v.tensor_tensor(vs1[:], vs1[:], iden[:], ALU.mult))
                v.tensor_scalar(vs2[:], vs1[:], EPS, None, ALU.add).then_inc(var_done, 1)

            def head_norm(n):
                h, t0 = n // 2, 2 * (n % 2)
                pv = bank[6 + n % 2][:, 0:2 * MV].rearrange("p (t c) -> p t c", t=2)
                v.wait_ge(vr_done, n + 1)
                link(v.tensor_tensor(hsc[:], vr[:], iden[:], ALU.mult))
                for q in range(2):
                    ins = v.tensor_scalar(ym[:, t0 + q, h * MD:(h + 1) * MD], pv[:, q, 0:MD], mva[:, q, 0:1],
                                          hsc[:, q:q + 1], ALU.subtract, ALU.mult)
                ins.then_inc(ym_done, 1)

            for b in range(S_QK, S_AV):
                if b == S_QK:
                    cut(b + AHEAD - 2)
                    cut(b + AHEAD - 1)
                cut(b + AHEAD)
                if b == S_QK + 2:
                    v.wait_ge(gcol_ps, 1)
                    v.tensor_copy(aT[:], bank[6][:, 0:NT * 32].rearrange("p (t c) -> p t c", t=NT)[:, :, 0:16])\
                        .then_inc(aT_done, 1)
                if b - 1 in PE_ST:
                    pm_low(PE_ST[b - 1][0] * NT + PE_ST[b - 1][1])
                if b in PE_ST:
                    weighted(*PE_ST[b])
                if b % 2 == 1 and b < S_AZ:
                    conv((b - S_QK) // 2)
                if b % 2 == 0 and S_QK + 4 <= b < S_QK + 4 + 4 * MH:
                    qk_low((b - S_QK - 4) // 2)
                if b - 1 in PE_PV:
                    head_norm(2 * PE_PV[b - 1][0] + PE_PV[b - 1][1])
                if b in PE_PV:
                    head_stats(2 * PE_PV[b][0] + PE_PV[b][1])

            def rope(buf, t):
                xs = buf.rearrange("p (h d) -> p h d", h=AH)
                ra_, rb = (rtmp[:, q, :].rearrange("p (h d) -> p h d", h=AH) for q in range(2))

                def table(at, n):
                    return rope_sb[:, t, at:at + n].unsqueeze(1).to_broadcast([P, AH, n])

                v.tensor_tensor(ra_, xs[:, :, 0:ROT], table(0, ROT), ALU.mult)
                v.tensor_tensor(rb[:, :, 0:HALF], xs[:, :, HALF:ROT], table(ROT, HALF), ALU.mult)
                link(v.tensor_tensor(rb[:, :, HALF:ROT], xs[:, :, 0:HALF], table(ROT + HALF, HALF), ALU.mult))
                return v.tensor_tensor(xs[:, :, 0:ROT], ra_, rb, ALU.add)

            def kt_low(t):
                part = (slice(None), slice(None), slice(t * P, (t + 1) * P))
                v.wait_ge(kt_hi, t + 1)
                v.tensor_tensor(kT_lo[part], bank[6 + t % 2][:].rearrange("p (k c) -> p k c", k=4), f32(kT_hi[part]),
                                ALU.subtract).then_inc(kt_lo, 1)

            v.wait_ge(rope_in, 16)
            for b in range(S_AV, S_MZ):
                if b == S_AQ:
                    for t in range(NT):
                        part = v_hl[:, t * AH:(t + 1) * AH]
                        v.wait_ge(v_hi_done, t + 1)
                        v.scalar_tensor_tensor(out=part[:, :, DH:], in0=bank[t][:].rearrange("p (h d) -> p h d", h=AH),
                                               scalar=rx[:, t:t + 1], in1=f32(part[:, :, 0:DH]), op0=ALU.mult,
                                               op1=ALU.subtract).then_inc(v_lo_done, 1)
                cut(b + AHEAD)
                if S_AV <= b < S_AV + 4:
                    t = b - S_AV
                    v.wait_ge(k_raw, t + 1)
                    if t:
                        v.wait_ge(k_roped, t)
                    rope(keys[:, t, :], t).then_inc(k_roped, 1)
                if S_AV + 2 <= b < S_AV + 6:
                    kt_low(b - S_AV - 2)

            def q_rope(i):
                v.wait_ge(q_raw, i + 1)
                v.wait_ge(k_roped, NT)
                if i:
                    v.wait_ge(q_roped, i)
                rope(queries[:, i, :], NT - 1 - i).then_inc(q_roped, 1)

            def q_low(i):
                v.wait_ge(qt_hi, i + 1)
                v.tensor_tensor(qT[:, 2 * i + 1, :], bank[4 + i][:], f32(qT[:, 2 * i, :]),
                                ALU.subtract).then_inc(qt_lo, 1)

            def turn(n):
                k, t = turn_tile(n)
                part = (slice(None), slice(k, k + 4), slice(t * P, (t + 1) * P))
                v.wait_ge(turn_ps, n + 1)
                if n >= 2:
                    v.wait_ge(turn_lo, n - 1)
                scaled(turned[:, n % 2, :], bank[1][:], R_MG if TURNS[n][1] == "ym" else R_AG).then_inc(turn_scaled, 1)
                v.wait_ge(turn_hi, n + 1)
                v.tensor_tensor(xT_lo[part], turned[:, n % 2, :].rearrange("p (k c) -> p k c", k=4), f32(xT_hi[part]),
                                ALU.subtract).then_inc(turn_lo, 1)

            q_rope(0)
            q_rope(1)
            cut(S_MZ + AHEAD)
            q_low(0)
            q_rope(2)
            q_rope(3)
            cut(S_MZ + AHEAD + 1)
            q_low(1)
            for s in range(STEPS):
                if s < NU:
                    n = (unit(s)[0] + 1) * P
                    v.wait_ge(score_ps, s + 1)
                    if s >= 2:
                        v.wait_ge(prob_done, s - 1)
                    v.tensor_tensor_reduce(sm[:, s % 2, 0:n], bank[2 + s % 2][:, 0:n], causal[:, SEQ - n:], -Q_SCALE,
                                           BIG, ALU.add, ALU.min, mx[:, s:s + 1]).then_inc(masked, 1)
                u = s - LAG_T
                if 0 <= u < NU:
                    n = (unit(u)[0] + 1) * P
                    v.wait_ge(pt_hi, u + 1)
                    v.tensor_tensor(pT[:, 2 * (u % 2) + 1, 0:n], bank[4 + u % 2][:, 0:n],
                                    f32(pT[:, 2 * (u % 2), 0:n]), ALU.subtract).then_inc(pt_lo, 1)
                for kind, what in EVENTS.get(s, ()):
                    i = what[0]
                    if kind == "q_T":
                        q_low(i)
                    elif kind == "cut":
                        cut(i)
                    elif kind == "turn":
                        turn(i)
                    elif kind == "ya":
                        v.wait_ge(pv_ps, AH * (i + 1))
                        link(v.reciprocal(rrec[:, AH * i:AH * i + AH], rsum[:, AH * i:AH * i + AH]))
                        yv = ya[:, i % 2, :].rearrange("p (h d) -> p h d", h=AH)
                        for q in range(2):
                            link(v.tensor_reduce(yv[:, 4 * q:4 * q + 4, :],
                                                 bank[6 + q][:].rearrange("p (h a d) -> p h d a", h=4, a=2),
                                                 mybir.AxisListType.X, ALU.add))
                        v.tensor_tensor(yv, yv,
                                        rrec[:, AH * i:AH * i + AH].unsqueeze(2).to_broadcast([P, AH, DH]),
                                        ALU.mult).then_inc(ya_done, 1)
                    elif kind == "ya_ms":
                        v.wait_ge(ssa_done, i + 1)
                        v.tensor_scalar(msa[:, i:i + 1], ssa[:, i:i + 1], 1.0 / AW, EPS, ALU.mult, ALU.add)\
                            .then_inc(msa_done, 1)
                    elif kind == "ya_gate":
                        v.wait_ge(ra_done, i + 1)
                        v.scalar_tensor_tensor(out=ya[:, i % 2, :], in0=ya[:, i % 2, :], scalar=ra[:, i:i + 1],
                                               in1=silu_az[:, NT - 1 - i, :], op0=ALU.mult, op1=ALU.mult)\
                            .then_inc(ya_gated, 1)
                    elif kind == "y":
                        i, c = what
                        cols = slice(c * AW, (c + 1) * AW)
                        v.wait_ge(oa_ps, 2 * i + c + 1)
                        v.wait_ge(om_done, 2 * NT)
                        if i >= 2:
                            v.wait_ge(out_ready, 2 * (i - 1))
                        v.tensor_tensor(yb[:, i % 2, cols], bank[oa_bank(i, c)][:], y_mlstm[:, c, NT - 1 - i, :],
                                        ALU.add).then_inc(y_done, 1)
                    elif kind == "y_ms":
                        v.wait_ge(ssy_done, 2 * i + 2)
                        link(v.tensor_tensor(msy[:, i:i + 1], ssy[:, 2 * i:2 * i + 1], ssy[:, 2 * i + 1:2 * i + 2],
                                             ALU.add))
                        v.tensor_scalar(msy[:, i:i + 1], msy[:, i:i + 1], 1.0 / D, EPS, ALU.mult, ALU.add)\
                            .then_inc(msy_done, 1)
                    elif kind == "y_fin":
                        v.wait_ge(ry_done, i + 1)
                        v.wait_ge(post_in, 16)
                        for c in range(2):
                            cols = slice(c * AW, (c + 1) * AW)
                            v.scalar_tensor_tensor(out=yb[:, i % 2, cols], in0=yb[:, i % 2, cols],
                                                   scalar=ry[:, i:i + 1], in1=post[:, cols], op0=ALU.mult,
                                                   op1=ALU.mult).then_inc(y_normed, 1)

        @block.tensor
        def _(pe):
            def product(o, hi, lo, m_hi, m_lo, start, stop):
                pe.matmul(o, hi, m_hi, start=start, stop=False)
                pe.matmul(o, hi, m_lo, start=False, stop=False)
                return pe.matmul(o, lo, m_hi, start=False, stop=stop)

            def x_part(k, t):
                cols = slice(t * P, (t + 1) * P)
                return xT_hi[:, k, cols], xT_lo[:, k, cols]

            def w_part(n, cols=slice(0, AW)):
                return w_hi[:, n % RING, cols], w_lo[:, n % RING, cols]

            pe.wait_ge(ident_done, 1)
            pe.wait_ge(par_in, 16)
            pe.transpose(bank[3][:, 0:R_AG], prow[:], ident[0:R_AG, 0:R_AG]).then_inc(par_ps, 1)

            def turn_x(t):
                pe.wait_ge(x_in[t], 16)
                for n in (2 * t, 2 * t + 1):
                    j = n % 2
                    if n >= 4:
                        pe.wait_ge(xt_scaled, n - 3)
                    for k in range(4):
                        mm = pe.transpose(bank[4 + n % 4][:, k * P:(k + 1) * P],
                                          x_sb[:, t, (4 * j + k) * P:(4 * j + k + 1) * P], ident[:])
                    mm.then_inc(xt_ps, 1)

            def mv_part(t, ks):
                for k in ks:
                    pe.wait_ge(xt_lo, 2 * t + 1 + k // 4)
                    pe.wait_ge(w_lo_done, k + 1)
                    mm = product(bank[t][:], *x_part(k, t), *w_part(k), k == 0, k == NK - 1)
                    if t == NT - 1:
                        mm.then_inc(w_used, 1)
                    elif k == NK - 1:
                        mm.then_inc(proj_ps, 1)

            turn_x(0)
            mv_part(0, range(4))
            turn_x(1)
            mv_part(0, range(4, NK))
            mv_part(1, range(4))
            turn_x(2)
            mv_part(1, range(4, NK))
            mv_part(2, range(4))
            turn_x(3)
            mv_part(2, range(4, NK))
            pe.wait_ge(par2_in, 64)
            pe.wait_ge(par_done, 1)
            pe.transpose(bank[3][:, 0:R_END - R_AG], prow2[:], ident[0:R_END - R_AG, 0:R_END - R_AG]).then_inc(par2_ps, 1)
            pe.wait_ge(wg_done, 2)
            pe.wait_ge(xt_lo, 2 * NT)
            for k in range(NK):
                mm = product(bank[4][0:32, :], wg_hi[:, k, :], wg_lo[:, k, :], xT_hi[:, k, :], xT_lo[:, k, :],
                             k == 0, k == NK - 1)
            mm.then_inc(gate_ps, 1)
            pe.wait_ge(par_done, 2)
            mv_part(3, range(4))
            pe.wait_ge(bias32_done, 2)
            for q in range(2):
                mm = pe.transpose(bank[6][0:16, q * P:(q + 1) * P], bias32[:, 16 * q:16 * q + 16], ident[:])
            mm.then_inc(bias_ps, 1)
            pe.wait_ge(consts, 1)
            for t in range(NT):
                pe.wait_ge(diag_done, t + 1)
                mm = pe.matmul(bank[7][:, t * P:(t + 1) * P], ones[:], rbc[:, t * P:(t + 1) * P], start=True, stop=True)
            mm.then_inc(rbc_ps, 1)
            mv_part(3, range(4, NK))
            pe.wait_ge(gate_sb, 1)
            pe.matmul(bank[5][0:16, :], ident[0:32, 16:32], gate_rows, start=True, stop=True).then_inc(fgate_ps, 1)

            def by_slot(n, k, nk, part, free):
                pe.wait_ge(w_lo_done, n + 1)
                for t in range(NT):
                    if k == 0:
                        free(t)
                    mm = product(bank[t][:], *part(k, t), *w_part(n), k == 0, k == nk - 1)
                    if k == nk - 1 and t < NT - 1:
                        mm.then_inc(proj_ps, 1)
                mm.then_inc(w_used, 1)

            def gate_cols():
                pe.wait_ge(grows_done, 1)
                for t in range(NT):
                    pe.transpose(bank[6][:, 32 * t:32 * t + 16], rows[5][:, t * P:(t + 1) * P], ident[0:16, 0:16])
                    mm = pe.transpose(bank[6][:, 32 * t + 16:32 * t + 32], rows[0][:, t * P:(t + 1) * P],
                                      ident[0:16, 0:16])
                mm.then_inc(gcol_ps, 1)

            def head_scores(h, j):
                n, q, kk = h * NT + j, 2 * (h % 2), 2 * (h % 2) + 1
                pe.wait_ge(qk_lo_done, 2 * h + 2)
                if n < 2:
                    pe.wait_ge(grows_done, 1)
                else:
                    pe.wait_ge(pm_done, n - 1)
                src = slice(j * P, (j + 1) * P)
                product(bank[4 + n % 2][:, 0:SEQ - j * P], qk_hi[:, kk, src], qk_lo[:, kk, src],
                        qk_hi[:, q, j * P:], qk_lo[:, q, j * P:], True, True).then_inc(st_ps, 1)

            def head_values(h, half):
                pe.wait_ge(mv_lo_done, NT)
                pe.wait_ge(pm_lo_done, NT * h + 2 * half + 2)
                n = 2 * h + half
                if n == 0:
                    pe.wait_ge(emt_done, 1)
                elif n == 1:
                    pe.wait_ge(rbc_done, 1)
                else:
                    pe.wait_ge(ym_done, n - 1)
                for q in range(2):
                    t = 2 * half + q
                    for j in range(t + 1):
                        w = slice(P_AT[j] + (t - j) * P, P_AT[j] + (t - j + 1) * P)
                        mm = product(bank[6 + half][:, MV * q:MV * (q + 1)], pm_hi[:, h % 2, w], pm_lo[:, h % 2, w],
                                     mv_hi[:, j, h, :], mv_lo[:, j, h, :], j == 0, j == t)
                mm.then_inc(mpv_ps, 1)

            def mlstm(b):
                if b in PE_ST:
                    head_scores(*PE_ST[b])
                if b in PE_PV:
                    head_values(*PE_PV[b])

            for b in range(S_QK, S_AZ):
                p = 4 + (b - S_QK) // 2
                pe.wait_ge(w_lo_done, b + 1)
                if b % 2 == 0:
                    if p < 8:
                        pe.wait_ge(mv_lo_done, p - 3)
                    else:
                        pe.wait_ge(u_done, p - 7)
                for kk in range(4):
                    k = 4 * (b % 2) + kk
                    mm = product(bank[p % 4][:], *w_part(b, slice(kk * P, (kk + 1) * P)), xT_hi[:, k, :],
                                 xT_lo[:, k, :], k == 0, k == NK - 1)
                mm.then_inc(w_used, 1)
                if b == S_QK + 2:
                    gate_cols()
                mlstm(b)
            for b in range(S_AZ, S_AV):
                if b < S_AK:
                    by_slot(b, b % NK, NK, x_part, lambda t: pe.wait_ge(u_done, 5 + t))
                else:
                    by_slot(b, b % NK, NK, x_part, lambda t: pe.wait_ge(az_done, 1 + t))
                mlstm(b)
            for b in range(S_AV, S_AQ):
                by_slot(b, b % NK, NK, x_part, lambda t: pe.wait_ge(k_raw, t + 1))
                t = b - S_AV - 2
                if 0 <= t < NT:
                    pe.wait_ge(k_roped, t + 1)
                    if t < 2:
                        pe.wait_ge(ym_done, 2 * MH)
                    else:
                        pe.wait_ge(kt_lo, t - 1)
                    for k in range(4):
                        mm = pe.transpose(bank[6 + t % 2][:, k * P:(k + 1) * P], keys[:, t, k * P:(k + 1) * P],
                                          ident[:])
                    mm.then_inc(kt_ps, 1)
            for b in range(S_AQ, S_MZ):
                by_slot(b, b % NK, NK, lambda k, i: x_part(k, NT - 1 - i), lambda i: pe.wait_ge(v_lo_done, i + 1))

            def z_part(n, k):
                t, slot = n % NT, S_MZ + NK * (n // NT) + k
                if t == 0:
                    pe.wait_ge(w_lo_done, slot + 1)
                if k == 0:
                    if n == 0:
                        pe.wait_ge(q_raw, 1)
                    else:
                        pe.wait_ge(z_done, n)
                mm = product(bank[0][:], *x_part(k, t), *w_part(slot), k == 0, k == NK - 1)
                if t == NT - 1:
                    mm.then_inc(w_used, 1)
                elif k == NK - 1:
                    mm.then_inc(proj_ps, 1)

            def om_part(n, k):
                t, slot = n // 2, S_OM + 4 * (n % 2) + k
                pe.wait_ge(turn_lo, t + 1)
                pe.wait_ge(w_lo_done, slot + 1)
                if k == 0:
                    if n == 0:
                        pe.wait_ge(z_done, 2 * NT)
                    else:
                        pe.wait_ge(om_done, n)
                mm = product(bank[0][:], *x_part(k, t), *w_part(slot), k == 0, k == 3)
                if t == NT - 1:
                    mm.then_inc(w_used, 1)
                elif k == 3:
                    mm.then_inc(proj_ps, 1)

            def turn_q(i):
                pe.wait_ge(q_roped, i + 1)
                pe.wait_ge(kt_lo, NT)
                for k in range(4):
                    mm = pe.transpose(bank[4 + i][:, k * P:(k + 1) * P], queries[:, i, k * P:(k + 1) * P], ident[:])
                mm.then_inc(qt_ps, 1)

            def turn(n):
                step, kind, i = TURNS[n]
                pe.wait_ge(ym_gated if kind == "ym" else ya_gated, i + 1)
                if n:
                    pe.wait_ge(turn_scaled, n)
                else:
                    pe.wait_ge(q_raw, 2)
                src = ym[:, i] if kind == "ym" else ya[:, i % 2]
                for k in range(4):
                    mm = pe.transpose(bank[1][:, k * P:(k + 1) * P], src[:, k * P:(k + 1) * P], ident[:])
                mm.then_inc(turn_ps, 1)

            def oa(i, k):
                c, kk = k // 4, k % 4
                pe.wait_ge(turn_lo, NT + i + 1)
                pe.wait_ge(w_lo_done, S_OA + k + 1)
                if kk == 0:
                    pe.wait_ge(om_done, 2 * NT)
                    if oa_bank(i, c) == 3:
                        pe.wait_ge(masked, NU)
                    if (i, c) != (2, 1):
                        if 2 * i + c:
                            pe.wait_ge(y_done, 2 * i + c - (i == NT - 1))
                mm = product(bank[oa_bank(i, c)][:], *x_part(4 + kk, NT - 1 - i), *w_part(S_OA + k), kk == 0, kk == 3)
                if kk == 3:
                    mm.then_inc(oa_ps, 1)

            for k in range(4):
                z_part(0, k)
            turn_q(0)
            for k in range(4, NK):
                z_part(0, k)
            turn_q(1)
            for s in range(STEPS):
                events = EVENTS.get(s, ())
                if s < NU:
                    t, h = unit(s)
                    i, n, half = s // AH, (t + 1) * P, slice(DH * (h % 2), DH * (h % 2 + 1))
                    pe.wait_ge(qt_lo, i + 1)
                    if s < 2:
                        pe.wait_ge(q_raw, NT)
                    else:
                        pe.wait_ge(masked, s - 1)
                    cols = slice(h // 2 * P, (h // 2 + 1) * P)
                    product(bank[2 + s % 2][:, 0:n], qT[half, 2 * i, cols], qT[half, 2 * i + 1, cols],
                            kT_hi[half, h // 2, 0:n], kT_lo[half, h // 2, 0:n], True, True).then_inc(score_ps, 1)
                u = s - LAG_T
                if 0 <= u < NU:
                    t, h = unit(u)
                    pe.wait_ge(prob_done, u + 1)
                    if u >= 2:
                        pe.wait_ge(pt_lo, u - 1)
                    else:
                        pe.wait_ge(qt_lo, 2)
                    for j in range(t + 1):
                        mm = pe.transpose(bank[4 + u % 2][:, j * P:(j + 1) * P], prob[:, u % 2, j * P:(j + 1) * P],
                                          ident[:])
                    mm.then_inc(pt_ps, 1)
                for kind, what in events:
                    if kind == "z_part":
                        z_part(*what)
                    elif kind == "om":
                        om_part(*what)
                    elif kind == "oa":
                        oa(*what)
                u = s - LAG_PV
                if 0 <= u < NU:
                    t, h = unit(u)
                    pe.wait_ge(pt_lo, u + 1)
                    pe.wait_ge(v_lo_done, NT)
                    if u == 0:
                        pe.wait_ge(qt_lo, NT)
                    if h == 0 and u:
                        pe.wait_ge(ya_done, u // AH)
                    for j in range(t + 1):
                        cols = slice(j * P, (j + 1) * P)
                        for q in range(2):
                            mm = pe.matmul(bank[6 + h // 4][:, h % 4 * P:(h % 4 + 1) * P], pT[:, 2 * (u % 2) + q, cols],
                                           v_hl[:, j * AH + h, :], start=j + q == 0, stop=j == t and q == 1)
                    mm.then_inc(pv_ps, 1)
                for kind, what in events:
                    if kind == "q_T":
                        turn_q(*what)
                    elif kind == "turn":
                        turn(*what)


_INS = ["x", "pre_norm_g", "w_in", "mlstm_i_bias", "mlstm_f_bias", "conv_w", "conv_b", "attn_out_g", "mlstm_out_g",
        "w_out", "post_norm_g"]


def rope_table():
    inv = np.power(np.float32(500000.0), -np.arange(HALF, dtype=np.float32) * np.float32(2.0) / np.float32(ROT))
    ang = np.arange(SEQ, dtype=np.float32)[:, None] * inv.astype(np.float32)[None, :]
    cos, sin = np.cos(ang), np.sin(ang)
    return np.concatenate([cos, cos, -sin, sin], axis=1).astype(np.float32)


def kernel(**inputs):
    import concourse.bacc as _bacc
    from concourse.bass_utils import run_bass_kernel_spmd as _run

    nc = _bacc.Bacc("TRN2", target_bir_lowering=False, num_devices=1)
    arrays = {f"in_{n}": np.ascontiguousarray(inputs[n]) for n in _INS}
    arrays["in_rope"] = rope_table()
    args = [nc.dram_tensor(n, a.shape, mybir.dt.from_np(a.dtype), kind="ExternalInput").ap() for n, a in arrays.items()]
    args.append(nc.dram_tensor("out_y", (1, SEQ, D), F32, kind="ExternalOutput").ap())
    build(nc, *args)
    r = _run(nc, [arrays], core_ids=[0])
    return r.results[0]["out_y"]
```

```python
from contextlib import ExitStack

import numpy as np

import concourse.bass as bass
from concourse import mybir

F32 = mybir.dt.float32
F32R = mybir.dt.float32r
ALU = mybir.AluOpType
ACT = mybir.ActivationFunctionType

P = 128
SEQ = 512
D = 1024
NT = SEQ // P
NK = D // P
AW = 512
AH, DH = 8, 64
MH, MD = 4, 128
MV = MD + 2
ROT = DH // 4
HALF = ROT // 2
KCONV = 4
EPS = 1e-6
FAR = -1e30
BIG = 3e38
Q_SCALE = DH ** -0.5
K_SCALE = MD ** -0.5

AQ, AK, AV, AZ, MQ, MK, MVC, MO, MZ, MG = (AW * i for i in range(10))

SLOTS = [("in", "cols", k, MVC) for k in range(NK)]
for _h in range(MH):
    for _c in (MQ, MK):
        SLOTS += [("in", "heads", k, _c + _h * MD) for k in (0, 4)]
for _c in (AZ, AK, AV, AQ, MZ, MO):
    SLOTS += [("in", "cols", k, _c) for k in range(NK)]
for _r in (4, 0):
    SLOTS += [("out", "cols", _r + k, c * AW) for c in range(2) for k in range(4)]
S_MV, S_QK, S_AZ, S_AK, S_AV, S_AQ, S_MZ, S_MO, S_OM, S_OA = 0, 8, 24, 32, 40, 48, 56, 64, 72, 80
NSLOT = len(SLOTS)
RAW = 4
RING = 8
AHEAD = 6
X_AFTER = {3: 1, 5: 2, 7: 3}
FIRST_ON_POOL = 22


def on_pool(n):
    return n >= FIRST_ON_POOL and n % 2 == 0


R_PRE, R_AG, R_MG, R_CB, R_CW, R_END = 0, 8, 12, 16, 24, 56

F_E, F_U, F_ACC, F_PM, F_END = 0, 5120, 6152, 7176, 8200
F_X = 0
F_SC, F_SM, F_P, F_YA, F_XR, F_Y = 0, 1024, 2048, 3072, 4096, 6144
R_QK, R_MV, R_P = 0, 4096, 8256
R_KT, R_V, R_QT, R_PT, R_SIZE = 0, 4096, 8192, 12288, 14336
E_AT = [0, 2048, 3584, 4608]
P_AT = [0, 512, 896, 1152]

NU = NT * AH


U_AZ, U_AK, U_AV, U_AQ, U_MZ, U_MO, U_OM = 12, 16, 20, 24, 28, 32, 36
UNIT_SLOT = {3: S_QK, 15: S_AK, 19: S_AV, 23: S_AQ, 27: S_MZ, 31: S_MO, 35: S_OM, 42: S_OM + 4, 43: S_OA}
UNIT_SLOT.update({4 + n: S_QK + 2 * n + 2 for n in range(2 * MH)})

HEAD_AT = (S_QK + 10, S_QK + 14, S_QK + 18, S_QK + 23)
PE_ST = {HEAD_AT[h] + j: (h, j) for h in range(MH) for j in range(NT)}
PE_PV = {HEAD_AT[h] + NT + q: (h, q) for h in range(MH) for q in range(2)}

LAG_T, LAG_PV = 2, 3
EVENTS = {}
PRIORITY = ("q_T", "z_part", "om", "oa", "ya_half", "ya", "ya_sq", "ya_ms", "ya_gate", "z", "z_gate", "om_out", "y_ms",
            "y_fin", "y", "cut", "turn")


def _event(step, kind, *what):
    EVENTS.setdefault(step, []).append((kind, what))


_event(0, "q_T", 2)
_event(1, "q_T", 3)
Z_RATE = (NK, 2, 3, 3, 3, 3, 3, 2)
Z_START, Z_END = [0], [0]
CUT_Z = (0, 0, 0, 1, 2, 2, 3, 3)
CUT_OM = (0, 0, 0, 1, 2, 2, 3, 3)
for _n in range(1, 2 * NT):
    Z_START.append(Z_END[-1] + (_n > 1))
    Z_END.append(Z_START[-1] + (NK - 1) // Z_RATE[_n])
    for _k in range(NK):
        _event(Z_START[_n] + _k // Z_RATE[_n], "z_part", _n, _k)
        if _n in (NT - 1, 2 * NT - 1):
            _event(Z_START[_n] + CUT_Z[_k], "cut", (S_MO if _n == NT - 1 else S_OM) + _k)
    _event(Z_END[_n], "z", _n)
    _event(Z_END[_n] + (_n == 2 * NT - 1), "z_gate", _n)
OM_START = Z_END[-1] + 1
for _n in range(2 * NT):
    for _k in range(4):
        _event(OM_START + _n, "om", _n, _k)
    _event(OM_START + _n, "om_out", _n)
for _k in range(8):
    _event(OM_START + 2 * NT - 2 + CUT_OM[_k], "cut", S_OA + _k)
TURNS = sorted([(Z_END[NT + _t] + 3, "ym", _t) for _t in range(NT)] + [
    (OM_START, "ya", 0), (OM_START + 3, "ya", 1), (AH * 3 + LAG_PV + 4, "ya", 2), (AH * 4 + LAG_PV + 2, "ya", 3)])
TURN_OF = {_turn[1:]: _n for _n, _turn in enumerate(TURNS)}
for _n, _turn in enumerate(TURNS):
    _event(_turn[0], "turn", _n)
OA_STEPS = ((32,) * 4 + (34,) * 4, (35,) * 4 + (36,) * 4, (37,) * 4 + (38,) * 4,
            (39,) * 4 + (40,) * 4)
for _i, _steps in enumerate(OA_STEPS):
    _late = (2, 2, 1, 0)[_i]
    _s = AH * _i + AH - 1 + LAG_PV
    _event(_s - 3, "ya_half", _i)
    _event(_s + min(_late, 1), "ya", _i)
    _event(_s + _late, "ya_sq", _i)
    _event(_s + 1 + _late, "ya_ms", _i)
    _event(_s + 2 + _late, "ya_gate", _i)
    for _k in range(8):
        _event(_steps[_k], "oa", _i, _k)
        if _k % 4 == 3:
            _event(_steps[_k], "y", _i, _k // 4)
    _event(_steps[-1] + 1, "y_ms", _i)
    _event(_steps[-1] + 2, "y_fin", _i)
STEPS = max(EVENTS) + 1
for _s in EVENTS:
    EVENTS[_s].sort(key=lambda e: PRIORITY.index(e[0]))


def _sharers():
    where, last, now = {("z", 0): (0, ("q", 0))}, {0: ("z", 0), 1: ("q", 1)}, 0
    starts = {"z_part": "z", "om": "om", "oa": "oa"}
    for s in range(STEPS):
        turned = False
        events = EVENTS.get(s, ())
        for kind, what in [e for e in events if e[0] == "turn"] + [e for e in events if e[0] in starts]:
            if kind == "turn":
                user, at, turned = (kind, what[0]), 1 - now, True
            elif what[-1] % (NK if kind == "z_part" else 4) == 0:
                user = (starts[kind], 2 * what[0] + what[1] // 4 if kind == "oa" else what[0])
                now = at = now if turned else 1 - now
                turned = False
            else:
                continue
            where[user] = (at, last[at])
            last[at] = user
    return where


SHARED = _sharers()


def unit(u):
    return NT - 1 - u // AH, u % AH


def build(nc, x, pre_g, w_in, i_bias, f_bias, conv_w, conv_b, attn_g, mlstm_g, w_out, post_g, rope, out):
    with ExitStack() as ctx:
        def sb(name, shape, dt=F32):
            return ctx.enter_context(nc.sbuf_tensor(name, shape, dt))

        def sem(name):
            return ctx.enter_context(nc.semaphore(name))

        xT_hi = sb("xT_hi", [P, NK, SEQ], F32R)
        xT_lo = sb("xT_lo", [P, NK, SEQ], F32R)
        w_raw = sb("w_raw", [P, RAW, AW])
        w_hi = sb("w_hi", [P, RING, AW], F32R)
        w_lo = sb("w_lo", [P, RING, AW], F32R)
        farena = sb("farena", [P, F_END])
        rarena = sb("rarena", [P, R_SIZE], F32R)
        silu_az = sb("silu_az", [P, NT, AW])
        gy = sb("gy", [P, 2, NT, AW])
        post = sb("post", [P, D])
        tmp = sb("tmp", [P, 2, AW])
        rbc = sb("rbc", [P, SEQ])
        junk = sb("junk", [P, D], mybir.dt.bfloat16)
        ident = sb("ident", [P, P])
        ones = sb("ones", [P, P])
        causal = sb("causal", [P, SEQ])
        causalT = sb("causalT", [P, P])
        rope_sb = sb("rope_sb", [P, NT, 2 * ROT])
        rtmp = sb("rtmp", [P, 2, AH * ROT])
        prow = sb("prow", [R_AG, P])
        prow2 = sb("prow2", [R_END - R_AG, P])
        pcol = sb("pcol", [P, R_END])
        wg_raw = sb("wg_raw", [P, NK, 8])
        wg_hi = sb("wg_hi", [P, NK, 32], F32R)
        wg_lo = sb("wg_lo", [P, NK, 32], F32R)
        bias8 = sb("bias8", [P, 8])
        bias32 = sb("bias32", [P, 32])
        bcol = sb("bcol", [16, 2])
        aT = sb("aT", [P, NT, 16])
        emt = sb("emt", [P, NT, MH])
        ssx = sb("ssx", [P, NT])
        msx = sb("msx", [P, NT])
        rx = sb("rx", [P, NT])
        mhalf = sb("mhalf", [P, NT])
        bns = sb("bns", [P, 2, 6])
        mva = sb("mva", [P, 2, 2])
        den = sb("den", [P, 2])
        iden = sb("iden", [P, 2])
        vs1 = sb("vs1", [P, 2])
        vs2 = sb("vs2", [P, 2])
        vr = sb("vr", [P, 2])
        hsc = sb("hsc", [P, 2])
        mx = sb("mx", [P, NU])
        rsum = sb("rsum", [P, NU])
        rrec = sb("rrec", [P, NU])
        ssa = sb("ssa", [P, NT])
        msa = sb("msa", [P, NT])
        ra = sb("ra", [P, NT])
        ssy = sb("ssy", [P, 2 * NT])
        msy = sb("msy", [P, NT])
        ry = sb("ry", [P, NT])

        bank = [ctx.enter_context(nc.psum_tensor(f"bank{i}", [P, 512], F32)) for i in range(8)]

        def f_part(at, *shape):
            n = int(np.prod(shape))
            v = farena[:, at:at + n]
            return v if len(shape) == 1 else v.rearrange("p (a b) -> p a b", a=shape[0]) if len(shape) == 2 \
                else v.rearrange("p (a b c) -> p a b c", a=shape[0], b=shape[1])

        def r_part(at, *shape):
            n = int(np.prod(shape))
            v = rarena[:, at:at + n]
            return v if len(shape) == 1 else v.rearrange("p (a b) -> p a b", a=shape[0]) if len(shape) == 2 \
                else v.rearrange("p (a b c) -> p a b c", a=shape[0], b=shape[1])

        x_sb = f_part(F_X, NT, D)
        decay = [f_part(F_E + E_AT[j], MH, SEQ - P * j) for j in range(NT)]
        upad = f_part(F_U, 2, 516)
        cacc = f_part(F_ACC, 2, SEQ)
        pm = f_part(F_PM, 2, SEQ)
        qk_hi = r_part(R_QK, 4, SEQ)
        qk_lo = r_part(R_QK + 4 * SEQ, 4, SEQ)
        mv_hi = r_part(R_MV, NT, MH, MV)
        mv_lo = r_part(R_MV + NT * MH * MV, NT, MH, MV)
        pm_hi = r_part(R_P, 2, 1280)
        pm_lo = r_part(R_P + 2560, 2, 1280)
        gate, ym = gy[:, 0], gy[:, 1]
        rows = [gy[0:16, i // 4, i % 4, :] for i in range(8)]
        gate_rows = gy[0:32, 1, 2, :]
        y_mlstm = gy
        turned = f_part(F_SC, 2, AW)
        queries = f_part(F_Y, NT, AW)
        keys = f_part(F_XR, NT, AW)
        sm = f_part(F_SM, 2, SEQ)
        prob = f_part(F_P, 2, SEQ)
        ya = f_part(F_YA, 2, AW)
        xr = f_part(F_XR, 2, D)
        yb = f_part(F_Y, 2, D)
        yg = (tmp[:].rearrange("p a c -> p (a c)"), f_part(F_SM, D))
        kT_hi = r_part(R_KT, 4, SEQ)
        kT_lo = r_part(R_KT + 4 * SEQ, 4, SEQ)
        v_hl = r_part(R_V, NT * AH, 2 * DH)
        qT = r_part(R_QT, 2 * NT, AW)
        pT = r_part(R_PT, 4, SEQ)
        g_dram = nc.dram_tensor("g_rows", (16, SEQ), F32, kind="Internal").ap()

        x_in = [sem(f"x_in{t}") for t in range(NT)]
        par_in = sem("par_in")
        wg_in = sem("wg_in")
        bias_in = sem("bias_in")
        rope_in = sem("rope_in")
        post_in = sem("post_in")
        raw_in = [sem(f"raw_in{r}") for r in range(RAW)]
        w_hi_done = sem("w_hi_done")
        w_lo_done = [sem(f"w_lo_done{q}") for q in range(2)]
        w_used = sem("w_used")
        consts = sem("consts")
        cleared = sem("cleared")
        par_ps = sem("par_ps")
        par_done = sem("par_done")
        xt_ps = sem("xt_ps")
        xt_scaled = sem("xt_scaled")
        xt_hi = sem("xt_hi")
        xt_lo = sem("xt_lo")
        ssx_done = sem("ssx_done")
        msx_done = sem("msx_done")
        rx_done = sem("rx_done")
        diag_done = sem("diag_done")
        rbc_ps = sem("rbc_ps")
        rbc_done = sem("rbc_done")
        wg_done = sem("wg_done")
        gate_ps = sem("gate_ps")
        gate_sb = sem("gate_sb")
        bias32_done = sem("bias32_done")
        bias_ps = sem("bias_ps")
        bcol_done = sem("bcol_done")
        fgate_ps = sem("fgate_ps")
        igate_done = sem("igate_done")
        par2_in = sem("par2_in")
        par2_ps = sem("par2_ps")
        ident_done = sem("ident_done")
        absf_done = sem("absf_done")
        expf_done = sem("expf_done")
        onep_done = sem("onep_done")
        ln_done = sem("ln_done")
        grows_done = sem("grows_done")
        gcol_ps = sem("gcol_ps")
        aT_done = sem("aT_done")
        emt_done = sem("emt_done")
        g_out = sem("g_out")
        g_back = sem("g_back")
        g_masked = sem("g_masked")
        decay_done = sem("decay_done")
        proj_ps = sem("proj_ps")
        mv_hi_done = sem("mv_hi_done")
        mv_lo_done = sem("mv_lo_done")
        mv_ones = sem("mv_ones")
        u_done = sem("u_done")
        conv_done = sem("conv_done")
        silu_done = sem("silu_done")
        qk_hi_done = sem("qk_hi_done")
        qk_lo_done = sem("qk_lo_done")
        st_ps = sem("st_ps")
        pm_done = sem("pm_done")
        pm_hi_done = sem("pm_hi_done")
        pm_lo_done = sem("pm_lo_done")
        mpv_ps = sem("mpv_ps")
        var_done = sem("var_done")
        vr_done = sem("vr_done")
        ym_done = sem("ym_done")
        az_done = sem("az_done")
        z_done = sem("z_done")
        gate_mul = sem("gate_mul")
        turn_ps = sem("turn_ps")
        turn_scaled = sem("turn_scaled")
        turn_hi = sem("turn_hi")
        turn_lo = sem("turn_lo")
        ym_gated = sem("ym_gated")
        k_raw = sem("k_raw")
        k_roped = sem("k_roped")
        kt_ps = sem("kt_ps")
        kt_hi = sem("kt_hi")
        kt_lo = sem("kt_lo")
        v_hi_done = sem("v_hi_done")
        v_lo_done = sem("v_lo_done")
        q_raw = sem("q_raw")
        q_roped = sem("q_roped")
        qt_ps = sem("qt_ps")
        qt_hi = sem("qt_hi")
        qt_lo = sem("qt_lo")
        score_ps = sem("score_ps")
        masked = sem("masked")
        prob_done = sem("prob_done")
        pt_ps = sem("pt_ps")
        pt_hi = sem("pt_hi")
        pt_lo = sem("pt_lo")
        pv_ps = sem("pv_ps")
        ya_summed = sem("ya_summed")
        ya_done = sem("ya_done")
        ssa_done = sem("ssa_done")
        msa_done = sem("msa_done")
        ra_done = sem("ra_done")
        ya_gated = sem("ya_gated")
        om_done = sem("om_done")
        oa_ps = sem("oa_ps")
        y_done = sem("y_done")
        ssy_done = sem("ssy_done")
        msy_done = sem("msy_done")
        ry_done = sem("ry_done")
        y_gained = sem("y_gained")
        xr_in = [sem(f"xr_in{t}") for t in range(NT)]
        out_ready = sem("out_ready")
        out_done = [sem(f"out_done{t}") for t in range(NT)]
        vchain = sem("vchain")

        block = ctx.enter_context(nc.Block())

        def projected(eng, p):
            if p in UNIT_SLOT:
                eng.wait_ge(w_used, UNIT_SLOT[p])
            else:
                eng.wait_ge(proj_ps, sum(1 for q in range(p + 1) if q not in UNIT_SLOT))

        def low_done(eng, n):
            eng.wait_ge(w_lo_done[n % 2], n // 2 + 1)

        def shared(kind, n):
            return bank[SHARED[kind, n][0]]

        def turn_tile(n):
            _, kind, i = TURNS[n]
            return (0, i) if kind == "ym" else (4, NT - 1 - i)

        def store(sp, i):
            t = NT - 1 - i
            for c in range(2):
                cols = slice(c * AW, (c + 1) * AW)
                sp.wait_ge(out_ready, 2 * i + c + 1)
                sp.dma_start(out[0, t * P:(t + 1) * P, cols], xr[:, i % 2, cols]).then_inc(out_done[i], 16)

        @block.sync
        def _(sp):
            x2 = x.rearrange("b s d -> (b s) d")

            def load_x(t):
                sp.dma_start(x_sb[:, t, :], x2[t * P:(t + 1) * P, :]).then_inc(x_in[t], 16)

            for j in range(2):
                sp.dma_start(x_sb[:, 0, j * AW:(j + 1) * AW], x2[0:P, j * AW:(j + 1) * AW]).then_inc(x_in[0], 16)
                if j == 0:
                    sp.dma_start(prow[:], pre_g.rearrange("o (c p) -> (o c) p", p=P)).then_inc(par_in, 16)
            for n, (mat, kind, k, c) in enumerate(SLOTS):
                if n >= RAW:
                    low_done(sp, n - RAW)
                w = w_in if mat == "in" else w_out
                if kind == "cols":
                    src = w[0, k * P:(k + 1) * P, c:c + AW]
                    dst = w_raw[:, n % RAW, :]
                else:
                    src = w[0, k * P:(k + 4) * P, c:c + MD].rearrange("(k p) c -> p k c", p=P)
                    dst = w_raw[:, n % RAW, :].rearrange("p (k c) -> p k c", k=4)
                sp.dma_start(dst, src).then_inc(raw_in[n % RAW], 16)
                if n in X_AFTER:
                    load_x(X_AFTER[n])
                if n == NK - 1:
                    sp.dma_start(wg_raw[:], w_in[0, :, MG:MG + 8].rearrange("(k p) c -> p k c", p=P)).then_inc(wg_in, 16)
                if n == S_QK + 4:
                    sp.dma_start(rope_sb[:], rope.rearrange("(t p) c -> p t c", p=P)).then_inc(rope_in, 16)
                    sp.dma_start(post[:], post_g.to_broadcast([P, D])).then_inc(post_in, 16)
            for i in range(NT):
                t = NT - 1 - i
                if i == 0:
                    sp.wait_ge(pm_lo_done, MH * NT)
                    sp.wait_ge(mpv_ps, 2 * MH)
                    sp.wait_ge(kt_ps, NT)
                if i >= 2:
                    sp.wait_ge(out_done[i - 2], 32)
                sp.dma_start(xr[:, i % 2, :], x2[t * P:(t + 1) * P, :]).then_inc(xr_in[i], 16)
                if i >= 1:
                    store(sp, i - 1)
            store(sp, NT - 1)
            for i in range(NT):
                sp.wait_ge(out_done[i], 32)

        @block.gpsimd
        def _(g):
            def rows_of(p):
                return p.rearrange("o (c p) -> (o c) p", p=P)

            g.memset(ident[:], 0.0).then_inc(cleared, 1)
            g.wait_ge(cleared, 1)
            g.affine_select(out=ident[:], in_=ident[:], compare_op=ALU.not_equal, fill=1.0, base=0,
                            pattern=[[-1, P]], channel_multiplier=1).then_inc(ident_done, 1)
            g.dma_start(prow2[0:4, :], rows_of(attn_g)).then_inc(par2_in, 16)
            g.dma_start(prow2[4:8, :], rows_of(mlstm_g)).then_inc(par2_in, 16)
            g.dma_start(prow2[8:16, :], rows_of(conv_b)).then_inc(par2_in, 16)
            g.dma_start(prow2[16:48, :], conv_w.rearrange("o j (c p) -> (o j c) p", p=P)).then_inc(par2_in, 16)
            g.dma_start(bias8[:, 0:MH], i_bias.to_broadcast([P, MH])).then_inc(bias_in, 16)
            g.dma_start(bias8[:, MH:2 * MH], f_bias.to_broadcast([P, MH])).then_inc(bias_in, 16)
            g.memset(causal[:], 0.0).then_inc(cleared, 1)
            g.memset(causalT[:], 0.0).then_inc(cleared, 1)
            g.memset(rows[7], 1.0).then_inc(cleared, 1)
            g.memset(upad[:, :, 0:KCONV - 1], 0.0).then_inc(cleared, 1)
            g.wait_ge(cleared, 5)
            g.memset(ones[:], 1.0).then_inc(consts, 1)
            g.memset(mhalf[:], -0.5).then_inc(consts, 1)
            g.affine_select(out=causal[:, SEQ - P:], in_=causal[:, SEQ - P:], compare_op=ALU.is_ge, fill=FAR, base=0,
                            pattern=[[-1, P]], channel_multiplier=1).then_inc(consts, 1)
            g.affine_select(out=causalT[:], in_=causalT[:], compare_op=ALU.is_ge, fill=FAR, base=0,
                            pattern=[[1, P]], channel_multiplier=-1).then_inc(consts, 1)
            g.affine_select(out=rows[7].rearrange("p (t c) -> p t c", t=NT),
                            in_=rows[7].rearrange("p (t c) -> p t c", t=NT), compare_op=ALU.is_ge, fill=0.0,
                            base=3, pattern=[[4, NT], [0, P]], channel_multiplier=-1).then_inc(consts, 1)
            g.memset(mv_hi[:, :, :, MD:MV].bitcast(F32), 1.0).then_inc(mv_ones, 1)
            g.memset(mv_lo[:, :, :, MD:MV].bitcast(F32), 0.0).then_inc(mv_ones, 1)

            def rsqrt(dst, src):
                return g.tensor_tensor(dst, src, mhalf[:, 0:src.shape[1]], ALU.pow)

            g.wait_ge(consts, 2)
            g.wait_ge(msx_done, 1)
            rsqrt(rx[:], msx[:]).then_inc(rx_done, 1)
            g.wait_ge(grows_done, 1)
            g.dma_start(g_dram, rows[4]).then_inc(g_out, 16)
            g.wait_ge(g_out, 16)
            for j in range(NT):
                g.dma_start(decay[j], g_dram[4 * j:4 * j + 4, j * P:].rearrange("(o h) c -> o h c", o=1)
                            .to_broadcast([P, MH, SEQ - j * P])).then_inc(g_back, 16)
            g.wait_ge(g_back, 16 * NT)
            for j in range(NT):
                v = decay[j][:, :, 0:P]
                g.tensor_tensor(v, v, causalT[:].unsqueeze(1).to_broadcast([P, MH, P]), ALU.add).then_inc(g_masked, 1)

            def pm_low(n):
                h, j = n // NT, n % NT
                w = SEQ - P * j
                g.wait_ge(pm_hi_done, n + 1)
                part = (slice(None), h % 2, slice(P_AT[j], P_AT[j] + w))
                g.tensor_tensor(pm_lo[part], pm[:, n % 2, 0:w], pm_hi[part].bitcast(F32), ALU.subtract)\
                    .then_inc(pm_lo_done, 1)

            def cut(n):
                if not on_pool(n):
                    return
                g.wait_ge(w_hi_done, n + 1)
                if n == FIRST_ON_POOL:
                    low_done(g, n - 2)
                g.tensor_tensor(w_lo[:, n % RING, :], w_raw[:, n % RAW, :], w_hi[:, n % RING, :].bitcast(F32),
                                ALU.subtract).then_inc(w_lo_done[n % 2], 1)

            for b in range(S_QK, S_MZ):
                if b - 1 in PE_ST:
                    pm_low(PE_ST[b - 1][0] * NT + PE_ST[b - 1][1])
                if b in PE_PV:
                    g.wait_ge(var_done, 2 * PE_PV[b][0] + PE_PV[b][1] + 1)
                    rsqrt(vr[:], vs2[:]).then_inc(vr_done, 1)
                cut(b + AHEAD)
            cut(S_MZ + AHEAD)

            def z_gate(n):
                t = n - NT
                g.wait_ge(z_done, n + 1)
                g.tensor_tensor(gate[:, t, :], gate[:, t, :], tmp[:, t % 2, :], ALU.mult).then_inc(gate_mul, 1)
                g.wait_ge(gate_mul, t + 1)
                if t == 0:
                    g.wait_ge(ym_done, 2 * MH)
                g.tensor_tensor(ym[:, t, :], ym[:, t, :], gate[:, t, :], ALU.mult).then_inc(ym_gated, 1)

            for s in range(STEPS):
                for kind, what in EVENTS.get(s, ()):
                    i = what[0]
                    if kind == "cut":
                        cut(i)
                    elif kind == "z_gate" and i >= NT:
                        z_gate(i)
                    elif kind == "ya_ms":
                        g.wait_ge(msa_done, i + 1)
                        rsqrt(ra[:, i:i + 1], msa[:, i:i + 1]).then_inc(ra_done, 1)
                    elif kind == "y_ms":
                        g.wait_ge(msy_done, i + 1)
                        rsqrt(ry[:, i:i + 1], msy[:, i:i + 1]).then_inc(ry_done, 1)

        def az_evac(a, t):
            projected(a, U_AZ + t)
            a.activation(silu_az[:, t, :], bank[t][:], ACT.Silu, scale=rx[:, t:t + 1]).then_inc(az_done, 1)

        def z_evac(a, n):
            t = n % NT
            projected(a, U_MZ + n)
            if n >= NT + 2:
                a.wait_ge(gate_mul, t - 1)
            a.activation(gate[:, t, :] if n < NT else tmp[:, t % 2, :], shared("z", n)[:],
                         ACT.Silu if n < NT else ACT.Sigmoid, scale=rx[:, t:t + 1]).then_inc(z_done, 1)

        def om_evac(a, n):
            t, c = n // 2, n % 2
            projected(a, U_OM + n)
            a.wait_ge(turn_ps, TURN_OF["ym", t] + 1)
            a.wait_ge(ym_gated, t + 1)
            a.activation(y_mlstm[:, c, t, :], shared("om", n)[:], ACT.Copy).then_inc(om_done, 1)

        def kt_high(a, t):
            a.wait_ge(kt_ps, t + 1)
            a.activation(kT_hi[:, :, t * P:(t + 1) * P], bank[6 + t % 2][:].rearrange("p (k c) -> p k c", k=4),
                         ACT.Copy).then_inc(kt_hi, 1)

        @block.scalar
        def _(a):
            def cut(n):
                if n >= NSLOT:
                    return
                a.wait_ge(raw_in[n % RAW], 16 * (n // RAW + 1))
                if n >= RING:
                    a.wait_ge(w_used, n - RING + 1)
                a.activation(w_hi[:, n % RING, :], w_raw[:, n % RAW, :], ACT.Copy).then_inc(w_hi_done, 1)

            def x_hi(n):
                t, j = n // 2, n % 2
                a.wait_ge(xt_scaled, n + 1)
                a.activation(xT_hi[:, 4 * j:4 * j + 4, t * P:(t + 1) * P],
                             tmp[:, n % 2, :].rearrange("p (k c) -> p k c", k=4), ACT.Copy).then_inc(xt_hi, 1)

            def x_squares(t):
                if t:
                    a.wait_ge(ssx_done, t)
                a.wait_ge(x_in[t], 16 if t else 32)
                a.activation(junk[:], x_sb[:, t, :], ACT.Square, accum_out=ssx[:, t:t + 1]).then_inc(ssx_done, 1)

            def mv_high(t):
                projected(a, t)
                a.wait_ge(rx_done, 1)
                a.activation(mv_hi[:, t, :, 0:MD], bank[t][:].rearrange("p (h d) -> p h d", h=MH), ACT.Copy,
                             scale=rx[:, t:t + 1]).then_inc(mv_hi_done, 1)

            x_hi(0)
            cut(0)
            x_hi(1)
            for n in range(1, NK):
                cut(n)
            x_hi(2)
            x_hi(3)
            x_squares(0)
            x_squares(1)
            x_hi(4)
            x_hi(5)
            x_squares(2)
            x_hi(6)
            x_hi(7)
            x_squares(3)
            for t in range(NT - 1):
                mv_high(t)
            for n in range(RING, RING + 4):
                cut(n)
            a.wait_ge(fgate_ps, 1)
            a.wait_ge(bcol_done, 1)
            a.activation(rows[0], bank[5][0:16, :], ACT.Abs, bias=bcol[:, 1:2]).then_inc(absf_done, 1)
            a.wait_ge(absf_done, 1)
            a.activation(rows[1], rows[0], ACT.Exp, scale=-1.0).then_inc(expf_done, 1)
            a.wait_ge(onep_done, 1)
            a.activation(rows[0], rows[2], ACT.Ln).then_inc(ln_done, 1)
            mv_high(NT - 1)

            def decays(j):
                a.wait_ge(g_masked, j + 1)
                for h in range(MH):
                    a.activation(decay[j][:, h, :], decay[j][:, h, :], ACT.Exp,
                                 bias=aT[:, j, 4 * j + h:4 * j + h + 1]).then_inc(decay_done, 1)

            def conv_silu(n):
                a.wait_ge(conv_done, n + 1)
                a.activation(cacc[:, n % 2, :], cacc[:, n % 2, :], ACT.Silu).then_inc(silu_done, 1)
                a.wait_ge(silu_done, n + 1)
                if n >= 4:
                    a.wait_ge(st_ps, 4 * (n // 2 - 1))
                a.activation(qk_hi[:, n % 4, :], cacc[:, n % 2, :], ACT.Copy).then_inc(qk_hi_done, 1)

            def pm_high(n):
                h, j = n // NT, n % NT
                w = SEQ - P * j
                a.wait_ge(pm_done, n + 1)
                if h >= 2:
                    a.wait_ge(mpv_ps, 2 * (h - 1))
                a.activation(pm_hi[:, h % 2, P_AT[j]:P_AT[j] + w], pm[:, n % 2, 0:w], ACT.Copy).then_inc(pm_hi_done, 1)

            for b in range(S_QK, S_AV):
                if b == S_AK:
                    for t in range(NT):
                        az_evac(a, t)
                if b == S_QK:
                    cut(b + AHEAD - 2)
                    cut(b + AHEAD - 1)
                cut(b + AHEAD)
                if b == S_QK + 6:
                    a.wait_ge(aT_done, 1)
                    a.activation(emt[:], bank[6][:, 0:NT * 32].rearrange("p (t c) -> p t c", t=NT)[:, :, 16:16 + MH],
                                 ACT.Exp).then_inc(emt_done, 1)
                if b in (S_QK + 6, S_QK + 7):
                    for j in range(2):
                        decays(2 * (b - S_QK - 6) + j)
                if b % 2 == 1 and S_QK + 3 <= b < S_QK + 3 + 4 * MH:
                    conv_silu((b - S_QK - 3) // 2)
                if b in PE_ST:
                    h, j = PE_ST[b]
                    pm_high(h * NT + j)
            for b in range(S_AV, S_MZ):
                if b == S_AV:
                    for t in range(NT):
                        projected(a, U_AK + t)
                        a.activation(keys[:, t, :], bank[t][:], ACT.Copy, scale=rx[:, t:t + 1]).then_inc(k_raw, 1)
                if b == S_AQ:
                    for t in range(NT):
                        projected(a, U_AV + t)
                        a.activation(v_hl[:, t * AH:(t + 1) * AH, 0:DH], bank[t][:].rearrange("p (h d) -> p h d", h=AH),
                                     ACT.Copy, scale=rx[:, t:t + 1]).then_inc(v_hi_done, 1)
                cut(b + AHEAD)
                if S_AV + 2 <= b < S_AV + 6:
                    kt_high(a, b - S_AV - 2)

            def q_copy(i):
                t = NT - 1 - i
                projected(a, U_AQ + i)
                a.activation(queries[:, i, :], bank[i][:], ACT.Copy, scale=rx[:, t:t + 1]).then_inc(q_raw, 1)

            def q_high(i):
                a.wait_ge(qt_ps, i + 1)
                a.activation(qT[:, 2 * i, :], bank[4 + i][:], ACT.Copy).then_inc(qt_hi, 1)

            def turn_high(n):
                k, t = turn_tile(n)
                a.wait_ge(turn_scaled, n + 1)
                projected(a, U_MO + t)
                a.activation(xT_hi[:, k:k + 4, t * P:(t + 1) * P], turned[:, n % 2, :].rearrange("p (k c) -> p k c", k=4),
                             ACT.Copy).then_inc(turn_hi, 1)

            squares = {"ya": 0, "y": 0}

            def junk_free():
                a.wait_ge(ssx_done, NT)
                for kind, done in (("ya", ssa_done), ("y", ssy_done)):
                    if squares[kind]:
                        a.wait_ge(done, squares[kind])

            q_copy(0)
            q_copy(1)
            cut(S_MZ + AHEAD)
            q_copy(2)
            cut(S_MZ + AHEAD + 1)
            q_copy(3)
            q_high(0)
            q_high(1)
            z_evac(a, 0)
            for s in range(STEPS):
                if s < NU:
                    n = (unit(s)[0] + 1) * P
                    a.wait_ge(masked, s + 1)
                    if s >= 2:
                        a.wait_ge(pt_ps, s - 1)
                    a.activation(prob[:, s % 2, 0:n], sm[:, s % 2, 0:n], ACT.Exp, scale=-1.0, bias=mx[:, s:s + 1],
                                 accum_out=rsum[:, s:s + 1]).then_inc(prob_done, 1)
                for kind, what in EVENTS.get(s, ()):
                    if kind == "turn":
                        turn_high(*what)
                for kind, what in EVENTS.get(s, ()):
                    if kind == "z":
                        z_evac(a, *what)
                    elif kind == "om_out":
                        om_evac(a, *what)
                u = s - LAG_T
                if 0 <= u < NU:
                    n = (unit(u)[0] + 1) * P
                    a.wait_ge(pt_ps, u + 1)
                    if u >= 2:
                        a.wait_ge(pv_ps, u - 1)
                    a.activation(pT[:, 2 * (u % 2), 0:n], bank[4 + u % 2][:, 0:n], ACT.Copy).then_inc(pt_hi, 1)
                for kind, what in EVENTS.get(s, ()):
                    i = what[0]
                    if kind == "q_T":
                        q_high(i)
                    elif kind == "cut":
                        cut(i)
                    elif kind == "ya_sq":
                        a.wait_ge(ya_done, i + 1)
                        junk_free()
                        squares["ya"] += 1
                        a.activation(junk[:, 0:AW], ya[:, i % 2, :], ACT.Square,
                                     accum_out=ssa[:, i:i + 1]).then_inc(ssa_done, 1)
                    elif kind == "y":
                        i, c = what
                        a.wait_ge(y_done, 2 * i + c + 1)
                        junk_free()
                        squares["y"] += 1
                        a.activation(junk[:, 0:AW], yb[:, i % 2, c * AW:(c + 1) * AW], ACT.Square,
                                     accum_out=ssy[:, 2 * i + c:2 * i + c + 1]).then_inc(ssy_done, 1)


        @block.vector
        def _(v):
            links = [0]

            def link(ins):
                links[0] += 1
                ins.then_inc(vchain, 1)
                v.wait_ge(vchain, links[0])

            def f32(ap):
                return ap.bitcast(F32)

            def cut(n):
                if on_pool(n):
                    return
                v.wait_ge(w_hi_done, n + 1)
                v.tensor_tensor(w_lo[:, n % RING, :], w_raw[:, n % RAW, :], f32(w_hi[:, n % RING, :]),
                                ALU.subtract).then_inc(w_lo_done[n % 2], 1)

            def scaled(dst, src, row):
                return v.tensor_tensor(dst.rearrange("p (k c) -> p k c", k=4), src.rearrange("p (k c) -> p k c", k=4),
                                       pcol[:, row:row + 4].unsqueeze(2).to_broadcast([P, 4, P]), ALU.mult)

            def mv_low(t):
                v.wait_ge(mv_hi_done, t + 1)
                v.wait_ge(mv_ones, 2)
                v.scalar_tensor_tensor(out=mv_lo[:, t, :, 0:MD], in0=bank[t][:].rearrange("p (h d) -> p h d", h=MH),
                                       scalar=rx[:, t:t + 1], in1=f32(mv_hi[:, t, :, 0:MD]), op0=ALU.mult,
                                       op1=ALU.subtract).then_inc(mv_lo_done, 1)

            v.wait_ge(par_ps, 1)
            v.tensor_copy(pcol[:, 0:R_AG], bank[3][:, 0:R_AG]).then_inc(par_done, 1)
            v.wait_ge(par_done, 1)

            def x_scale(n):
                v.wait_ge(xt_ps, n + 1)
                if n >= 2:
                    v.wait_ge(xt_lo, n - 1)
                scaled(tmp[:, n % 2, :], bank[4 + n % 4][:], R_PRE + 4 * (n % 2)).then_inc(xt_scaled, 1)

            def x_low(n):
                t, j = n // 2, n % 2
                part = (slice(None), slice(4 * j, 4 * j + 4), slice(t * P, (t + 1) * P))
                v.wait_ge(xt_hi, n + 1)
                v.tensor_tensor(xT_lo[part], tmp[:, n % 2, :].rearrange("p (k c) -> p k c", k=4), f32(xT_hi[part]),
                                ALU.subtract).then_inc(xt_lo, 1)

            def x_cut(t):
                for n in (2 * t, 2 * t + 1):
                    x_scale(n)
                for n in (2 * t, 2 * t + 1):
                    x_low(n)

            x_scale(0)
            x_scale(1)
            x_low(0)
            for n in range(4):
                cut(n)
            x_low(1)
            for n in range(4, NK):
                cut(n)
            x_cut(1)
            x_cut(2)
            v.wait_ge(wg_in, 16)
            v.wait_ge(bias_in, 32)
            for q in range(2):
                raw = wg_raw[:, :, 4 * q:4 * q + 4].unsqueeze(2).to_broadcast([P, NK, NT, MH])
                hi = wg_hi[:, :, 16 * q:16 * q + 16].rearrange("p k (j h) -> p k j h", j=NT)
                lo = wg_lo[:, :, 16 * q:16 * q + 16].rearrange("p k (j h) -> p k j h", j=NT)
                link(v.tensor_copy(hi, raw))
                v.tensor_tensor(lo, raw, f32(hi), ALU.subtract).then_inc(wg_done, 1)
                v.tensor_copy(bias32[:, 16 * q:16 * q + 16].rearrange("p (j h) -> p j h", j=NT),
                              bias8[:, 4 * q:4 * q + 4].unsqueeze(1).to_broadcast([P, NT, MH])).then_inc(bias32_done, 1)
            x_cut(3)
            v.wait_ge(par2_ps, 1)
            v.tensor_copy(pcol[:, R_AG:], bank[3][:, 0:R_END - R_AG]).then_inc(par_done, 1)
            v.wait_ge(ssx_done, NT)
            v.tensor_scalar(msx[:], ssx[:], 1.0 / D, EPS, ALU.mult, ALU.add).then_inc(msx_done, 1)
            v.wait_ge(rx_done, 1)
            for t in range(NT):
                v.tensor_scalar(rbc[:, t * P:(t + 1) * P], ident[:], rx[:, t:t + 1], None,
                                ALU.mult).then_inc(diag_done, 1)
            for t in range(NT - 1):
                mv_low(t)
            cut(RING)
            cut(RING + 1)
            v.wait_ge(rbc_ps, 1)
            v.tensor_copy(rbc[:], bank[7][:]).then_inc(rbc_done, 1)
            v.wait_ge(rbc_done, 1)
            v.wait_ge(gate_ps, 1)
            v.wait_ge(consts, 5)
            v.tensor_tensor(gate_rows, bank[4][0:32, :], rbc[0:32, :], ALU.mult).then_inc(gate_sb, 1)
            v.wait_ge(gate_sb, 1)
            v.wait_ge(bias_ps, 1)
            v.tensor_copy(bcol[:], bank[6][0:16, 0:2 * P].rearrange("p (a c) -> p a c", a=2)[:, :, 0])\
                .then_inc(bcol_done, 1)
            v.wait_ge(bcol_done, 1)
            cut(RING + 2)
            cut(RING + 3)
            v.wait_ge(fgate_ps, 1)
            v.tensor_scalar(rows[6], rows[6], bcol[:, 0:1], None, ALU.add).then_inc(igate_done, 1)
            v.wait_ge(expf_done, 1)
            v.tensor_scalar(rows[2], rows[1], 1.0, None, ALU.add).then_inc(onep_done, 1)
            v.wait_ge(onep_done, 1)
            link(v.scalar_tensor_tensor(out=rows[1], in0=rows[2], scalar=-1.0, in1=rows[1], op0=ALU.add,
                                        op1=ALU.subtract))
            link(v.tensor_scalar(rows[3], bank[5][0:16, :], bcol[:, 1:2], 0.0, ALU.add, ALU.min))
            link(v.tensor_tensor(rows[3], rows[3], rows[1], ALU.add))
            v.wait_ge(ln_done, 1)
            link(v.tensor_tensor(rows[3], rows[3], rows[0], ALU.subtract))
            link(v.tensor_tensor(rows[0], rows[3], rows[7], ALU.mult))
            link(v.tensor_tensor_scan(rows[1], rows[7], rows[0], 0.0, ALU.mult, ALU.add))
            v.wait_ge(igate_done, 1)
            link(v.tensor_tensor_scan(rows[2], rows[3], rows[6], 0.0, ALU.add, ALU.max))
            link(v.tensor_tensor(rows[5], rows[6], rows[1], ALU.subtract))
            link(v.tensor_scalar(rows[0], rows[2], -1.0, None, ALU.mult))
            v.tensor_tensor(rows[4], rows[1], rows[2], ALU.subtract).then_inc(grows_done, 1)
            v.wait_ge(grows_done, 1)
            mv_low(NT - 1)

            def conv_in(n):
                u = upad[:, n % 2, :]
                projected(v, 4 + n)
                v.wait_ge(rbc_done, 1)
                if n >= 2:
                    v.wait_ge(conv_done, n - 1)
                v.tensor_tensor(u[:, KCONV - 1:KCONV - 1 + SEQ], bank[n % 4][:], rbc[:], ALU.mult).then_inc(u_done, 1)

            def conv(n):
                c = n // 2 + MH * (n % 2)
                u, acc = upad[:, n % 2, :], cacc[:, n % 2, :]
                v.wait_ge(u_done, n + 1)
                v.wait_ge(cleared, 5)
                if n >= 2:
                    v.wait_ge(qk_lo_done, n - 1)
                tap = [pcol[:, R_CW + 8 * j + c:R_CW + 8 * j + c + 1] for j in range(KCONV)]
                link(v.tensor_scalar(acc, u[:, 0:SEQ], tap[0], pcol[:, R_CB + c:R_CB + c + 1], ALU.mult, ALU.add))
                for j in range(1, KCONV):
                    ins = v.scalar_tensor_tensor(out=acc, in0=u[:, j:j + SEQ], scalar=tap[j], in1=acc, op0=ALU.mult,
                                                 op1=ALU.add)
                    if j < KCONV - 1:
                        link(ins)
                    else:
                        ins.then_inc(conv_done, 1)

            def qk_low(n):
                v.wait_ge(qk_hi_done, n + 1)
                v.tensor_tensor(qk_lo[:, n % 4, :], cacc[:, n % 2, :], f32(qk_hi[:, n % 4, :]),
                                ALU.subtract).then_inc(qk_lo_done, 1)

            def weighted(h, j):
                n = h * NT + j
                w = SEQ - P * j
                v.wait_ge(st_ps, n + 1)
                v.wait_ge(decay_done, MH * NT)
                if n >= 2:
                    v.wait_ge(pm_lo_done, n - 1)
                v.scalar_tensor_tensor(out=pm[:, n % 2, 0:w], in0=bank[4 + n % 2][:, 0:w], scalar=K_SCALE,
                                       in1=decay[j][:, h, :], op0=ALU.mult, op1=ALU.mult).then_inc(pm_done, 1)

            def head_stats(n):
                h, t0 = n // 2, 2 * (n % 2)
                pv = bank[6 + n % 2][:, 0:2 * MV].rearrange("p (t c) -> p t c", t=2)
                v.wait_ge(mpv_ps, n + 1)
                v.wait_ge(emt_done, 1)
                if n:
                    v.wait_ge(ym_done, n)
                for q in range(2):
                    v.bn_stats(bns[:, q, :], pv[:, q, 0:MD])
                link(v.scalar_tensor_tensor(out=den[:], in0=pv[:, :, MD], scalar=-1.0, in1=emt[:, t0:t0 + 2, h],
                                            op0=ALU.mult, op1=ALU.max))
                link(v.tensor_tensor(den[:], pv[:, :, MD], den[:], ALU.max))
                for q in range(2):
                    v.bn_aggr(mva[:, q, :], bns[:, q, :])
                link(v.reciprocal(iden[:], den[:]))
                link(v.tensor_tensor(vs1[:], mva[:, :, 1], iden[:], ALU.mult))
                link(v.tensor_tensor(vs1[:], vs1[:], iden[:], ALU.mult))
                v.tensor_scalar(vs2[:], vs1[:], EPS, None, ALU.add).then_inc(var_done, 1)

            def head_norm(n):
                h, t0 = n // 2, 2 * (n % 2)
                pv = bank[6 + n % 2][:, 0:2 * MV].rearrange("p (t c) -> p t c", t=2)
                v.wait_ge(vr_done, n + 1)
                link(v.tensor_tensor(hsc[:], vr[:], iden[:], ALU.mult))
                for q in range(2):
                    ins = v.tensor_scalar(ym[:, t0 + q, h * MD:(h + 1) * MD], pv[:, q, 0:MD], mva[:, q, 0:1],
                                          hsc[:, q:q + 1], ALU.subtract, ALU.mult)
                ins.then_inc(ym_done, 1)

            for b in range(S_QK, S_AV):
                if b == S_QK:
                    cut(b + AHEAD - 2)
                    cut(b + AHEAD - 1)
                cut(b + AHEAD)
                if b == S_QK + 2:
                    v.wait_ge(gcol_ps, 1)
                    v.tensor_copy(aT[:], bank[6][:, 0:NT * 32].rearrange("p (t c) -> p t c", t=NT)[:, :, 0:16])\
                        .then_inc(aT_done, 1)
                if b % 2 == 1 and b < S_AZ:
                    conv_in((b - S_QK) // 2)
                if b in PE_ST:
                    weighted(*PE_ST[b])
                if b % 2 == 1 and b < S_AZ:
                    conv((b - S_QK) // 2)
                if b % 2 == 0 and S_QK + 4 <= b < S_QK + 4 + 4 * MH:
                    qk_low((b - S_QK - 4) // 2)
                if b - 1 in PE_PV:
                    head_norm(2 * PE_PV[b - 1][0] + PE_PV[b - 1][1])
                if b in PE_PV:
                    head_stats(2 * PE_PV[b][0] + PE_PV[b][1])

            def rope(buf, t):
                xs = buf.rearrange("p (h d) -> p h d", h=AH)
                ra_, rb = (rtmp[:, q, :].rearrange("p (h d) -> p h d", h=AH) for q in range(2))

                def table(at, n):
                    return rope_sb[:, t, at:at + n].unsqueeze(1).to_broadcast([P, AH, n])

                v.tensor_tensor(ra_, xs[:, :, 0:ROT], table(0, ROT), ALU.mult)
                v.tensor_tensor(rb[:, :, 0:HALF], xs[:, :, HALF:ROT], table(ROT, HALF), ALU.mult)
                link(v.tensor_tensor(rb[:, :, HALF:ROT], xs[:, :, 0:HALF], table(ROT + HALF, HALF), ALU.mult))
                return v.tensor_tensor(xs[:, :, 0:ROT], ra_, rb, ALU.add)

            def kt_low(t):
                part = (slice(None), slice(None), slice(t * P, (t + 1) * P))
                v.wait_ge(kt_hi, t + 1)
                v.tensor_tensor(kT_lo[part], bank[6 + t % 2][:].rearrange("p (k c) -> p k c", k=4), f32(kT_hi[part]),
                                ALU.subtract).then_inc(kt_lo, 1)

            v.wait_ge(rope_in, 16)
            for b in range(S_AV, S_MZ):
                if b == S_AQ:
                    for t in range(NT):
                        part = v_hl[:, t * AH:(t + 1) * AH]
                        v.wait_ge(v_hi_done, t + 1)
                        v.scalar_tensor_tensor(out=part[:, :, DH:], in0=bank[t][:].rearrange("p (h d) -> p h d", h=AH),
                                               scalar=rx[:, t:t + 1], in1=f32(part[:, :, 0:DH]), op0=ALU.mult,
                                               op1=ALU.subtract).then_inc(v_lo_done, 1)
                cut(b + AHEAD)
                if S_AV <= b < S_AV + 4:
                    t = b - S_AV
                    v.wait_ge(k_raw, t + 1)
                    if t:
                        v.wait_ge(k_roped, t)
                    rope(keys[:, t, :], t).then_inc(k_roped, 1)
                if S_AV + 2 <= b < S_AV + 6:
                    kt_low(b - S_AV - 2)

            def q_rope(i):
                v.wait_ge(q_raw, i + 1)
                v.wait_ge(k_roped, NT)
                if i:
                    v.wait_ge(q_roped, i)
                rope(queries[:, i, :], NT - 1 - i).then_inc(q_roped, 1)

            def q_low(i):
                v.wait_ge(qt_hi, i + 1)
                v.tensor_tensor(qT[:, 2 * i + 1, :], bank[4 + i][:], f32(qT[:, 2 * i, :]),
                                ALU.subtract).then_inc(qt_lo, 1)

            def turn(n):
                k, t = turn_tile(n)
                part = (slice(None), slice(k, k + 4), slice(t * P, (t + 1) * P))
                v.wait_ge(turn_ps, n + 1)
                if n >= 2:
                    v.wait_ge(turn_lo, n - 1)
                scaled(turned[:, n % 2, :], shared("turn", n)[:], R_MG if TURNS[n][1] == "ym" else R_AG).then_inc(turn_scaled, 1)
                v.wait_ge(turn_hi, n + 1)
                v.tensor_tensor(xT_lo[part], turned[:, n % 2, :].rearrange("p (k c) -> p k c", k=4), f32(xT_hi[part]),
                                ALU.subtract).then_inc(turn_lo, 1)

            def ya_half(i, q):
                v.wait_ge(pv_ps, AH * i + 4 * q + 4)
                if i >= 2:
                    v.wait_ge(turn_ps, TURN_OF["ya", i - 2] + 1)
                v.tensor_reduce(ya[:, i % 2, :].rearrange("p (h d) -> p h d", h=AH)[:, 4 * q:4 * q + 4, :],
                                bank[6 + q][:].rearrange("p (h a d) -> p h d a", h=4, a=2), mybir.AxisListType.X,
                                ALU.add).then_inc(ya_summed, 1)

            q_rope(0)
            q_rope(1)
            cut(S_MZ + AHEAD)
            q_low(0)
            cut(S_MZ + AHEAD + 1)
            q_rope(2)
            q_rope(3)
            q_low(1)
            for s in range(STEPS):
                if s < NU:
                    n = (unit(s)[0] + 1) * P
                    v.wait_ge(score_ps, s + 1)
                    if s >= 2:
                        v.wait_ge(prob_done, s - 1)
                    v.tensor_tensor_reduce(sm[:, s % 2, 0:n], bank[2 + s % 2][:, 0:n], causal[:, SEQ - n:], -Q_SCALE,
                                           BIG, ALU.add, ALU.min, mx[:, s:s + 1]).then_inc(masked, 1)
                for kind, what in EVENTS.get(s, ()):
                    if kind == "turn":
                        turn(*what)
                u = s - LAG_T
                if 0 <= u < NU:
                    n = (unit(u)[0] + 1) * P
                    v.wait_ge(pt_hi, u + 1)
                    v.tensor_tensor(pT[:, 2 * (u % 2) + 1, 0:n], bank[4 + u % 2][:, 0:n],
                                    f32(pT[:, 2 * (u % 2), 0:n]), ALU.subtract).then_inc(pt_lo, 1)
                for kind, what in EVENTS.get(s, ()):
                    i = what[0]
                    if kind == "q_T":
                        q_low(i)
                    elif kind == "cut":
                        cut(i)
                    elif kind == "ya_half":
                        ya_half(i, 0)
                    elif kind == "ya":
                        ya_half(i, 1)
                        link(v.reciprocal(rrec[:, AH * i:AH * i + AH], rsum[:, AH * i:AH * i + AH]))
                        v.wait_ge(ya_summed, 2 * i + 2)
                        yv = ya[:, i % 2, :].rearrange("p (h d) -> p h d", h=AH)
                        v.tensor_tensor(yv, yv,
                                        rrec[:, AH * i:AH * i + AH].unsqueeze(2).to_broadcast([P, AH, DH]),
                                        ALU.mult).then_inc(ya_done, 1)
                    elif kind == "ya_ms":
                        v.wait_ge(ssa_done, i + 1)
                        v.tensor_scalar(msa[:, i:i + 1], ssa[:, i:i + 1], 1.0 / AW, EPS, ALU.mult, ALU.add)\
                            .then_inc(msa_done, 1)
                    elif kind == "ya_gate":
                        v.wait_ge(ra_done, i + 1)
                        v.scalar_tensor_tensor(out=ya[:, i % 2, :], in0=ya[:, i % 2, :], scalar=ra[:, i:i + 1],
                                               in1=silu_az[:, NT - 1 - i, :], op0=ALU.mult, op1=ALU.mult)\
                            .then_inc(ya_gated, 1)
                    elif kind == "y":
                        i, c = what
                        cols = slice(c * AW, (c + 1) * AW)
                        v.wait_ge(oa_ps, 2 * i + c + 1)
                        v.wait_ge(om_done, 2 * NT)
                        if i >= 2:
                            v.wait_ge(ssy_done, 2 * (i - 1))
                        v.tensor_tensor(yb[:, i % 2, cols], shared("oa", 2 * i + c)[:], y_mlstm[:, c, NT - 1 - i, :],
                                        ALU.add).then_inc(y_done, 1)
                        v.wait_ge(y_done, 2 * i + c + 1)
                        v.wait_ge(post_in, 16)
                        if i == 0:
                            v.wait_ge(gate_mul, NT)
                        elif i == 1:
                            v.wait_ge(prob_done, NU)
                        else:
                            v.wait_ge(out_ready, 2 * (i - 1))
                        v.tensor_tensor(yg[i % 2][:, cols], yb[:, i % 2, cols], post[:, cols],
                                        ALU.mult).then_inc(y_gained, 1)
                    elif kind == "y_ms":
                        v.wait_ge(ssy_done, 2 * i + 2)
                        link(v.tensor_tensor(msy[:, i:i + 1], ssy[:, 2 * i:2 * i + 1], ssy[:, 2 * i + 1:2 * i + 2],
                                             ALU.add))
                        v.tensor_scalar(msy[:, i:i + 1], msy[:, i:i + 1], 1.0 / D, EPS, ALU.mult, ALU.add)\
                            .then_inc(msy_done, 1)
                    elif kind == "y_fin":
                        v.wait_ge(ry_done, i + 1)
                        v.wait_ge(xr_in[i], 16)
                        v.wait_ge(y_gained, 2 * i + 2)
                        for c in range(2):
                            cols = slice(c * AW, (c + 1) * AW)
                            v.scalar_tensor_tensor(out=xr[:, i % 2, cols], in0=yg[i % 2][:, cols],
                                                   scalar=ry[:, i:i + 1], in1=xr[:, i % 2, cols], op0=ALU.mult,
                                                   op1=ALU.add).then_inc(out_ready, 1)

        @block.tensor
        def _(pe):
            def product(o, hi, lo, m_hi, m_lo, start, stop):
                pe.matmul(o, hi, m_hi, start=start, stop=False)
                pe.matmul(o, hi, m_lo, start=False, stop=False)
                return pe.matmul(o, lo, m_hi, start=False, stop=stop)

            def x_part(k, t):
                cols = slice(t * P, (t + 1) * P)
                return xT_hi[:, k, cols], xT_lo[:, k, cols]

            def w_part(n, cols=slice(0, AW)):
                return w_hi[:, n % RING, cols], w_lo[:, n % RING, cols]

            pe.wait_ge(ident_done, 1)
            pe.wait_ge(par_in, 16)
            pe.transpose(bank[3][:, 0:R_AG], prow[:], ident[0:R_AG, 0:R_AG]).then_inc(par_ps, 1)

            def turn_x(t):
                for n in (2 * t, 2 * t + 1):
                    j = n % 2
                    pe.wait_ge(x_in[t], 16 if t else 32)
                    if n >= 4:
                        pe.wait_ge(xt_scaled, n - 3)
                    for k in range(4):
                        mm = pe.transpose(bank[4 + n % 4][:, k * P:(k + 1) * P],
                                          x_sb[:, t, (4 * j + k) * P:(4 * j + k + 1) * P], ident[:])
                    mm.then_inc(xt_ps, 1)

            def mv_part(t, ks):
                for k in ks:
                    pe.wait_ge(xt_lo, 2 * t + 1 + k // 4)
                    low_done(pe, k)
                    mm = product(bank[t][:], *x_part(k, t), *w_part(k), k == 0, k == NK - 1)
                    if t == NT - 1:
                        mm.then_inc(w_used, 1)
                    elif k == NK - 1:
                        mm.then_inc(proj_ps, 1)

            turn_x(0)
            mv_part(0, range(4))
            turn_x(1)
            mv_part(0, range(4, NK))
            mv_part(1, range(4))
            turn_x(2)
            mv_part(1, range(4, NK))
            mv_part(2, range(4))
            turn_x(3)
            mv_part(2, range(4, NK))
            pe.wait_ge(par2_in, 64)
            pe.wait_ge(par_done, 1)
            pe.transpose(bank[3][:, 0:R_END - R_AG], prow2[:], ident[0:R_END - R_AG, 0:R_END - R_AG]).then_inc(par2_ps, 1)
            pe.wait_ge(wg_done, 2)
            pe.wait_ge(xt_lo, 2 * NT)
            for k in range(NK):
                mm = product(bank[4][0:32, :], wg_hi[:, k, :], wg_lo[:, k, :], xT_hi[:, k, :], xT_lo[:, k, :],
                             k == 0, k == NK - 1)
            mm.then_inc(gate_ps, 1)
            pe.wait_ge(par_done, 2)
            mv_part(3, range(4))
            pe.wait_ge(bias32_done, 2)
            for q in range(2):
                mm = pe.transpose(bank[6][0:16, q * P:(q + 1) * P], bias32[:, 16 * q:16 * q + 16], ident[:])
            mm.then_inc(bias_ps, 1)
            pe.wait_ge(consts, 1)
            for t in range(NT):
                pe.wait_ge(diag_done, t + 1)
                mm = pe.matmul(bank[7][:, t * P:(t + 1) * P], ones[:], rbc[:, t * P:(t + 1) * P], start=True, stop=True)
            mm.then_inc(rbc_ps, 1)
            mv_part(3, range(4, NK))
            pe.wait_ge(gate_sb, 1)
            pe.matmul(bank[5][0:16, :], ident[0:32, 16:32], gate_rows, start=True, stop=True).then_inc(fgate_ps, 1)

            def by_slot(n, k, nk, part, free):
                low_done(pe, n)
                for t in range(NT):
                    if k == 0:
                        free(t)
                    mm = product(bank[t][:], *part(k, t), *w_part(n), k == 0, k == nk - 1)
                    if k == nk - 1 and t < NT - 1:
                        mm.then_inc(proj_ps, 1)
                mm.then_inc(w_used, 1)

            def gate_cols():
                pe.wait_ge(grows_done, 1)
                for t in range(NT):
                    pe.transpose(bank[6][:, 32 * t:32 * t + 16], rows[5][:, t * P:(t + 1) * P], ident[0:16, 0:16])
                    mm = pe.transpose(bank[6][:, 32 * t + 16:32 * t + 32], rows[0][:, t * P:(t + 1) * P],
                                      ident[0:16, 0:16])
                mm.then_inc(gcol_ps, 1)

            def head_scores(h, j):
                n, q, kk = h * NT + j, 2 * (h % 2), 2 * (h % 2) + 1
                pe.wait_ge(qk_lo_done, 2 * h + 2)
                if n < 2:
                    pe.wait_ge(grows_done, 1)
                else:
                    pe.wait_ge(pm_done, n - 1)
                src = slice(j * P, (j + 1) * P)
                product(bank[4 + n % 2][:, 0:SEQ - j * P], qk_hi[:, kk, src], qk_lo[:, kk, src],
                        qk_hi[:, q, j * P:], qk_lo[:, q, j * P:], True, True).then_inc(st_ps, 1)

            def head_values(h, half):
                pe.wait_ge(mv_lo_done, NT)
                pe.wait_ge(pm_lo_done, NT * h + 2 * half + 2)
                n = 2 * h + half
                if n == 0:
                    pe.wait_ge(emt_done, 1)
                elif n == 1:
                    pe.wait_ge(rbc_done, 1)
                else:
                    pe.wait_ge(ym_done, n - 1)
                for q in range(2):
                    t = 2 * half + q
                    for j in range(t + 1):
                        w = slice(P_AT[j] + (t - j) * P, P_AT[j] + (t - j + 1) * P)
                        mm = product(bank[6 + half][:, MV * q:MV * (q + 1)], pm_hi[:, h % 2, w], pm_lo[:, h % 2, w],
                                     mv_hi[:, j, h, :], mv_lo[:, j, h, :], j == 0, j == t)
                mm.then_inc(mpv_ps, 1)

            def mlstm(b):
                if b in PE_ST:
                    head_scores(*PE_ST[b])
                if b in PE_PV:
                    head_values(*PE_PV[b])

            for b in range(S_QK, S_AZ):
                p = 4 + (b - S_QK) // 2
                low_done(pe, b)
                if b % 2 == 0:
                    if p < 8:
                        pe.wait_ge(mv_lo_done, p - 3)
                    else:
                        pe.wait_ge(u_done, p - 7)
                for kk in range(4):
                    k = 4 * (b % 2) + kk
                    mm = product(bank[p % 4][:], *w_part(b, slice(kk * P, (kk + 1) * P)), xT_hi[:, k, :],
                                 xT_lo[:, k, :], k == 0, k == NK - 1)
                mm.then_inc(w_used, 1)
                if b == S_QK + 2:
                    gate_cols()
                mlstm(b)
            for b in range(S_AZ, S_AV):
                if b < S_AK:
                    by_slot(b, b % NK, NK, x_part, lambda t: pe.wait_ge(u_done, 5 + t))
                else:
                    by_slot(b, b % NK, NK, x_part, lambda t: pe.wait_ge(az_done, 1 + t))
                mlstm(b)
            for b in range(S_AV, S_AQ):
                by_slot(b, b % NK, NK, x_part, lambda t: pe.wait_ge(k_raw, t + 1))
                t = b - S_AV - 2
                if 0 <= t < NT:
                    pe.wait_ge(k_roped, t + 1)
                    if t < 2:
                        pe.wait_ge(ym_done, 2 * MH)
                    else:
                        pe.wait_ge(kt_lo, t - 1)
                    for k in range(4):
                        mm = pe.transpose(bank[6 + t % 2][:, k * P:(k + 1) * P], keys[:, t, k * P:(k + 1) * P],
                                          ident[:])
                    mm.then_inc(kt_ps, 1)
            for b in range(S_AQ, S_MZ):
                by_slot(b, b % NK, NK, lambda k, i: x_part(k, NT - 1 - i), lambda i: pe.wait_ge(v_lo_done, i + 1))

            def shared_free(kind, n):
                before, m = SHARED[kind, n][1]
                pe.wait_ge({"q": q_raw, "z": z_done, "om": om_done, "oa": y_done, "turn": turn_scaled}[before], m + 1)

            def z_part(n, k):
                t, slot = n % NT, S_MZ + NK * (n // NT) + k
                if t == 0:
                    low_done(pe, slot)
                if k == 0:
                    shared_free("z", n)
                mm = product(shared("z", n)[:], *x_part(k, t), *w_part(slot), k == 0, k == NK - 1)
                if t == NT - 1:
                    mm.then_inc(w_used, 1)
                elif k == NK - 1:
                    mm.then_inc(proj_ps, 1)

            def om_part(n, k):
                t, slot = n // 2, S_OM + 4 * (n % 2) + k
                pe.wait_ge(turn_lo, TURN_OF["ym", t] + 1)
                low_done(pe, slot)
                if k == 0:
                    shared_free("om", n)
                mm = product(shared("om", n)[:], *x_part(k, t), *w_part(slot), k == 0, k == 3)
                if t == NT - 1:
                    mm.then_inc(w_used, 1)
                elif k == 3:
                    mm.then_inc(proj_ps, 1)

            def turn_q(i):
                pe.wait_ge(q_roped, i + 1)
                pe.wait_ge(kt_lo, NT)
                for k in range(4):
                    mm = pe.transpose(bank[4 + i][:, k * P:(k + 1) * P], queries[:, i, k * P:(k + 1) * P], ident[:])
                mm.then_inc(qt_ps, 1)

            def turn(n):
                _, kind, i = TURNS[n]
                pe.wait_ge(ym_gated if kind == "ym" else ya_gated, i + 1)
                shared_free("turn", n)
                src = ym[:, i] if kind == "ym" else ya[:, i % 2]
                for k in range(4):
                    mm = pe.transpose(shared("turn", n)[:, k * P:(k + 1) * P], src[:, k * P:(k + 1) * P], ident[:])
                mm.then_inc(turn_ps, 1)

            def oa(i, k):
                c, kk = k // 4, k % 4
                pe.wait_ge(turn_lo, TURN_OF["ya", i] + 1)
                low_done(pe, S_OA + k)
                if kk == 0:
                    shared_free("oa", 2 * i + c)
                mm = product(shared("oa", 2 * i + c)[:], *x_part(4 + kk, NT - 1 - i), *w_part(S_OA + k), kk == 0,
                             kk == 3)
                if kk == 3:
                    mm.then_inc(oa_ps, 1)

            for k in range(4):
                z_part(0, k)
            turn_q(0)
            for k in range(4, NK):
                z_part(0, k)
            turn_q(1)
            for s in range(STEPS):
                events = EVENTS.get(s, ())
                if s < NU:
                    t, h = unit(s)
                    i, n, half = s // AH, (t + 1) * P, slice(DH * (h % 2), DH * (h % 2 + 1))
                    pe.wait_ge(qt_lo, i + 1)
                    if s < 2:
                        pe.wait_ge(q_raw, NT)
                    else:
                        pe.wait_ge(masked, s - 1)
                    cols = slice(h // 2 * P, (h // 2 + 1) * P)
                    product(bank[2 + s % 2][:, 0:n], qT[half, 2 * i, cols], qT[half, 2 * i + 1, cols],
                            kT_hi[half, h // 2, 0:n], kT_lo[half, h // 2, 0:n], True, True).then_inc(score_ps, 1)
                u = s - LAG_T
                if 0 <= u < NU:
                    t, h = unit(u)
                    pe.wait_ge(prob_done, u + 1)
                    if u >= 2:
                        pe.wait_ge(pt_lo, u - 1)
                    else:
                        pe.wait_ge(qt_lo, 2)
                    for j in range(t + 1):
                        mm = pe.transpose(bank[4 + u % 2][:, j * P:(j + 1) * P], prob[:, u % 2, j * P:(j + 1) * P],
                                          ident[:])
                    mm.then_inc(pt_ps, 1)
                for kind, what in events:
                    if kind == "turn":
                        turn(*what)
                for kind, what in events:
                    if kind == "z_part":
                        z_part(*what)
                    elif kind == "om":
                        om_part(*what)
                    elif kind == "oa":
                        oa(*what)
                u = s - LAG_PV
                if 0 <= u < NU:
                    t, h = unit(u)
                    pe.wait_ge(pt_lo, u + 1)
                    pe.wait_ge(v_lo_done, NT)
                    if u == 0:
                        pe.wait_ge(qt_lo, NT)
                    if h % 4 == 0 and u >= AH:
                        pe.wait_ge(ya_summed, 2 * (u // AH) - 1 + h // 4)
                    for j in range(t + 1):
                        cols = slice(j * P, (j + 1) * P)
                        for q in range(2):
                            mm = pe.matmul(bank[6 + h // 4][:, h % 4 * P:(h % 4 + 1) * P], pT[:, 2 * (u % 2) + q, cols],
                                           v_hl[:, j * AH + h, :], start=j + q == 0, stop=j == t and q == 1)
                    mm.then_inc(pv_ps, 1)
                for kind, what in events:
                    if kind == "q_T":
                        turn_q(*what)


_INS = ["x", "pre_norm_g", "w_in", "mlstm_i_bias", "mlstm_f_bias", "conv_w", "conv_b", "attn_out_g", "mlstm_out_g",
        "w_out", "post_norm_g"]


def rope_table():
    inv = np.power(np.float32(500000.0), -np.arange(HALF, dtype=np.float32) * np.float32(2.0) / np.float32(ROT))
    ang = np.arange(SEQ, dtype=np.float32)[:, None] * inv.astype(np.float32)[None, :]
    cos, sin = np.cos(ang), np.sin(ang)
    return np.concatenate([cos, cos, -sin, sin], axis=1).astype(np.float32)


def kernel(**inputs):
    import concourse.bacc as _bacc
    from concourse.bass_utils import run_bass_kernel_spmd as _run

    nc = _bacc.Bacc("TRN2", target_bir_lowering=False, num_devices=1)
    arrays = {f"in_{n}": np.ascontiguousarray(inputs[n]) for n in _INS}
    arrays["in_rope"] = rope_table()
    args = [nc.dram_tensor(n, a.shape, mybir.dt.from_np(a.dtype), kind="ExternalInput").ap() for n, a in arrays.items()]
    args.append(nc.dram_tensor("out_y", (1, SEQ, D), F32, kind="ExternalOutput").ap())
    build(nc, *args)
    r = _run(nc, [arrays], core_ids=[0])
    return r.results[0]["out_y"]
```
